# Optimizing a Trainium2 kernel written in Bass

```python
import jax, jax.numpy as jnp
from jax import lax
import numpy as np

D_MODEL = 1024
BATCH = 1
SEQ = 512
DEPTH = 2

HEAD_DIM = 64
N_HEADS_A = 8
N_HEADS_B = 8
N_HEADS_C = 8
WIDTH_A = N_HEADS_A * HEAD_DIM
WIDTH_B = N_HEADS_B * HEAD_DIM
WIDTH_C = N_HEADS_C * HEAD_DIM
WIDTH_D = D_MODEL // 2
POOL_WINDOWS = (2, 4, 8, 16)
N_POOL_GROUPS = len(POOL_WINDOWS)
POOL_GROUP_DIM = WIDTH_D // N_POOL_GROUPS
CHUNK = 128
Q_BLOCK = 128
PLE_DIM = 256
N_EXPERT_GROUPS = 4
EXPERTS_PER_GROUP = 4
N_EXPERTS = N_EXPERT_GROUPS * EXPERTS_PER_GROUP
TOP_K_INNER = 2
D_EXPERT = 256
RMS_EPS = 1e-6
N_EVEN = (DEPTH + 1) // 2
N_ODD = DEPTH // 2
EVEN_IN = 2 * WIDTH_A + 3 * WIDTH_B
ODD_IN = 3 * WIDTH_C + N_HEADS_C + WIDTH_D

kernel_name = "hybrid_sgu_stickbreak_fox_pool_hmoe"

def _rms_unit(x):
    xf = x.astype(jnp.float32)
    return (xf * lax.rsqrt(jnp.mean(xf * xf, axis=-1, keepdims=True) + RMS_EPS)).astype(x.dtype)

def rmsnorm(x, g):
    xf = x.astype(jnp.float32)
    y = xf * lax.rsqrt(jnp.mean(xf * xf, axis=-1, keepdims=True) + RMS_EPS)
    return (y * g.astype(jnp.float32)).astype(x.dtype)

def spatial_gating(u, v, w_s, b_s, g_v):
    bsz, seq, nh, hd = u.shape
    nc = seq // CHUNK
    u = jax.nn.gelu(u)
    v = rmsnorm(jax.nn.gelu(v), g_v)
    mask = jnp.tril(jnp.ones((CHUNK, CHUNK), dtype=bool))
    w = jnp.where(mask, w_s, 0.0)
    vc = v.reshape(bsz, nc, CHUNK, nh, hd)
    mixed = jnp.einsum('hts,bcshd->bcthd', w, vc) + b_s.T[None, None, :, :, None]
    return u * mixed.reshape(bsz, seq, nh, hd)

def stick_breaking_attention(q, k, v):
    bsz, seq, nh, hd = q.shape
    nb = seq // Q_BLOCK
    kf = k.astype(jnp.float32)
    vf = v.astype(jnp.float32)
    qb = q.astype(jnp.float32).reshape(bsz, nb, Q_BLOCK, nh, hd).swapaxes(0, 1)
    key_pos = jnp.arange(seq)
    scale = hd ** -0.5

    def block(args):
        q_blk, blk = args
        q_pos = blk * Q_BLOCK + jnp.arange(Q_BLOCK)
        strict = key_pos[None, :] < q_pos[:, None]
        z = jnp.einsum('bqhd,bkhd->bhqk', q_blk, kf) * scale
        log_1m_beta = jnp.where(strict, jax.nn.log_sigmoid(-z), 0.0)
        between = lax.cumsum(log_1m_beta, axis=3, reverse=True) - log_1m_beta
        weights = jnp.where(strict, jnp.exp(jax.nn.log_sigmoid(z) + between), 0.0)
        return jnp.einsum('bhqk,bkhd->bqhd', weights, vf)

    out = lax.map(block, (qb, jnp.arange(nb)))
    return out.swapaxes(0, 1).reshape(bsz, seq, nh, hd).astype(q.dtype)

def forgetting_attention(q, k, v, log_f):
    bsz, seq, nh, hd = q.shape
    nb = seq // Q_BLOCK
    cum_f = jnp.cumsum(log_f.astype(jnp.float32), axis=1)
    f_key = cum_f.transpose(0, 2, 1)
    f_qb = cum_f.reshape(bsz, nb, Q_BLOCK, nh).swapaxes(0, 1)
    kf = k.astype(jnp.float32)
    vf = v.astype(jnp.float32)
    qb = q.astype(jnp.float32).reshape(bsz, nb, Q_BLOCK, nh, hd).swapaxes(0, 1)
    key_pos = jnp.arange(seq)
    scale = hd ** -0.5

    def block(args):
        q_blk, fq_blk, blk = args
        q_pos = blk * Q_BLOCK + jnp.arange(Q_BLOCK)
        causal = key_pos[None, :] <= q_pos[:, None]
        z = (jnp.einsum('bqhd,bkhd->bhqk', q_blk, kf) * scale
             + fq_blk.transpose(0, 2, 1)[..., None] - f_key[:, :, None, :])
        probs = jax.nn.softmax(jnp.where(causal, z, -jnp.inf), axis=-1)
        return jnp.einsum('bhqk,bkhd->bqhd', probs, vf)

    out = lax.map(block, (qb, f_qb, jnp.arange(nb)))
    return out.swapaxes(0, 1).reshape(bsz, seq, nh, hd).astype(q.dtype)

def multiscale_pool(xd, w_pool, pool_scale):
    bsz, seq, _ = xd.shape
    xg = xd.astype(jnp.float32).reshape(bsz, seq, N_POOL_GROUPS, POOL_GROUP_DIM)
    cs = jnp.concatenate([jnp.zeros((bsz, 1, N_POOL_GROUPS, POOL_GROUP_DIM), jnp.float32),
                          jnp.cumsum(xg, axis=1)], axis=1)
    pos = jnp.arange(seq)
    outs = []
    for g, win in enumerate(POOL_WINDOWS):
        csg = cs[:, :, g]
        start = jnp.maximum(pos + 1 - win, 0)
        count = (pos + 1 - start).astype(jnp.float32)
        mean = (csg[:, 1:] - csg[:, start]) / count[None, :, None]
        outs.append(mean - xg[:, :, g])
    pooled = jnp.stack(outs, axis=2)
    mixed = jnp.einsum('bsgc,gcd->bsgd', pooled, w_pool.astype(jnp.float32))
    return (mixed.reshape(bsz, seq, WIDTH_D) * pool_scale.astype(jnp.float32)).astype(xd.dtype)

def even_mixer(h, w_in, sgu_w, sgu_b, sgu_norm, w_out):
    bsz, seq, _ = h.shape
    proj = h @ w_in
    u, va, q, k, vb = jnp.split(
        proj, [WIDTH_A, 2 * WIDTH_A, 2 * WIDTH_A + WIDTH_B, 2 * WIDTH_A + 2 * WIDTH_B], axis=-1)
    heads = lambda t, n: t.reshape(bsz, seq, n, HEAD_DIM)
    ya = spatial_gating(heads(u, N_HEADS_A), heads(va, N_HEADS_A), sgu_w, sgu_b, sgu_norm)
    yb = stick_breaking_attention(heads(q, N_HEADS_B), heads(k, N_HEADS_B), heads(vb, N_HEADS_B))
    y = jnp.concatenate([ya.reshape(bsz, seq, WIDTH_A), yb.reshape(bsz, seq, WIDTH_B)], axis=-1)
    return y @ w_out

def odd_mixer(h, w_in, forget_bias, q_norm, k_norm, pool_w, pool_scale, w_out):
    bsz, seq, _ = h.shape
    proj = h @ w_in
    q, k, v, f_logit, xd = jnp.split(
        proj, [WIDTH_C, 2 * WIDTH_C, 3 * WIDTH_C, 3 * WIDTH_C + N_HEADS_C], axis=-1)
    heads = lambda t: t.reshape(bsz, seq, N_HEADS_C, HEAD_DIM)
    q = rmsnorm(heads(q), q_norm)
    k = rmsnorm(heads(k), k_norm)
    log_f = jax.nn.log_sigmoid(f_logit.astype(jnp.float32) + forget_bias.astype(jnp.float32))
    yc = forgetting_attention(q, k, heads(v), log_f)
    yd = multiscale_pool(xd, pool_w, pool_scale)
    y = jnp.concatenate([yc.reshape(bsz, seq, WIDTH_C), yd], axis=-1)
    return y @ w_out

def hierarchical_moe(h, rg_w, rg_b, re_w, re_b, w_gate, w_up, w_down):

    def one_sequence(t):
        n_tok = t.shape[0]
        group_prob = jax.nn.softmax((t @ rg_w).astype(jnp.float32) + rg_b.astype(jnp.float32), axis=-1)
        g_p, g_idx = lax.top_k(group_prob, 1)
        e_logits = ((t @ re_w).astype(jnp.float32) + re_b.astype(jnp.float32)).reshape(
            n_tok, N_EXPERT_GROUPS, EXPERTS_PER_GROUP)
        in_group = jnp.take_along_axis(e_logits, g_idx[:, :, None], axis=1)[:, 0]
        e_top, e_idx = lax.top_k(in_group, TOP_K_INNER)
        e_w = jax.nn.softmax(e_top, axis=-1) * g_p
        flat_idx = g_idx * EXPERTS_PER_GROUP + e_idx
        gates = jnp.sum(jax.nn.one_hot(flat_idx, N_EXPERTS, dtype=jnp.float32) * e_w[..., None], axis=1)
        hg = jnp.einsum('sd,edf->sef', t, w_gate)
        hu = jnp.einsum('sd,edf->sef', t, w_up)
        act = jax.nn.silu(hg) * hu * gates[:, :, None].astype(t.dtype)
        return jnp.einsum('sef,efd->sd', act, w_down)

    return lax.map(one_sequence, h)

def per_layer_embedding(h, p_i, w_proj, g_norm, w_gate):
    e = rmsnorm(p_i @ w_proj, g_norm)
    gate = jax.nn.sigmoid(_rms_unit(h) @ w_gate)
    return h + gate * e

def setup_inputs(seed: int = 0) -> dict:
    key = jax.random.key(seed)
    ks = iter(jax.random.split(key, 32))
    nrm = lambda shape, scale: jax.random.normal(next(ks), shape, jnp.float32) * scale
    gain = lambda shape: 1.0 + 0.02 * jax.random.normal(next(ks), shape, jnp.float32)
    return {
        "x": nrm((BATCH, SEQ, D_MODEL), 1.0),
        "p": nrm((DEPTH, BATCH, SEQ, PLE_DIM), 1.0),
        "norm_mix": gain((DEPTH, D_MODEL)),
        "norm_ffn": gain((DEPTH, D_MODEL)),
        "even_w_in": nrm((N_EVEN, D_MODEL, EVEN_IN), D_MODEL ** -0.5),
        "sgu_w": nrm((N_EVEN, N_HEADS_A, CHUNK, CHUNK), CHUNK ** -0.5),
        "sgu_b": gain((N_EVEN, N_HEADS_A, CHUNK)),
        "sgu_norm": gain((N_EVEN, N_HEADS_A, HEAD_DIM)),
        "even_w_out": nrm((N_EVEN, WIDTH_A + WIDTH_B, D_MODEL), (WIDTH_A + WIDTH_B) ** -0.5),
        "odd_w_in": nrm((N_ODD, D_MODEL, ODD_IN), D_MODEL ** -0.5),
        "forget_bias": jax.random.uniform(next(ks), (N_ODD, N_HEADS_C), jnp.float32, 1.0, 4.0),
        "q_norm": gain((N_ODD, HEAD_DIM)),
        "k_norm": gain((N_ODD, HEAD_DIM)),
        "pool_w": nrm((N_ODD, N_POOL_GROUPS, POOL_GROUP_DIM, POOL_GROUP_DIM), POOL_GROUP_DIM ** -0.5),
        "pool_scale": 1.0 + 0.1 * jax.random.normal(next(ks), (N_ODD, WIDTH_D), jnp.float32),
        "odd_w_out": nrm((N_ODD, WIDTH_C + WIDTH_D, D_MODEL), (WIDTH_C + WIDTH_D) ** -0.5),
        "router_group_w": nrm((DEPTH, D_MODEL, N_EXPERT_GROUPS), D_MODEL ** -0.5),
        "router_group_b": nrm((DEPTH, N_EXPERT_GROUPS), 0.01),
        "router_expert_w": nrm((DEPTH, D_MODEL, N_EXPERTS), D_MODEL ** -0.5),
        "router_expert_b": nrm((DEPTH, N_EXPERTS), 0.01),
        "expert_w_gate": nrm((DEPTH, N_EXPERTS, D_MODEL, D_EXPERT), D_MODEL ** -0.5),
        "expert_w_up": nrm((DEPTH, N_EXPERTS, D_MODEL, D_EXPERT), D_MODEL ** -0.5),
        "expert_w_down": nrm((DEPTH, N_EXPERTS, D_EXPERT, D_MODEL), D_EXPERT ** -0.5),
        "ple_w_proj": nrm((DEPTH, PLE_DIM, D_MODEL), PLE_DIM ** -0.5),
        "ple_norm": gain((DEPTH, D_MODEL)),
        "ple_w_gate": nrm((DEPTH, D_MODEL, D_MODEL), D_MODEL ** -0.5),
    }

def reference(x, p, norm_mix, norm_ffn, even_w_in, sgu_w, sgu_b, sgu_norm, even_w_out,
              odd_w_in, forget_bias, q_norm, k_norm, pool_w, pool_scale, odd_w_out,
              router_group_w, router_group_b, router_expert_w, router_expert_b,
              expert_w_gate, expert_w_up, expert_w_down, ple_w_proj, ple_norm, ple_w_gate):
    h = x
    for i in range(DEPTH):
        j = i // 2
        hn = rmsnorm(h, norm_mix[i])
        if i % 2 == 0:
            h = h + even_mixer(hn, even_w_in[j], sgu_w[j], sgu_b[j], sgu_norm[j], even_w_out[j])
        else:
            h = h + odd_mixer(hn, odd_w_in[j], forget_bias[j], q_norm[j], k_norm[j],
                              pool_w[j], pool_scale[j], odd_w_out[j])
        h = h + hierarchical_moe(rmsnorm(h, norm_ffn[i]), router_group_w[i], router_group_b[i],
                                 router_expert_w[i], router_expert_b[i],
                                 expert_w_gate[i], expert_w_up[i], expert_w_down[i])
        h = per_layer_embedding(h, p[i], ple_w_proj[i], ple_norm[i], ple_w_gate[i])
    return h


_drawn_inputs = setup_inputs


def setup_inputs(seed=0):
    import zlib

    import numpy as np

    out = dict(_drawn_inputs(seed))
    spreads = {}
    factors = {'sgu_b': 2.971,
     'sgu_norm': 4.409,
     'q_norm': 8.0,
     'k_norm': 8.0,
     'router_group_b': 22.626,
     'router_expert_b': 9.736,
     'ple_norm': 3.772,
     'norm_ffn': 3.391,
     'pool_scale': 3.436}
    for name, (base, spread) in spreads.items():
        noise = np.random.default_rng([zlib.crc32(name.encode()), seed]).standard_normal(out[name].shape)
        drawn = base * np.exp(spread * noise) if base else spread * noise
        out[name] = __import__('jax').numpy.asarray(drawn.astype(out[name].dtype))
    for name, factor in factors.items():
        out[name] = (out[name] * factor).astype(out[name].dtype)
    return out
```

```python
from contextlib import ExitStack

import numpy as np
import concourse.bass as bass
from concourse import mybir

F32 = mybir.dt.float32
BF16 = mybir.dt.bfloat16
I32 = mybir.dt.int32
ALU = mybir.AluOpType
ACT = mybir.ActivationFunctionType
AX = mybir.AxisListType.X

P = 128
D = 1024
S = 512
MT = S // P
KD = D // P
HD = 64
NH = 8
W = NH * HD
DEPTH = 2
PLE = 256
KP = PLE // P
NE = 16
NG = 4
EG = NE // NG
DE = 256
OV = 7
TILES = NE + OV
EPS = 1e-6
SCALE = HD ** -0.5
NEG = -1e30
WINDOWS = (2, 4, 8, 16)
BW = P + 16
SMALL = 48


def constants():
    i = np.arange(P)
    ident = np.eye(P, dtype=np.float32)
    strict = np.where(i[None, :] >= i[:, None], NEG, 0.0)
    causal = np.where(i[None, :] > i[:, None], NEG, 0.0)
    before = (i[:, None] < i[None, :]).astype(np.float32)
    cb = np.stack([ident, strict, causal, before, np.ones((P, P))], 1).astype(np.float32)
    upto = (i[:, None] <= i[None, :]).astype(np.float32)
    tril = (i[None, :] <= i[:, None]).astype(np.float32)
    cf = np.stack([ident, upto, np.ones((P, P), np.float32), tril], 1)
    bands = np.zeros((P, 2, len(WINDOWS), BW), np.float32)
    t = np.arange(BW)
    for first in (0, 1):
        for g, win in enumerate(WINDOWS):
            inside = (t[None, :] >= i[:, None]) & (t[None, :] - i[:, None] < win)
            count = np.minimum(t + 1, win) if first else np.full(BW, win)
            bands[:, first, g] = inside / count[None, :].astype(np.float32) - (t[None, :] == i[:, None])
    sel = np.zeros((P, NH, P), np.float32)
    for part in range(3):
        for h in range(NH):
            sel[32 * part + h, h, :] = -1.0 / SCALE
    small = np.zeros((P, SMALL), np.float32)
    small[:, 0:NE] = NE - np.arange(NE)
    small[:, NE:2 * NE] = P * np.arange(NE)
    small[:, 32:32 + OV] = np.arange(OV)
    small[:, 40:44] = -0.5
    return {"c_bf": cb, "c_f": cf, "c_bands": bands, "c_sel": sel, "c_small": small}


def trunk(nc, a, out):
    ctx = ExitStack()
    with ctx:
        def sb(name, shape, dt=F32):
            return ctx.enter_context(nc.sbuf_tensor(name, shape, dt))

        def sem(name):
            return ctx.enter_context(nc.semaphore(name))

        def sems(name, n=DEPTH):
            return [sem(f"{name}{i}") for i in range(n)]

        bank = [ctx.enter_context(nc.psum_tensor(f"bank{i}", [P, 512], F32)) for i in range(8)]

        h = sb("h", [P, MT, D])
        xT = sb("xT", [P, KD, S])
        y = sb("y", [P, MT, D])
        R1 = sb("R1", [P, 4 * S * MT // 2])
        R2 = sb("R2", [P, 4 * S * MT // 2])
        qkT = sb("qkT", [P, 8 * S])
        ring = sb("ring", [P, 2, KD, 512])
        gu = sb("gu", [P, 2, KD, 2 * DE])
        wd = sb("wd", [P, 2, DE // P, D])
        attE = sb("attE", [P, 2, 512])
        attB = sb("attB", [P, 2, 512])
        attS = sb("attS", [P, 2, 513])
        attP = sb("attP", [P, 2, 512])
        cbf = sb("cbf", [P, 5, P], BF16)
        cf = sb("cf", [P, 4, P])
        small = sb("small", [P, SMALL])
        mixw = sb("mixw", [P, 2 * len(WINDOWS) * BW])
        mixg = sb("mixg", [P, 512])
        gmix = sb("gmix", [P, DEPTH, KD])
        gffn = sb("gffn", [P, DEPTH, KD])
        sgb = sb("sgb", [P, NH])
        qkg = sb("qkg", [P, 2])
        pscale = sb("pscale", [P, 4])
        wf = sb("wf", [P, KD, NH])
        fb = sb("fb", [P, NH])
        wr = sb("wr", [P, DEPTH, KD, 20])
        rb = sb("rb", [P, DEPTH, 20])
        ss = sb("ss", [P, DEPTH, 4, MT])
        rr = sb("rr", [P, DEPTH, 4, MT])
        hss = sb("hss", [P, 2, MT * NH])
        hrr = sb("hrr", [P, 2, MT * NH])
        pw = sb("pw", [P, 2 * MT * NH])
        mxs = sb("mxs", [P, 8, MT])
        wts = sb("wts", [P, 2, MT])
        selb = sb("selb", [P, MT, NE], BF16)
        posf = sb("posf", [P, 2, MT])
        posi = sb("posi", [P, 2, MT], I32)
        ove = sb("ove", [1, 8])
        ovi = sb("ovi", [1, 8], I32)
        rs = sb("rs", [P, 4 * NH])
        ri = sb("ri", [P, 4 * NH])
        mx = sb("mx", [P, 4 * NH])
        nb = sb("nb", [P, 4 * NH])
        lf = sb("lf", [P, 4, MT, NH])

        ident, upto, ones, tril = (cf[:, i, :] for i in range(4))
        identb, strictb, causalb, beforeb, onesb = (cbf[:, i, :] for i in range(5))
        rows = lambda x: x.rearrange("p (m n) -> p m n", m=MT)
        VA, Q = rows(R1[:, 0:MT * W]), rows(R1[:, MT * W:])
        K, V = rows(R2[:, 0:MT * W]), rows(R2[:, MT * W:])
        U = y[:, :, 0:W]
        E = rows(R1[:, :])
        zeros = y[:, MT - 1, :]
        G2 = rows(R2[:, :])
        xs = [R2[:, p * D:(p + 1) * D] for p in range(2)]
        ys = [R2[:, (2 + p) * D:(3 + p) * D] for p in range(2)]
        qT = qkT[:, 0:4 * S].rearrange("p (c n) -> p c n", c=4)
        kT = qkT[:, 4 * S:].rearrange("p (c n) -> p c n", c=4)
        xgT = qkT[:, 0:KD * P].rearrange("p (k n) -> p k n", k=KD)
        sil, act, actT = (qkT[:, D + i * DE:D + (i + 1) * DE] for i in range(3))
        pin = qkT[:, 2048:3072].rearrange("p (m n) -> p m n", m=MT)
        pT = qkT[:, 3072:4096].rearrange("p (k n) -> p k n", k=KP)
        pgain = attB[:, :, :].rearrange("p a n -> p (a n)")
        routing = attP[:, :, :].rearrange("p a n -> p (a n)")
        at = [0]

        def part(*shape):
            n = int(np.prod(shape))
            at[0] += n
            x = routing[:, at[0] - n:at[0]]
            names = " ".join(f"d{i}" for i in range(len(shape)))
            return x.rearrange(f"p ({names}) -> p {names}", **{f"d{i}": k for i, k in enumerate(shape)})

        t16, le, lg, exps = part(3, MT, NE), part(MT, NE), part(MT, 20), part(2, MT, 5)
        mask1, mask2, gmask, row16 = part(MT, NE), part(MT, NE), part(MT, NG), part(6, NE)
        ovf = part(OV, NE)[0:1]
        junk = attS[:, :, :].rearrange("p a n -> p (a n)")[:, 0:D]
        gate = attE
        sgw = attP[:, :, :].rearrange("p a (h s) -> p (a h) s", s=P)
        sguT = mixw[:, 0:NH * P].rearrange("p (h t) -> p h t", h=NH)
        bands = mixw[:, :].rearrange("p (f g t) -> p f g t", f=2, g=4)
        poolw = mixg[:, :].rearrange("p (g d) -> p g d", g=4)
        self_ = attE[:, 0, :].bitcast(BF16).rearrange("p (h n) -> p h n", h=NH)
        Fp = attE[:, 1, :].bitcast(BF16)[:, 0:S]
        Frow = attS[0:NH, 0, 0:S]
        Frest = attS[0:NH, 1, 0:S]
        pT2 = attP

        xg = nc.dram_tensor("xg", [TILES * P, D], F32, kind="Internal").ap()
        yg = nc.dram_tensor("yg", [TILES * P, D], F32, kind="Internal").ap()

        s_cbf, s_selin = sem("s_cbf"), sem("s_selin")
        s_const, s_ident, s_zero, s_xgz = sem("s_const"), sem("s_ident"), sem("s_zero"), sem("s_xgz")
        s_in = sems("s_in", MT)
        s_ring = sems("s_ring", 2)
        s_mixin, s_pin, s_pg = sem("s_mixin"), sems("s_pin"), sems("s_pg")
        s_ss, s_rr = sem("s_ss"), sem("s_rr")
        s_t, s_tD, s_tA = sem("s_t"), sem("s_tD"), sem("s_tA")
        s_m, s_mD, s_mA = sem("s_m"), sem("s_mD"), sem("s_mA")
        s_z, s_pr, s_w, s_pt, s_ptv, s_o, s_ov = (sems(n) for n in ("s_z", "s_pr", "s_w", "s_pt", "s_ptv", "s_o", "s_ov"))
        s_qn, s_hs, s_hr = sems("s_qn"), sems("s_hs"), sems("s_hr")
        s_y, s_mixd, s_gel, s_sg, s_sgT = sems("s_y"), sem("s_mixd"), sem("s_gel"), sem("s_sg"), sem("s_sgT")
        s_f, s_fa, s_fl, s_fc, s_fp = (sem(n) for n in ("s_f", "s_fa", "s_fl", "s_fc", "s_fp"))
        s_pl, s_plv, s_pm = sem("s_pl"), sem("s_plv"), sem("s_pm")
        s_xn, s_lg, s_lgv, s_ex, s_sel, s_rank, s_pos = (sems(n) for n in ("s_xn", "s_lg", "s_lgv", "s_ex", "s_sel", "s_rank", "s_pos"))
        s_sc, s_xl, s_gu, s_wd = sems("s_sc"), [sems(f"s_xl{l}_", 2) for l in range(2)], [sems(f"s_gu{l}_", 2) for l in range(2)], [sems(f"s_wd{l}_", 2) for l in range(2)]
        s_tx, s_xv, s_g, s_sil, s_act, s_at, s_atv = (sems(n) for n in ("s_tx", "s_xv", "s_g", "s_sil", "s_act", "s_at", "s_atv"))
        s_dn, s_yD, s_yA, s_st = sems("s_dn"), sems("s_yD"), sems("s_yA"), [sems(f"s_st{l}_", 2) for l in range(2)]
        o_ld, o_st, o_end = sems("o_ld"), sems("o_st"), sems("o_end")
        s_ga, s_cmb, s_e, s_pse, s_gt, s_h = sems("s_ga"), sems("s_cmb"), sems("s_e"), sems("s_pse"), sems("s_gt"), sems("s_h")
        s_dve, s_act_, s_pool = sem("s_dve"), sem("s_actchain"), sem("s_poolchain")
        s_out = sem("s_out")

        def cols(w, c, k=KD):
            return w[:, c * 512:(c + 1) * 512].rearrange("(k p) n -> p k n", p=P)

        wi, wo = a["even_w_in"][0], a["even_w_out"][0]
        oi, oo = a["odd_w_in"][0], a["odd_w_out"][0]
        XD0 = 3 * W + NH
        chunks = [cols(wi, c) for c in (2, 3, 4, 1, 0)] + [cols(wo, 0), cols(wo, 1)]
        first = [0]
        ffn = []
        for l in range(DEPTH):
            ffn.append(len(chunks))
            chunks += [None, cols(a["ple_w_gate"][l], 0), cols(a["ple_w_gate"][l], 1)]
            if l == 0:
                first.append(len(chunks))
                chunks += [cols(oi, 0), cols(oi, 1), cols(oi, 2), oi[:, XD0:XD0 + W].rearrange("(k p) n -> p k n", p=P)]
                chunks += [cols(oo, 0), cols(oo, 1)]
        NIN = [5, 4]

        def chunk_ready(pe, c):
            pe.wait_ge(s_ring[c % 2], 16 * (c // 2 + 1))

        TM, TF, TY, TP, TQ = range(5)
        GI, GO, GE, GG = range(4)
        SM, SF, SE, SP_ = range(4)

        before_t, before_m, before_mD, before_mA = {}, {}, {}, {}
        nt = nm = nD = nA = 0
        for l in range(DEPTH):
            for which, steps in ((TM, KD), (TQ, 8), (TY, [8, 4][l]), (TF, KD), (TP, KD)):
                before_t[l, which] = nt
                nt += steps
            for which, groups, byD, byA in ((GI, MT * NIN[l], MT * NIN[l] // 2, MT * NIN[l] // 2),
                                            (GO, 2 * MT, 2 * MT, 0), (GE, 2 * MT, 2 * MT, 0), (GG, 2 * MT, 0, 0)):
                before_m[l, which], before_mD[l, which], before_mA[l, which] = nm, nD, nA
                nm, nD, nA = nm + groups, nD + byD, nA + byA

        def steps_turned(l, which, n):
            return before_t[l, which] + n

        def steps_moved(l, which, n):
            return before_t[l, which] // 2 + n

        def groups_done(l, which, n):
            return before_m[l, which] + n

        def movedD(l, which, n):
            return before_mD[l, which] + n

        def movedA(l, which, n):
            return before_mA[l, which] + n

        last_group = []
        for l in range(DEPTH):
            last_group += [groups_done(l, GI, MT * (j + 1)) for j in range(NIN[l])]
            last_group += [groups_done(l, which, 2 * MT) for which in (GO, GO, GE, GG, GG)]

        block = ctx.enter_context(nc.Block())

        @block.sync
        def _(sp):
            def chunk(c):
                if c >= 2:
                    sp.wait_ge(s_m, last_group[c - 2])
                if chunks[c] is None:
                    l = ffn.index(c)
                    sp.dma_start(ring[:, c % 2, 0:2 * KP, :].rearrange("p (k n) c -> p k (n c)", k=KP),
                                 a["ple_w_proj"][l].rearrange("(k p) n -> p k n", p=P)).then_inc(s_ring[c % 2], 16)
                else:
                    sp.dma_start(ring[:, c % 2, :, :], chunks[c]).then_inc(s_ring[c % 2], 16)

            def load_gu(l, e, p):
                sp.dma_start(gu[:, p, :, 0:DE], a["expert_w_gate"][l, e].rearrange("(k p) f -> p k f", p=P)).then_inc(s_gu[l][p], 16)
                sp.dma_start(gu[:, p, :, DE:], a["expert_w_up"][l, e].rearrange("(k p) f -> p k f", p=P)).then_inc(s_gu[l][p], 16)

            def load_wd(l, e, p):
                sp.dma_start(wd[:, p, :, :], a["expert_w_down"][l, e].rearrange("(k p) n -> p k n", p=P)).then_inc(s_wd[l][p], 16)

            chunk(0)
            chunk(1)
            sp.wait_ge(s_zero, 1)
            sp.dma_start(xg.rearrange("(t p) d -> p t d", p=P),
                         zeros.unsqueeze(1).to_broadcast([P, TILES, D])).then_inc(s_xgz, 16)
            sp.dma_start(yg[NE * P:, :].rearrange("(t p) d -> p t d", p=P),
                         zeros.unsqueeze(1).to_broadcast([P, OV, D])).then_inc(s_xgz, 16)
            for l in range(DEPTH):
                for c in range(first[l] + 2, ffn[l]):
                    chunk(c)
                    if l == 0 and c == 2:
                        for e in range(2):
                            load_gu(0, e, e)
                            load_wd(0, e, e)
                if l == 1:
                    for e in range(2):
                        load_gu(1, e, e)
                        load_wd(1, e, e)
                sp.wait_ge(s_t, steps_turned(l, TY, 8 if l == 0 else 4))
                sp.dma_start(pgain, a["ple_norm"][l].partition_broadcast(P)).then_inc(s_pg[l], 16)
                sp.dma_start(pin, a["p"][l, 0].rearrange("(m p) n -> p m n", p=P)).then_inc(s_pin[l], 16)
                for c in range(ffn[l], ffn[l] + 3):
                    chunk(c)
                sp.wait_ge(s_sc[l], 16 * 2 * MT)
                for e in range(2):
                    sp.dma_start(xs[e], xg[e * P:(e + 1) * P, :]).then_inc(s_xl[l][e], 16)
                with sp.Fori(1, NE // 2) as i:
                    for p in range(2):
                        e = 2 * i + p
                        sp.wait_ge(s_tx[l], 2 * (e - 1))
                        sp.dma_start(xs[p], xg.rearrange("(t p) d -> t p d", p=P)[bass.ds(e, 1), :, :].rearrange("t p d -> p (t d)"))\
                            .then_inc(s_xl[l][p], 16)
                        sp.wait_ge(s_g[l], e - 1)
                        sp.dma_start(gu[:, p, :, 0:DE], a["expert_w_gate"][l, bass.ds(e, 1)].rearrange("e (k p) f -> p (e k) f", p=P))\
                            .then_inc(s_gu[l][p], 16)
                        sp.dma_start(gu[:, p, :, DE:], a["expert_w_up"][l, bass.ds(e, 1)].rearrange("e (k p) f -> p (e k) f", p=P))\
                            .then_inc(s_gu[l][p], 16)
                sp.wait_ge(s_dn[l], 2 * NE)
                sp.wait_ge(s_st[l][0], 16 * NE // 2)
                n = sp.value_load(ovi[0:1, OV:OV + 1], min_val=0, max_val=OV)
                with sp.If(n > 0):
                    with sp.Fori(0, n) as i:
                        sp.wait_ge(s_dn[l], 2 * (i + NE))
                        e = sp.value_load(ovi[0:1, bass.ds(i, 1)], min_val=0, max_val=NE - 1)
                        sp.dma_start(xs[0], xg.rearrange("(t p) d -> t p d", p=P)[bass.ds(i + NE, 1), :, :].rearrange("t p d -> p (t d)"))\
                            .then_inc(o_ld[l], 16)
                        sp.dma_start(gu[:, 0, :, 0:DE], a["expert_w_gate"][l, bass.ds(e, 1)].rearrange("e (k p) f -> p (e k) f", p=P))\
                            .then_inc(o_ld[l], 16)
                        sp.dma_start(gu[:, 0, :, DE:], a["expert_w_up"][l, bass.ds(e, 1)].rearrange("e (k p) f -> p (e k) f", p=P))\
                            .then_inc(o_ld[l], 16)
                        sp.dma_start(wd[:, 0, :, :], a["expert_w_down"][l, bass.ds(e, 1)].rearrange("e (k p) n -> p (e k) n", p=P))\
                            .then_inc(o_ld[l], 16)
                if l == 0:
                    sp.wait_ge(s_h[0], 2 * MT)
                    sp.dma_start(mixw[:, :], a["c_bands"].rearrange("p f g t -> p (f g t)")).then_inc(s_mixin, 16)
                    sp.dma_start(poolw, a["pool_w"][0].rearrange("g c d -> c g d")).then_inc(s_mixin, 16)
                    for c in range(first[1], first[1] + 2):
                        chunk(c)

        @block.scalar
        def _(sc):
            A = nc.scalar
            chain = [0]

            def link(ins):
                chain[0] += 1
                ins.then_inc(s_act_, 1)
                sc.wait_ge(s_act_, chain[0])

            sc.dma_start(cf[:, :, :], a["c_f"]).then_inc(s_ident, 16)
            for m in range(MT):
                sc.dma_start(h[:, m, :], a["x"][0, m * P:(m + 1) * P, :]).then_inc(s_in[m], 16)
            with nc.allow_non_contiguous_dma(reason="gain columns"):
                for dst, src in ((small[:, :], a["c_small"]),
                                 (gmix[:, :, :], a["norm_mix"].rearrange("l (k p) -> p l k", p=P)),
                                 (gffn[:, :, :], a["norm_ffn"].rearrange("l (k p) -> p l k", p=P)),
                                 (sgb[:, :], a["sgu_b"][0].rearrange("h t -> t h")),
                                 (qkg[0:HD, 0:1], a["q_norm"][0].unsqueeze(1)), (qkg[HD:P, 0:1], a["q_norm"][0].unsqueeze(1)),
                                 (qkg[0:HD, 1:2], a["k_norm"][0].unsqueeze(1)), (qkg[HD:P, 1:2], a["k_norm"][0].unsqueeze(1)),
                                 (pscale[:, :], a["pool_scale"][0].rearrange("(g p) -> p g", p=P)),
                                 (wf[:, :, :], oi[:, 3 * W:3 * W + NH].rearrange("(k p) n -> p k n", p=P)),
                                 (fb[:, :], a["forget_bias"][0].partition_broadcast(P)),
                                 (wr[:, 0, :, 0:4], a["router_group_w"][0].rearrange("(k p) n -> p k n", p=P)),
                                 (wr[:, 1, :, 0:4], a["router_group_w"][1].rearrange("(k p) n -> p k n", p=P)),
                                 (wr[:, 0, :, 4:20], a["router_expert_w"][0].rearrange("(k p) n -> p k n", p=P)),
                                 (wr[:, 1, :, 4:20], a["router_expert_w"][1].rearrange("(k p) n -> p k n", p=P)),
                                 (rb[:, 0, 0:4], a["router_group_b"][0].partition_broadcast(P)),
                                 (rb[:, 1, 0:4], a["router_group_b"][1].partition_broadcast(P)),
                                 (rb[:, 0, 4:20], a["router_expert_b"][0].partition_broadcast(P)),
                                 (rb[:, 1, 4:20], a["router_expert_b"][1].partition_broadcast(P)),
                                 (sgw, a["sgu_w"][0].rearrange("h t s -> t h s")),
                                 (mixg[:, :], a["sgu_norm"][0].rearrange("h d -> (h d)").partition_broadcast(P))):
                    sc.dma_start(dst, src).then_inc(s_const, 16)

            def stat(l, which, src, dst):
                done = MT * (4 * l + which) + dst
                if done:
                    sc.wait_ge(s_ss, done)
                A.activation(junk, src, ACT.Square, accum_out=ss[:, l, which, dst:dst + 1]).then_inc(s_ss, 1)

            def turn(l, which, n, put):
                for j in range(1, n, 2):
                    sc.wait_ge(s_t, steps_turned(l, which, j + 1))
                    put(j).then_inc(s_tA, 1)

            for l in range(DEPTH):
                for m in range(MT):
                    if l == 0:
                        sc.wait_ge(s_in[m], 16)
                    else:
                        sc.wait_ge(s_h[0], 2 * (m + 1))
                    stat(l, SM, h[:, m, :], m)
                if l == 0:
                    sc.wait_ge(s_const, 16 * 21)
                turn(l, TM, KD, lambda j: A.mul(xT[:, j, :], bank[4 + j % 4][:, :], gmix[:, l, j:j + 1]))
                sc.wait_ge(s_rr, 4 * l + SM + 1)
                dst = [[Q, K, V, VA, U], [Q, K, V, y[:, :, W:]]][l]
                for g in range(1, MT * NIN[l], 2):
                    c, m = g // MT, g % MT
                    sc.wait_ge(s_m, groups_done(l, GI, g + 1))
                    if l == 0 and g == 4 * MT + 1:
                        sc.wait_ge(s_xgz, 32)
                    A.mul(dst[c][:, m, :], bank[g % 4][:, :], rr[:, l, SM, m:m + 1]).then_inc(s_mA, 1)
                if l == 1:
                    sc.wait_ge(s_f, 1)
                    link(A.activation(lf[:, 1, :, :], lf[:, 0, :, :], ACT.Abs))
                    link(A.activation(lf[:, 1, :, :], lf[:, 1, :, :], ACT.Exp, scale=-1.0))
                    A.activation(lf[:, 2, :, :], lf[:, 1, :, :], ACT.Ln, bias=1.0).then_inc(s_fl, 1)
                    turn(1, TQ, 8, lambda j: A.mul(qT[:, j, :] if j < 4 else kT[:, j - 4, :], bank[4 + j % 4][:, :],
                                                   qkg[:, j // 4:j // 4 + 1]))
                else:
                    turn(0, TQ, 8, lambda j: A.copy(qT[:, j, :] if j < 4 else kT[:, j - 4, :], bank[4 + j % 4][:, :]))
                for v in range(4 * NH + 2):
                    if v < 4 * NH:
                        n = (v % 4 + 1) * P
                        sc.wait_ge(s_z[l], v + 1)
                        if v >= 2:
                            sc.wait_ge(s_pt[l], v - 1)
                        if l == 0:
                            A.activation(attE[:, v % 2, 512 - n:512], bank[v % 2][:, 0:n], ACT.Sigmoid, scale=-SCALE)
                            A.activation(attB[:, v % 2, 0:n], bank[v % 2][:, 0:n], ACT.Sigmoid, scale=SCALE).then_inc(s_pr[0], 1)
                        else:
                            sc.wait_ge(s_w[1], v + 1)
                            A.activation(attB[:, v % 2, 0:n], bank[v % 2][:, 0:n], ACT.Exp, scale=SCALE,
                                         bias=nb[:, v:v + 1], accum_out=rs[:, v:v + 1]).then_inc(s_pr[1], 1)
                    if v >= 2:
                        u = v - 2
                        n = (u % 4 + 1) * P
                        sc.wait_ge(s_pt[l], u + 1)
                        A.copy(attP[:, u % 2, 0:n], bank[2 + u % 2][:, 0:n]).then_inc(s_ptv[l], 1)
                if l == 0:
                    sc.wait_ge(s_mD, movedD(0, GI, MT * NIN[0] // 2))
                    sc.wait_ge(s_mA, movedA(0, GI, MT * NIN[0] // 2))
                    A.activation(VA, VA, ACT.Gelu_apprx_tanh).then_inc(s_gel, 1)
                    A.activation(U, U, ACT.Gelu_apprx_tanh).then_inc(s_gel, 1)
                if l == 0:
                    turn(0, TY, 8, lambda j: A.copy(xT[:, j, :], bank[4 + j % 4][:, :]))
                else:
                    turn(1, TY, 4, lambda j: A.copy(xT[:, j, :], bank[4 + j % 4][:, :]))
                for m in range(MT):
                    sc.wait_ge(s_mD, movedD(l, GO, 2 * (m + 1)))
                    stat(l, SF, h[:, m, :], m)
                sc.wait_ge(s_rr, 4 * l + SF + 1)
                for m in range(1, MT, 2):
                    A.mul(y[:, m, :], h[:, m, :], rr[:, l, SF, m:m + 1]).then_inc(s_xn[l], 1)
                turn(l, TF, KD, lambda j: A.mul(xT[:, j, :], bank[4 + j % 4][:, :], gffn[:, l, j:j + 1]))
                sc.wait_ge(s_lgv[l], 1)
                A.activation(exps[:, 1, :, :], exps[:, 0, :, :], ACT.Exp).then_inc(s_ex[l], 1)
                for m in range(MT):
                    sc.wait_ge(s_mD, movedD(l, GE, 2 * (m + 1)))
                    stat(l, SE, E[:, m, :], m)

                def silu(e):
                    sc.wait_ge(s_g[l], e + 1)
                    A.activation(sil, bank[2][:, 0:DE], ACT.Silu).then_inc(s_sil[l], 1)

                def act_moved(e):
                    sc.wait_ge(s_at[l], e + 1)
                    A.copy(actT, bank[3][:, 0:DE]).then_inc(s_atv[l], 1)

                def result(e, p):
                    sc.wait_ge(s_dn[l], 2 * e + 2)
                    A.copy(ys[p][:, 512:D], bank[5][:, :]).then_inc(s_yA[l], 1)

                def store(e, p, done):
                    sc.wait_ge(s_yD[l], e + 1)
                    sc.wait_ge(s_yA[l], e + 1)
                    sc.dma_start(yg.rearrange("(t p) d -> t p d", p=P)[bass.ds(e, 1), :, :].rearrange("t p d -> p (t d)"), ys[p])\
                        .then_inc(done, 16)

                def stage(e, p, i, stored):
                    silu(e - 1)
                    if stored:
                        sc.wait_ge(s_st[l][p], 16 * (i - 1))
                    result(e - 2, p)
                    sc.dma_start(wd[:, p, :, :], a["expert_w_down"][l, bass.ds(e, 1)].rearrange("e (k p) n -> p (e k) n", p=P))\
                        .then_inc(s_wd[l][p], 16)
                    act_moved(e - 1)
                    store(e - 2, p, s_st[l][p])

                silu(0)
                act_moved(0)
                stage(2, 0, 1, False)
                stage(3, 1, 1, False)
                with sc.Fori(2, NE // 2) as i:
                    for p in range(2):
                        stage(2 * i + p, p, i, True)
                sc.wait_ge(s_st[l][0], 16 * (NE // 2 - 1))
                result(NE - 2, 0)
                store(NE - 2, 0, s_st[l][0])
                silu(NE - 1)
                act_moved(NE - 1)
                sc.wait_ge(s_st[l][1], 16 * (NE // 2 - 1))
                result(NE - 1, 1)
                store(NE - 1, 1, s_st[l][1])
                sc.wait_ge(s_st[l][0], 16 * NE // 2)
                n = sc.value_load(ovi[0:1, OV:OV + 1], min_val=0, max_val=OV)
                with sc.If(n > 0):
                    with sc.Fori(0, n) as i:
                        silu(i + NE)
                        act_moved(i + NE)
                        result(i + NE, 0)
                        store(i + NE, 0, o_st[l])
                        sc.wait_ge(o_st[l], 16 * i + 16)
                sc.sem_inc(o_end[l], 1)
                for m in range(MT):
                    sc.wait_ge(s_cmb[l], m + 1)
                    stat(l, SP_, h[:, m, :], m)
                turn(l, TP, KD, lambda j: A.copy(xT[:, j, :], bank[4 + j % 4][:, :]))
                sc.wait_ge(s_rr, 4 * l + SP_ + 1)
                for g in range(2 * MT):
                    m = g // 2
                    sc.wait_ge(s_m, groups_done(l, GG, g + 1))
                    if g >= 2:
                        sc.wait_ge(s_h[l], g - 1)
                    A.activation(gate[:, g % 2, :], bank[g % 4][:, :], ACT.Sigmoid, scale=rr[:, l, SP_, m:m + 1])\
                        .then_inc(s_gt[l], 1)
            for m in range(MT):
                sc.wait_ge(s_h[1], 2 * (m + 1))
                sc.dma_start(out[0, m * P:(m + 1) * P, :], h[:, m, :]).then_inc(s_out, 16)
            sc.wait_ge(s_out, 16 * MT)

        @block.gpsimd
        def _(pool):
            G = nc.gpsimd
            chain = [0]

            def link(ins):
                chain[0] += 1
                ins.then_inc(s_pool, 1)
                pool.wait_ge(s_pool, chain[0])

            pool.dma_start(cbf[:, :, :], a["c_bf"]).then_inc(s_cbf, 16)
            G.memset(zeros, 0.0).then_inc(s_zero, 1)
            link(G.memset(pw[:, :], -0.5))

            def root(dst, src, n, width, done):
                link(G.tensor_scalar(dst, src, 1.0 / n, EPS, ALU.mult, ALU.add))
                G.tensor_tensor(dst, dst, pw[:, 0:width], ALU.pow).then_inc(done, 1)

            def stat(l, which):
                pool.wait_ge(s_ss, MT * (4 * l + which + 1))
                root(rr[:, l, which, :], ss[:, l, which, :], D, MT, s_rr)

            for l in range(DEPTH):
                stat(l, SM)
                n = [1, 2][l]
                pool.wait_ge(s_hs[l], n)
                root(hrr[:, 0:n, :].rearrange("p a b -> p (a b)"), hss[:, 0:n, :].rearrange("p a b -> p (a b)"),
                     HD, n * MT * NH, s_hr[l])
                stat(l, SF)
                if l == 0:
                    pool.wait_ge(s_xgz, 32)
                pool.wait_ge(s_xn[l], MT)
                pool.wait_ge(s_pos[l], 1)
                for j in range(2):
                    for m in range(MT):
                        G.indirect_dma_start(xg, bass.IndirectOffsetOnAxis(posi[:, j, m:m + 1], 0), y[:, m, :], None)\
                            .then_inc(s_sc[l], 16)
                stat(l, SE)
                pool.wait_ge(s_st[l][0], 16 * NE // 2)
                pool.wait_ge(s_st[l][1], 16 * NE // 2)
                pool.wait_ge(o_end[l], 1)
                pool.wait_ge(s_sc[l], 16 * 2 * MT)
                for m in range(MT):
                    for j, dst in enumerate((y, G2)):
                        G.indirect_dma_start(dst[:, m, :], None, yg, bass.IndirectOffsetOnAxis(posi[:, j, m:m + 1], 0))\
                            .then_inc(s_ga[l], 16)
                stat(l, SP_)
                if l == 0:
                    pool.wait_ge(s_h[0], 2 * MT)
                    pool.dma_start(self_, a["c_sel"]).then_inc(s_selin, 16)

        @block.vector
        def _(dve):
            Ve = nc.vector
            chain = [0]

            def link(ins):
                chain[0] += 1
                ins.then_inc(s_dve, 1)
                dve.wait_ge(s_dve, chain[0])

            def turn(l, which, n, put):
                for j in range(0, n, 2):
                    dve.wait_ge(s_t, steps_turned(l, which, j + 1))
                    put(j).then_inc(s_tD, 1)

            def over(x, n):
                return x.unsqueeze(2).to_broadcast([P, MT, n])

            def first_max(values, n, top, mask, t):
                link(Ve.tensor_reduce(top, values, AX, ALU.max))
                link(Ve.tensor_tensor(t[0], values, over(top, n), ALU.is_ge))
                link(Ve.tensor_tensor(t[1], t[0], small[:, NE - n:NE].unsqueeze(1).to_broadcast([P, MT, n]), ALU.mult))
                link(Ve.tensor_reduce(mxs[:, 7, :], t[1], AX, ALU.max))
                link(Ve.tensor_tensor(mask, t[1], over(mxs[:, 7, :], n), ALU.is_equal))

            dve.wait_ge(s_const, 16 * 21)
            Ve.tensor_tensor(sgw, sgw, tril.unsqueeze(1).to_broadcast([P, NH, P]), ALU.mult).then_inc(s_sg, 1)
            for l in range(DEPTH):
                turn(l, TM, KD, lambda j: Ve.tensor_scalar(xT[:, j, :], bank[4 + j % 4][:, :], gmix[:, l, j:j + 1], None, ALU.mult))
                dve.wait_ge(s_rr, 4 * l + SM + 1)
                if l == 0:
                    for b in range(2):
                        dve.wait_ge(s_sgT, b + 1)
                        Ve.tensor_copy(sguT[:, 4 * b:4 * b + 4, :].rearrange("p h t -> p (h t)"), bank[6 + b][:, :]).then_inc(s_mixd, 1)
                dst = [[Q, K, V, VA, U], [Q, K, V, y[:, :, W:]]][l]
                for g in range(0, MT * NIN[l], 2):
                    c, m = g // MT, g % MT
                    dve.wait_ge(s_m, groups_done(l, GI, g + 1))
                    Ve.tensor_scalar(dst[c][:, m, :], bank[g % 4][:, :], rr[:, l, SM, m:m + 1], None, ALU.mult).then_inc(s_mD, 1)
                heads = lambda x: x.rearrange("p m (h d) -> p (m h) d", d=HD)
                if l == 0:
                    link(Ve.memset(attS[:, :, 512:513], 1.0))
                    turn(0, TQ, 8, lambda j: Ve.tensor_copy(qT[:, j, :] if j < 4 else kT[:, j - 4, :], bank[4 + j % 4][:, :]))
                else:
                    dve.wait_ge(s_fa, 1)
                    link(Ve.tensor_tensor(lf[:, 3, :, :], bank[4][:, 0:MT * NH].rearrange("p (m h) -> p m h", h=NH),
                                          over(rr[:, 1, SM, :], NH), ALU.mult))
                    Ve.tensor_tensor(lf[:, 0, :, :], lf[:, 3, :, :], fb[:, :].unsqueeze(1).to_broadcast([P, MT, NH]), ALU.add).then_inc(s_f, 1)
                    dve.wait_ge(s_mA, movedA(1, GI, MT * NIN[1] // 2))
                    dve.wait_ge(s_mD, movedD(1, GI, MT * NIN[1] // 2))
                    sq = attB[:, :, :].rearrange("p a n -> p (a n)")
                    for b, x in enumerate((Q, K)):
                        if b:
                            dve.wait_ge(s_hs[1], 1)
                        for c in range(2):
                            part = x[:, 2 * c:2 * c + 2, :]
                            link(Ve.tensor_tensor(sq.rearrange("p (m n) -> p m n", m=2), part, part, ALU.mult))
                            ins = Ve.tensor_reduce(hss[:, b, 16 * c:16 * c + 16], sq.rearrange("p (a d) -> p a d", d=HD), AX, ALU.add)
                            if c == 0:
                                link(ins)
                            else:
                                ins.then_inc(s_hs[1], 1)
                    dve.wait_ge(s_fl, 1)
                    dve.wait_ge(s_f, 1)
                    Ve.scalar_tensor_tensor(lf[:, 3, :, :], lf[:, 0, :, :], 0.0, lf[:, 2, :, :], ALU.min, ALU.subtract).then_inc(s_fc, 1)
                    dve.wait_ge(s_hr[1], 1)
                    for b, x in enumerate((Q, K)):
                        Ve.tensor_tensor(heads(x), heads(x), hrr[:, b, :].unsqueeze(2).to_broadcast([P, MT * NH, HD]), ALU.mult)\
                            .then_inc(s_qn[1], 1)
                    dve.wait_ge(s_fa, 2)
                    link(Ve.memset(Fp[0:96, :], 0.0))
                    link(Ve.tensor_copy(Frow, bank[3][0:NH, :]))
                    link(Ve.tensor_copy(Fp[0:NH, :], Frow))
                    link(Ve.tensor_tensor(Frest, Frow, Fp[0:NH, :], ALU.subtract))
                    link(Ve.tensor_copy(Fp[32:32 + NH, :], Frest))
                    link(Ve.tensor_copy(Frow, Fp[32:32 + NH, :]))
                    link(Ve.tensor_tensor(Frest, Frest, Frow, ALU.subtract))
                    Ve.tensor_copy(Fp[64:64 + NH, :], Frest).then_inc(s_fp, 1)
                    turn(1, TQ, 8, lambda j: Ve.tensor_scalar(qT[:, j, :] if j < 4 else kT[:, j - 4, :], bank[4 + j % 4][:, :],
                                                              qkg[:, j // 4:j // 4 + 1], None, ALU.mult))

                def head_out(hd):
                    dve.wait_ge(s_o[l], hd + 1)
                    o = bank[6 + hd % 2][:, 0:MT * HD].rearrange("p (m d) -> p m d", d=HD)
                    c0 = (W if l == 0 else 0) + hd * HD
                    if l == 0:
                        Ve.tensor_copy(y[:, :, c0:c0 + HD], o).then_inc(s_ov[0], 1)
                    else:
                        link(Ve.reciprocal(ri[:, 4 * hd:4 * hd + 4], rs[:, 4 * hd:4 * hd + 4]))
                        Ve.tensor_tensor(y[:, :, c0:c0 + HD], o, over(ri[:, 4 * hd:4 * hd + 4], HD), ALU.mult).then_inc(s_ov[1], 1)

                for v in range(4 * NH + 4):
                    if v < 4 * NH:
                        n = (v % 4 + 1) * P
                        b = v % 2
                        if l == 0:
                            dve.wait_ge(s_pr[0], v + 1)
                            link(Ve.tensor_tensor_scan(attS[:, b, 512 - n:512][:, ::-1], attE[:, b, 512 - n:512][:, ::-1],
                                                       attE[:, b, 512 - n:512][:, ::-1], 1.0, ALU.mult, ALU.bypass))
                            Ve.tensor_tensor(attB[:, b, 0:n], attB[:, b, 0:n], attS[:, b, 513 - n:513], ALU.mult).then_inc(s_w[0], 1)
                        else:
                            dve.wait_ge(s_z[1], v + 1)
                            link(Ve.tensor_reduce(mx[:, v:v + 1], bank[b][:, 0:n], AX, ALU.max))
                            Ve.tensor_scalar(nb[:, v:v + 1], mx[:, v:v + 1], -SCALE, None, ALU.mult).then_inc(s_w[1], 1)
                    if v >= 7 and v % 4 == 3:
                        head_out((v - 7) // 4)
                if l == 0:
                    dve.wait_ge(s_gel, 1)
                    sq = attB[:, :, :].rearrange("p a n -> p (a n)")
                    for c in range(2):
                        part = VA[:, 2 * c:2 * c + 2, :]
                        link(Ve.tensor_tensor(sq.rearrange("p (m n) -> p m n", m=2), part, part, ALU.mult))
                        ins = Ve.tensor_reduce(hss[:, 0, 16 * c:16 * c + 16], sq.rearrange("p (a d) -> p a d", d=HD), AX, ALU.add)
                        if c == 0:
                            link(ins)
                        else:
                            ins.then_inc(s_hs[0], 1)
                    dve.wait_ge(s_hr[0], 1)
                    link(Ve.tensor_tensor(heads(VA), heads(VA), hrr[:, 0, :].unsqueeze(2).to_broadcast([P, MT * NH, HD]), ALU.mult))
                    Ve.tensor_tensor(VA, VA, mixg[:, :].unsqueeze(1).to_broadcast([P, MT, W]), ALU.mult).then_inc(s_qn[0], 1)
                    dve.wait_ge(s_gel, 2)
                    for hd in range(NH):
                        if hd % 2 == 0:
                            dve.wait_ge(s_pm, hd // 2 + 1)
                        o = bank[hd // 2][:, 256 * (hd % 2):256 * (hd % 2) + 256].rearrange("p (m d) -> p m d", d=HD)
                        u = U[:, :, hd * HD:(hd + 1) * HD]
                        Ve.scalar_tensor_tensor(u, o, sgb[:, hd:hd + 1], u, ALU.add, ALU.mult).then_inc(s_y[0], 1)
                    turn(0, TY, 8, lambda j: Ve.tensor_copy(xT[:, j, :], bank[4 + j % 4][:, :]))
                else:
                    turn(1, TY, 4, lambda j: Ve.tensor_copy(xT[:, j, :], bank[4 + j % 4][:, :]))
                    for g in range(4):
                        dve.wait_ge(s_pl, g + 1)
                        Ve.tensor_copy(pT2[:, g % 2, :], bank[g % 2][:, :]).then_inc(s_plv, 1)
                        dve.wait_ge(s_pm, 4 + g + 1)
                        Ve.tensor_scalar(xT[:, 4 + g, :], bank[2 + g % 2][:, :], pscale[:, g:g + 1], None, ALU.mult).then_inc(s_y[1], 1)
                for g in range(2 * MT):
                    m, c = g // 2, g % 2
                    dve.wait_ge(s_m, groups_done(l, GO, g + 1))
                    hh = h[:, m, c * 512:(c + 1) * 512]
                    Ve.tensor_tensor(hh, hh, bank[g % 4][:, :], ALU.add).then_inc(s_mD, 1)
                dve.wait_ge(s_rr, 4 * l + SF + 1)
                dve.wait_ge(s_mD, movedD(l, GO, 2 * MT))
                for m in range(0, MT, 2):
                    Ve.tensor_scalar(y[:, m, :], h[:, m, :], rr[:, l, SF, m:m + 1], None, ALU.mult).then_inc(s_xn[l], 1)
                turn(l, TF, KD, lambda j: Ve.tensor_scalar(xT[:, j, :], bank[4 + j % 4][:, :], gffn[:, l, j:j + 1], None, ALU.mult))
                dve.wait_ge(s_lg[l], 1)
                lp = bank[0][:, 0:MT * 20].rearrange("p (m n) -> p m n", n=20)
                Ve.tensor_tensor(lg[:, :, 0:4], lp[:, :, 0:4], rb[:, l, 0:4].unsqueeze(1).to_broadcast([P, MT, 4]), ALU.add)
                link(Ve.tensor_tensor(le[:, :, :], lp[:, :, 4:20], rb[:, l, 4:20].unsqueeze(1).to_broadcast([P, MT, NE]), ALU.add))
                first_max(lg[:, :, 0:4], NG, mxs[:, 0, :], gmask[:, :, :], (t16[:, 0, :, 0:NG], t16[:, 1, :, 0:NG]))
                Ve.tensor_tensor(exps[:, 0, :, 0:4], lg[:, :, 0:4], over(mxs[:, 0, :], NG), ALU.subtract)
                link(Ve.tensor_scalar(t16[:, 2, :, 0:NG], gmask[:, :, :], -NEG, NEG, ALU.mult, ALU.add))
                link(Ve.tensor_copy(lg[:, :, 0:4], t16[:, 2, :, 0:NG]))
                link(Ve.tensor_copy(row16[:, 5, :], lg[:, :, 0:4]))
                lev = le[:, :, :].rearrange("p m (g e) -> p (m g) e", g=NG)
                link(Ve.tensor_tensor(lev, lev, row16[:, 5, :].unsqueeze(2).to_broadcast([P, MT * NG, EG]), ALU.add))
                first_max(le[:, :, :], NE, mxs[:, 1, :], mask1[:, :, :], (t16[:, 0, :, :], t16[:, 1, :, :]))
                link(Ve.scalar_tensor_tensor(le[:, :, :], mask1[:, :, :], 3 * NEG, le[:, :, :], ALU.mult, ALU.add))
                first_max(le[:, :, :], NE, mxs[:, 2, :], mask2[:, :, :], (t16[:, 0, :, :], t16[:, 1, :, :]))
                Ve.tensor_tensor(exps[:, 0, :, 4:5], mxs[:, 2, :].unsqueeze(2), mxs[:, 1, :].unsqueeze(2), ALU.subtract).then_inc(s_lgv[l], 1)
                Ve.tensor_tensor(selb[:, :, :], mask1[:, :, :], mask2[:, :, :], ALU.add).then_inc(s_sel[l], 1)
                dve.wait_ge(s_rank[l], 1)
                rk = bank[1][:, 0:MT * NE].rearrange("p (m e) -> p m e", e=NE)
                ct = row16[:, 4, :]
                link(Ve.tensor_copy(ct, bank[1][:, 64:64 + NE]))
                link(Ve.tensor_scalar(row16[:, 0, :], ct, float(P + 1), None, ALU.is_ge))
                for k in range(2, S // P):
                    link(Ve.scalar_tensor_tensor(row16[:, 0, :], ct, float(k * P + 1), row16[:, 0, :], ALU.is_ge, ALU.add))
                link(Ve.tensor_tensor_scan(row16[:, 1, :], row16[:, 0, :], row16[:, 0, :], 0.0, ALU.add, ALU.bypass))
                link(Ve.tensor_tensor(row16[:, 2, :], row16[:, 1, :], row16[:, 0, :], ALU.subtract))
                link(Ve.tensor_scalar(row16[:, 2, :], row16[:, 2, :], float(P), float((NE - 1) * P), ALU.mult, ALU.add))
                link(Ve.tensor_tensor(row16[:, 2, :], row16[:, 2, :], small[:, NE:2 * NE], ALU.subtract))
                link(Ve.tensor_scalar(t16[:, 0, :, :], rk, float(P), None, ALU.is_ge))
                link(Ve.tensor_tensor(t16[:, 0, :, :], t16[:, 0, :, :], row16[:, 2, :].unsqueeze(1).to_broadcast([P, MT, NE]), ALU.mult))
                link(Ve.tensor_tensor(t16[:, 0, :, :], t16[:, 0, :, :], rk, ALU.add))
                link(Ve.tensor_tensor(t16[:, 0, :, :], t16[:, 0, :, :], small[:, NE:2 * NE].unsqueeze(1).to_broadcast([P, MT, NE]), ALU.add))
                Ve.tensor_tensor(t16[:, 1, :, :], t16[:, 0, :, :], mask1[:, :, :], ALU.mult)
                link(Ve.tensor_tensor(t16[:, 2, :, :], t16[:, 0, :, :], mask2[:, :, :], ALU.mult))
                Ve.tensor_reduce(posf[:, 0, :], t16[:, 1, :, :], AX, ALU.add)
                link(Ve.tensor_reduce(posf[:, 1, :], t16[:, 2, :, :], AX, ALU.add))
                link(Ve.tensor_copy(posi[:, :, :], posf[:, :, :]))
                link(Ve.tensor_tensor(ovf[:, :, :], row16[0:1, 1, :].unsqueeze(1).to_broadcast([1, OV, NE]),
                                      small[0:1, 32:32 + OV].unsqueeze(2).to_broadcast([1, OV, NE]), ALU.is_le))
                link(Ve.tensor_reduce(ove[:, 0:OV], ovf[:, :, :], AX, ALU.add))
                link(Ve.tensor_scalar(ove[:, 0:OV], ove[:, 0:OV], float(NE - 1), None, ALU.min))
                link(Ve.tensor_copy(ove[:, OV:OV + 1], row16[0:1, 1, NE - 1:NE]))
                Ve.tensor_copy(ovi[:, :], ove[:, :]).then_inc(s_pos[l], 1)
                dve.wait_ge(s_ex[l], 1)
                link(Ve.tensor_reduce(mxs[:, 3, :], exps[:, 1, :, 0:4], AX, ALU.add))
                ex2 = exps[:, 1, :, 4:5]
                col = lambda k: mxs[:, k, :].unsqueeze(2)
                link(Ve.tensor_scalar(col(4), ex2, 1.0, None, ALU.add))
                link(Ve.tensor_tensor(mxs[:, 5, :], mxs[:, 3, :], mxs[:, 4, :], ALU.mult))
                link(Ve.reciprocal(wts[:, 0, :], mxs[:, 5, :]))
                link(Ve.tensor_tensor(wts[:, 1, :].unsqueeze(2), wts[:, 0, :].unsqueeze(2), ex2, ALU.mult))
                dve.wait_ge(s_e[l], 1)
                for k in range(KP):
                    Ve.tensor_copy(pT[:, k, :], bank[4 + k][:, :]).then_inc(s_pse[l], 1)
                for g in range(2 * MT):
                    m, c = g // 2, g % 2
                    dve.wait_ge(s_m, groups_done(l, GE, g + 1))
                    Ve.tensor_copy(E[:, m, c * 512:(c + 1) * 512], bank[g % 4][:, :]).then_inc(s_mD, 1)
                dve.wait_ge(s_rr, 4 * l + SE + 1)
                dve.wait_ge(s_pg[l], 16)
                for m in range(MT):
                    ins = Ve.scalar_tensor_tensor(E[:, m, :], E[:, m, :], rr[:, l, SE, m:m + 1], pgain, ALU.mult, ALU.mult)
                link(ins)

                gains = lambda b: gffn[:, l, 4 * b:4 * b + 4].unsqueeze(2).to_broadcast([P, 4, P])
                tb = lambda b: bank[b][:, :].rearrange("p (k n) -> p k n", k=4)

                def rows_in(e):
                    for b in range(2):
                        dve.wait_ge(s_tx[l], 2 * e + b + 1)
                        Ve.tensor_tensor(xgT[:, 4 * b:4 * b + 4, :], tb(b), gains(b), ALU.mult).then_inc(s_xv[l], 1)

                def activations(e):
                    dve.wait_ge(s_sil[l], e + 1)
                    Ve.tensor_tensor(act, sil, bank[2][:, DE:2 * DE], ALU.mult).then_inc(s_act[l], 1)

                def result(e, p):
                    dve.wait_ge(s_dn[l], 2 * e + 1)
                    Ve.tensor_copy(ys[p][:, 0:512], bank[4][:, :]).then_inc(s_yD[l], 1)

                def stage(e, p, i, stored):
                    rows_in(e)
                    activations(e - 1)
                    if stored:
                        dve.wait_ge(s_st[l][p], 16 * (i - 1))
                    result(e - 2, p)

                rows_in(0)
                rows_in(1)
                activations(0)
                stage(2, 0, 1, False)
                stage(3, 1, 1, False)
                with dve.Fori(2, NE // 2) as i:
                    for p in range(2):
                        stage(2 * i + p, p, i, True)
                dve.wait_ge(s_st[l][0], 16 * (NE // 2 - 1))
                result(NE - 2, 0)
                activations(NE - 1)
                dve.wait_ge(s_st[l][1], 16 * (NE // 2 - 1))
                result(NE - 1, 1)
                dve.wait_ge(s_st[l][0], 16 * NE // 2)
                n = dve.value_load(ovi[0:1, OV:OV + 1], min_val=0, max_val=OV)
                with dve.If(n > 0):
                    with dve.Fori(0, n) as i:
                        rows_in(i + NE)
                        activations(i + NE)
                        result(i + NE, 0)
                dve.wait_ge(s_ga[l], 16 * 2 * MT)
                for m in range(MT):
                    link(Ve.scalar_tensor_tensor(h[:, m, :], y[:, m, :], wts[:, 0, m:m + 1], h[:, m, :], ALU.mult, ALU.add))
                    Ve.scalar_tensor_tensor(h[:, m, :], G2[:, m, :], wts[:, 1, m:m + 1], h[:, m, :], ALU.mult, ALU.add).then_inc(s_cmb[l], 1)
                turn(l, TP, KD, lambda j: Ve.tensor_copy(xT[:, j, :], bank[4 + j % 4][:, :]))
                for g in range(2 * MT):
                    m, c = g // 2, g % 2
                    dve.wait_ge(s_gt[l], g + 1)
                    part = slice(c * 512, (c + 1) * 512)
                    link(Ve.tensor_tensor(E[:, m, part], E[:, m, part], gate[:, g % 2, :], ALU.mult))
                    Ve.tensor_tensor(h[:, m, part], h[:, m, part], E[:, m, part], ALU.add).then_inc(s_h[l], 1)

        @block.tensor
        def _(pe):
            T = nc.tensor

            def turn(l, which, n, src, ready=None):
                for j in range(n):
                    if j >= 4:
                        pe.wait_ge(s_tD if j % 2 == 0 else s_tA, steps_moved(l, which, (j - 4) // 2 + 1))
                    for m in range(MT):
                        if j == 0 and ready:
                            ready(m)
                        mm = T.transpose(bank[4 + j % 4][:, m * P:(m + 1) * P], src(j, m), ident)
                    mm.then_inc(s_t, 1)

            def turned(l, which, n):
                pe.wait_ge(s_tD, steps_moved(l, which, n // 2))
                pe.wait_ge(s_tA, steps_moved(l, which, n // 2))

            def group(dst, m, w, nk, x=None):
                for k in range(nk):
                    mm = T.matmul(dst, (x if x is not None else xT)[:, k, m * P:(m + 1) * P], w(k), start=(k == 0), stop=(k == nk - 1))
                return mm

            pe.wait_ge(s_ident, 16)
            pe.wait_ge(s_cbf, 16)
            for l in range(DEPTH):
                turn(l, TM, KD, lambda j, m: h[:, m, j * P:(j + 1) * P],
                     (lambda m: pe.wait_ge(s_in[m], 16)) if l == 0 else (lambda m: pe.wait_ge(s_h[0], 2 * (m + 1))))
                turned(l, TM, KD)
                if l == 0:
                    pe.wait_ge(s_sg, 1)
                    for hd in range(NH):
                        mm = T.transpose(bank[6 + hd // 4][:, (hd % 4) * P:(hd % 4 + 1) * P], sgw[:, hd, :], ident)
                        if hd % 4 == 3:
                            mm.then_inc(s_sgT, 1)
                for g in range(MT * NIN[l]):
                    c, m = first[l] + g // MT, g % MT
                    if m == 0:
                        chunk_ready(pe, c)
                    if g >= 4:
                        n = (g - 4) // 2 + 1
                        pe.wait_ge(s_mD if g % 2 == 0 else s_mA, (movedD if g % 2 == 0 else movedA)(l, GI, n))
                    mm = group(bank[g % 4][:, :], m, lambda k: ring[:, c % 2, k, :], KD)
                    mm.then_inc(s_m, 1)
                if l == 1:
                    for m in range(MT):
                        mm = group(bank[4][:, m * NH:(m + 1) * NH], m, lambda k: wf[:, k, :], KD)
                    mm.then_inc(s_fa, 1)
                pe.wait_ge(s_mD, movedD(l, GI, MT * NIN[l] // 2))
                pe.wait_ge(s_mA, movedA(l, GI, MT * NIN[l] // 2))
                if l == 0:
                    pe.wait_ge(s_mixd, 2)
                if l == 1:
                    pe.wait_ge(s_fc, 1)
                    for i in range(MT):
                        for j in range(i + 1):
                            mm = T.matmul(bank[3][0:NH, i * P:(i + 1) * P], lf[:, 3, j, :], upto if i == j else ones,
                                          start=(j == 0), stop=(j == i))
                    mm.then_inc(s_fa, 1)
                    pe.wait_ge(s_qn[1], 2)
                turn(l, TQ, 8, lambda j, m: (Q if j < 4 else K)[:, m, (j % 4) * P:(j % 4 + 1) * P])
                turned(l, TQ, 8)
                if l == 1:
                    pe.wait_ge(s_fp, 1)
                    pe.wait_ge(s_mixin, 32)
                    pe.wait_ge(s_selin, 16)
                for v in range(4 * NH + 3):
                    if v < 4 * NH:
                        hd, i = v // 4, v % 4
                        n = (i + 1) * P
                        r = slice(HD * (hd % 2), HD * (hd % 2) + HD)
                        if v >= 2:
                            pe.wait_ge(s_pr[l], v - 1)
                        T.matmul(bank[v % 2][:, n - P:n], identb, strictb if l == 0 else causalb, start=True, stop=False,
                                 skip_group_check=True)
                        if l == 1:
                            T.matmul(bank[v % 2][:, 0:n], self_[0:96, hd, :], Fp[0:96, 0:n], start=False, stop=False,
                                     skip_group_check=True)
                        T.matmul(bank[v % 2][:, 0:n], qT[r, hd // 2, i * P:(i + 1) * P], kT[r, hd // 2, 0:n], start=False, stop=True,
                                 skip_group_check=True).then_inc(s_z[l], 1)
                    if 2 <= v < 4 * NH + 2:
                        u = v - 2
                        pe.wait_ge((s_w if l == 0 else s_pr)[l], u + 1)
                        for j in range(u % 4 + 1):
                            mm = T.transpose(bank[2 + u % 2][:, j * P:(j + 1) * P], attB[:, u % 2, j * P:(j + 1) * P], ident)
                        mm.then_inc(s_pt[l], 1)
                    if v >= 3:
                        u = v - 3
                        hd, i = u // 4, u % 4
                        pe.wait_ge(s_ptv[l], u + 1)
                        if i == 0 and hd >= 2:
                            pe.wait_ge(s_ov[l], hd - 1)
                        for j in range(i + 1):
                            mm = T.matmul(bank[6 + hd % 2][:, i * HD:(i + 1) * HD], attP[:, u % 2, j * P:(j + 1) * P],
                                          V[:, j, hd * HD:(hd + 1) * HD], start=(j == 0), stop=(j == i))
                        if i == 3:
                            mm.then_inc(s_o[l], 1)
                if l == 0:
                    pe.wait_ge(s_qn[0], 1)
                    for hd in range(NH):
                        mm = T.matmul(bank[hd // 2][:, 256 * (hd % 2):256 * (hd % 2) + 256], sguT[:, hd, :],
                                      VA[:, :, hd * HD:(hd + 1) * HD], start=True, stop=True)
                        if hd % 2:
                            mm.then_inc(s_pm, 1)
                    pe.wait_ge(s_y[0], NH)
                    pe.wait_ge(s_ov[0], NH)
                    turn(0, TY, 8, lambda j, m: y[:, m, j * P:(j + 1) * P])
                    turned(0, TY, 8)
                else:
                    pe.wait_ge(s_ov[1], NH)
                    turn(1, TY, 4, lambda j, m: y[:, m, j * P:(j + 1) * P])
                    for g in range(4):
                        for j in range(MT):
                            width = BW if j < MT - 1 else P
                            mm = T.matmul(bank[g % 2][:, j * P:j * P + width], y[:, j, W + g * P:W + (g + 1) * P],
                                          bands[:, 1 if j == 0 else 0, g, 0:width], start=(j == 0), stop=(j == MT - 1),
                                          skip_group_check=True)
                        mm.then_inc(s_pl, 1)
                        pe.wait_ge(s_plv, g + 1)
                        T.matmul(bank[2 + g % 2][:, :], poolw[:, g, :], pT2[:, g % 2, :], start=True, stop=True).then_inc(s_pm, 1)
                    turned(1, TY, 4)
                    pe.wait_ge(s_y[1], 4)
                c0 = ffn[l] - 2
                chunk_ready(pe, c0)
                chunk_ready(pe, c0 + 1)
                for g in range(2 * MT):
                    if g >= 4:
                        pe.wait_ge(s_mD, movedD(l, GO, g - 3))
                    c = c0 + g % 2
                    group(bank[g % 4][:, :], g // 2, lambda k: ring[:, c % 2, k, :], KD).then_inc(s_m, 1)
                pe.wait_ge(s_xn[l], MT)
                turn(l, TF, KD, lambda j, m: y[:, m, j * P:(j + 1) * P])
                turned(l, TF, KD)
                for m in range(MT):
                    mm = group(bank[0][:, m * 20:(m + 1) * 20], m, lambda k: wr[:, l, k, :], KD)
                mm.then_inc(s_lg[l], 1)
                pe.wait_ge(s_pin[l], 16)
                for k in range(KP):
                    for m in range(MT):
                        mm = T.transpose(bank[4 + k][:, m * P:(m + 1) * P], pin[:, m, k * P:(k + 1) * P], ident)
                mm.then_inc(s_e[l], 1)
                pe.wait_ge(s_sel[l], 1)
                for m in range(MT):
                    for j in range(m + 1):
                        T.matmul(bank[1][:, m * NE:(m + 1) * NE], beforeb if j == m else onesb, selb[:, j, :],
                                 start=(j == 0), stop=(j == m))
                for j in range(MT):
                    mm = T.matmul(bank[1][:, 64:64 + NE], onesb, selb[:, j, :], start=(j == 0), stop=(j == MT - 1))
                mm.then_inc(s_rank[l], 1)
                pe.wait_ge(s_pse[l], KP)
                pe.wait_ge(s_pos[l], 1)
                c = ffn[l]
                chunk_ready(pe, c)
                wp = ring[:, c % 2, 0:2 * KP, :].rearrange("p (k n) c -> p k (n c)", k=KP)
                for g in range(2 * MT):
                    if g >= 4:
                        pe.wait_ge(s_mD, movedD(l, GE, g - 3))
                    group(bank[g % 4][:, :], g // 2, lambda k: wp[:, k, (g % 2) * 512:(g % 2 + 1) * 512], KP, pT).then_inc(s_m, 1)
                pe.wait_ge(s_mD, movedD(l, GE, 2 * MT))

                def rows_turned(e, p, i):
                    pe.wait_ge(s_xl[l][p], 16 * i + 16)
                    turn_rows(e, p)

                def turn_rows(e, p):
                    for b in range(2):
                        for k in range(4):
                            mm = T.transpose(bank[b][:, k * P:(k + 1) * P], xs[p][:, (4 * b + k) * P:(4 * b + k + 1) * P], ident)
                        mm.then_inc(s_tx[l], 1)

                def gate_up(e, p, i):
                    pe.wait_ge(s_gu[l][p], 32 * i + 32)
                    multiply_gate_up(e, p)

                def multiply_gate_up(e, p):
                    pe.wait_ge(s_xv[l], 2 * e + 2)
                    for k in range(KD):
                        mm = T.matmul(bank[2][:, :], xgT[:, k, :], gu[:, p, k, :], start=(k == 0), stop=(k == KD - 1))
                    mm.then_inc(s_g[l], 1)

                def act_turned(e):
                    pe.wait_ge(s_act[l], e + 1)
                    for f in range(DE // P):
                        mm = T.transpose(bank[3][:, f * P:(f + 1) * P], act[:, f * P:(f + 1) * P], ident)
                    mm.then_inc(s_at[l], 1)

                def down(e, p, i):
                    pe.wait_ge(s_wd[l][p], 16 * i + 16)
                    multiply_down(e, p, first=isinstance(e, int) and e == 0)

                def multiply_down(e, p, first=False):
                    pe.wait_ge(s_atv[l], e + 1)
                    if not first:
                        pe.wait_ge(s_yD[l], e)
                        pe.wait_ge(s_yA[l], e)
                    for c in range(2):
                        for f in range(DE // P):
                            mm = T.matmul(bank[4 + c][:, :], actT[:, f * P:(f + 1) * P], wd[:, p, f, c * 512:(c + 1) * 512],
                                          start=(f == 0), stop=(f == DE // P - 1))
                        mm.then_inc(s_dn[l], 1)

                rows_turned(0, 0, 0)
                gate_up(0, 0, 0)
                rows_turned(1, 1, 0)
                act_turned(0)
                gate_up(1, 1, 0)

                def stage(e, p, i):
                    rows_turned(e, p, i)
                    down(e - 2, p, i - 1)
                    act_turned(e - 1)
                    gate_up(e, p, i)

                stage(2, 0, 1)
                stage(3, 1, 1)
                with pe.Fori(2, NE // 2) as i:
                    for p in range(2):
                        stage(2 * i + p, p, i)
                down(NE - 2, 0, NE // 2 - 1)
                act_turned(NE - 1)
                down(NE - 1, 1, NE // 2 - 1)
                pe.wait_ge(s_yD[l], NE)
                pe.wait_ge(s_yA[l], NE)
                n = pe.value_load(ovi[0:1, OV:OV + 1], min_val=0, max_val=OV)
                with pe.If(n > 0):
                    with pe.Fori(0, n) as i:
                        pe.wait_ge(o_ld[l], 64 * i + 64)
                        turn_rows(i + NE, 0)
                        multiply_gate_up(i + NE, 0)
                        act_turned(i + NE)
                        multiply_down(i + NE, 0)
                turn(l, TP, KD, lambda j, m: h[:, m, j * P:(j + 1) * P], lambda m: pe.wait_ge(s_cmb[l], m + 1))
                turned(l, TP, KD)
                c0 = ffn[l] + 1
                chunk_ready(pe, c0)
                chunk_ready(pe, c0 + 1)
                for g in range(2 * MT):
                    if g >= 4:
                        pe.wait_ge(s_gt[l], g - 3)
                    c = c0 + g % 2
                    group(bank[g % 4][:, :], g // 2, lambda k: ring[:, c % 2, k, :], KD).then_inc(s_m, 1)
                pe.wait_ge(s_gt[l], 2 * MT)


_OUT = ((1, 512, 1024), "float32")


def kernel(**inputs):
    import numpy as _np
    import concourse.bacc as _bacc
    from concourse import mybir as _mybir
    from concourse.bass_utils import run_bass_kernel_spmd as _run

    nc = _bacc.Bacc("TRN2", target_bir_lowering=False, num_devices=1)
    arrays, aps = {}, {}
    for name, value in {**inputs, **constants()}.items():
        v = _np.ascontiguousarray(value)
        arrays[f"in_{name}_dram"] = v
        aps[name] = nc.dram_tensor(f"in_{name}_dram", v.shape, _mybir.dt.from_np(v.dtype), kind="ExternalInput").ap()
    out = nc.dram_tensor("out_dram", _OUT[0], _mybir.dt.from_np(_np.dtype(_OUT[1])), kind="ExternalOutput").ap()
    trunk(nc, aps, out)
    r = _run(nc, [arrays], core_ids=[0])
    return r.results[0]["out_dram"]
```

```python
from contextlib import ExitStack

import numpy as np
import concourse.bass as bass
from concourse import mybir

F32 = mybir.dt.float32
F32R = mybir.dt.float32r
BF16 = mybir.dt.bfloat16
I32 = mybir.dt.int32
ALU = mybir.AluOpType
ACT = mybir.ActivationFunctionType
AX = mybir.AxisListType.X

P = 128
D = 1024
S = 512
MT = S // P
KD = D // P
HD = 64
NH = 8
W = NH * HD
DEPTH = 2
PLE = 256
KP = PLE // P
NE = 16
NG = 4
EG = NE // NG
DE = 256
OV = 7
OVT = OV + OV % 2
TILES = NE + OVT
EPS = 1e-6
SCALE = HD ** -0.5
NEG = -1e30
WINDOWS = (2, 4, 8, 16)
BW = P + 16
SMALL = 48


def constants():
    i = np.arange(P)
    ident = np.eye(P, dtype=np.float32)
    strict = np.where(i[None, :] >= i[:, None], NEG, 0.0)
    causal = np.where(i[None, :] > i[:, None], NEG, 0.0)
    before = (i[:, None] < i[None, :]).astype(np.float32)
    cb = np.stack([ident, strict, causal, before, np.ones((P, P))], 1).astype(np.float32)
    upto = (i[:, None] <= i[None, :]).astype(np.float32)
    tril = (i[None, :] <= i[:, None]).astype(np.float32)
    cf = np.stack([ident, upto, np.ones((P, P), np.float32), tril], 1)
    bands = np.zeros((P, 2, len(WINDOWS), BW), np.float32)
    t = np.arange(BW)
    for first in (0, 1):
        for g, win in enumerate(WINDOWS):
            inside = (t[None, :] >= i[:, None]) & (t[None, :] - i[:, None] < win)
            count = np.minimum(t + 1, win) if first else np.full(BW, win)
            bands[:, first, g] = inside / count[None, :].astype(np.float32) - (t[None, :] == i[:, None])
    sel = np.zeros((P, NH, P), np.float32)
    for part in range(3):
        for h in range(NH):
            sel[32 * part + h, h, :] = -1.0 / SCALE
    small = np.zeros((P, SMALL), np.float32)
    small[:, 0:NE] = NE - np.arange(NE)
    small[:, NE:2 * NE] = P * np.arange(NE)
    small[:, 32:32 + OVT] = np.arange(OVT)
    small[:, 40:44] = 1 + 2 * np.arange(4)
    return {"c_bf": cb, "c_f": cf, "c_bands": bands, "c_sel": sel, "c_small": small}


def trunk(nc, a, out):
    ctx = ExitStack()
    with ctx:
        def sb(name, shape, dt=F32):
            return ctx.enter_context(nc.sbuf_tensor(name, shape, dt))

        def sem(name):
            return ctx.enter_context(nc.semaphore(name))

        def sems(name, n=DEPTH):
            return [sem(f"{name}{i}") for i in range(n)]

        bank = [ctx.enter_context(nc.psum_tensor(f"bank{i}", [P, 512], F32)) for i in range(8)]

        h = sb("h", [P, MT, D])
        def at_(name, offset, shape, dt=F32):
            return nc.alloc_sbuf_tensor_at(name, shape, dt, offset=arena + offset)

        arena = nc.sbuf_base
        sb("arena", [P, 16 * 1024])
        KB = 1024
        xT = at_("xT", 0, [P, KD, S])
        xh = at_("xh", 0, [P, KD, S], F32R)
        gu = at_("gu", 16 * KB, [P, 2, KD, 2 * DE])
        wd = at_("wd", 48 * KB, [P, 2, DE // P, D])
        xl = at_("xl", 16 * KB, [P, KD, S], F32R)
        wh = at_("wh", 32 * KB, [P, 4, 2, 512], F32R)
        wl = at_("wl", 48 * KB, [P, 4, 2, 512], F32R)
        y = sb("y", [P, MT, D])
        R1 = sb("R1", [P, 4 * S * MT // 2])
        R2 = sb("R2", [P, 4 * S * MT // 2])
        qkT = sb("qkT", [P, 8 * S])
        ring = sb("ring", [P, 2, KD, 512])
        attE = sb("attE", [P, 2, 512])
        attB = sb("attB", [P, 2, 512])
        attS = sb("attS", [P, 2, 513])
        attP = sb("attP", [P, 2, 512])
        cbf = sb("cbf", [P, 5, P], BF16)
        cf = sb("cf", [P, 4, P])
        small = sb("small", [P, SMALL])
        mixw = sb("mixw", [P, 2 * len(WINDOWS) * BW])
        mixg = sb("mixg", [P, 512])
        grow = sb("grow", [46, P])
        gcol = sb("gcol", [P, 46])
        wf = sb("wf", [P, KD, NH])
        wfh = sb("wfh", [P, KD, NH], F32R)
        wfl = sb("wfl", [P, KD, NH], F32R)
        fb = sb("fb", [P, NH])
        wr = sb("wr", [P, DEPTH, KD, 20])
        rb = sb("rb", [P, DEPTH, 20])
        ss = sb("ss", [P, DEPTH, 4, MT])
        rr = sb("rr", [P, DEPTH, 4, MT])
        hss = sb("hss", [P, 2, MT * NH])
        hrr = sb("hrr", [P, 2, MT * NH])
        pw = sb("pw", [P, 2 * MT * NH])
        mxs = sb("mxs", [P, 8, MT])
        wts = sb("wts", [P, 2, MT])
        selb = sb("selb", [P, MT, NE], BF16)
        posf = sb("posf", [P, 2, MT])
        posi = sb("posi", [P, 2, MT], I32)
        ove = sb("ove", [1, OVT + 1])
        ovi = sb("ovi", [1, OVT + 1], I32)
        rs = sb("rs", [P, 4 * NH])
        ri = sb("ri", [P, 4 * NH])
        mx = sb("mx", [P, 4 * NH])
        nb = sb("nb", [P, 4 * NH])
        lf = sb("lf", [P, 4, MT, NH])

        gmix = lambda l, k: gcol[:, l * KD + k:l * KD + k + 1]
        gffn = lambda l, k, n=1: gcol[:, (2 + l) * KD + k:(2 + l) * KD + k + n]
        sgb = lambda hd: gcol[:, 32 + hd:33 + hd]
        pscale = lambda g: gcol[:, 40 + g:41 + g]
        qkg = lambda b: gcol[:, 44 + b:45 + b]
        f32 = lambda x: x.bitcast(F32)
        ident, upto, ones, tril = (cf[:, i, :] for i in range(4))
        identb, strictb, causalb, beforeb, onesb = (cbf[:, i, :] for i in range(5))
        rows = lambda x: x.rearrange("p (m n) -> p m n", m=MT)
        VA, Q = rows(R1[:, 0:MT * W]), rows(R1[:, MT * W:])
        K, V = rows(R2[:, 0:MT * W]), rows(R2[:, MT * W:])
        U = y[:, :, 0:W]
        E = rows(R1[:, :])
        zeros = y[:, MT - 1, :]
        G2 = rows(R2[:, :])
        xs = [R2[:, p * D:(p + 1) * D] for p in range(2)]
        ys = [R2[:, (2 + p) * D:(3 + p) * D] for p in range(2)]
        qT = qkT[:, 0:4 * S].rearrange("p (c n) -> p c n", c=4)
        kT = qkT[:, 4 * S:].rearrange("p (c n) -> p c n", c=4)
        xgT = qkT[:, 0:KD * P].rearrange("p (k n) -> p k n", k=KD)
        sil, act, actT = (qkT[:, D + i * DE:D + (i + 1) * DE] for i in range(3))
        pin = qkT[:, 2048:3072].rearrange("p (m n) -> p m n", m=MT)
        pT = qkT[:, 3072:4096].rearrange("p (k n) -> p k n", k=KP)
        pgain = attB[:, :, :].rearrange("p a n -> p (a n)")
        routing = attP[:, :, :].rearrange("p a n -> p (a n)")
        at = [0]

        def part(*shape):
            n = int(np.prod(shape))
            at[0] += n
            x = routing[:, at[0] - n:at[0]]
            names = " ".join(f"d{i}" for i in range(len(shape)))
            return x.rearrange(f"p ({names}) -> p {names}", **{f"d{i}": k for i, k in enumerate(shape)})

        t16, le, lg, exps = part(3, MT, NE), part(MT, NE), part(MT, 20), part(2, MT, 5)
        mask1, mask2, gmask, row16 = part(MT, NE), part(MT, NE), part(MT, NG), part(6, NE)
        ovf = part(OVT, NE)[0:1]
        junk = attS[:, :, :].rearrange("p a n -> p (a n)")[:, 0:D]
        gate = attE
        sgw = attP[:, :, :].rearrange("p a (h s) -> p (a h) s", s=P)
        sguT = mixw[:, 0:NH * P].rearrange("p (h t) -> p h t", h=NH)
        bands = mixw[:, :].rearrange("p (f g t) -> p f g t", f=2, g=4)
        poolw = mixg[:, :].rearrange("p (g d) -> p g d", g=4)
        self_ = attE[:, 0, :].bitcast(BF16).rearrange("p (h n) -> p h n", h=NH)
        Fp = attE[:, 1, :].bitcast(BF16)[:, 0:S]
        Frow = attS[0:NH, 0, 0:S]
        Frest = attS[0:NH, 1, 0:S]
        Flog = attP[0:NH, 0, :]
        pT2 = attP

        xg = nc.dram_tensor("xg", [TILES * P, D], F32, kind="Internal").ap()
        yg = nc.dram_tensor("yg", [TILES * P, D], F32, kind="Internal").ap()

        s_cbf, s_selin = sem("s_cbf"), sem("s_selin")
        s_grow, s_gT, s_gcol, s_sgin, s_wf = sem("s_grow"), sem("s_gT"), sem("s_gcol"), sem("s_sgin"), sem("s_wf")
        s_hi, s_lo, s_un = sem("s_hi"), sem("s_lo"), sem("s_un")
        s_const, s_ident, s_zero, s_xgz = sem("s_const"), sem("s_ident"), sem("s_zero"), sem("s_xgz")
        s_in = sems("s_in", MT)
        s_ring = sems("s_ring", 2)
        s_mixin, s_pin, s_pg = sem("s_mixin"), sems("s_pin"), sems("s_pg")
        s_ss, s_rr = sem("s_ss"), sem("s_rr")
        s_t, s_tD, s_tA = sem("s_t"), sem("s_tD"), sem("s_tA")
        s_m, s_mD, s_mA = sem("s_m"), sem("s_mD"), sem("s_mA")
        s_z, s_pr, s_w, s_pt, s_ptv, s_o, s_ov = (sems(n) for n in ("s_z", "s_pr", "s_w", "s_pt", "s_ptv", "s_o", "s_ov"))
        s_qn, s_hs, s_hr = sems("s_qn"), sems("s_hs"), sems("s_hr")
        s_y, s_mixd, s_sg, s_sgT = sems("s_y"), sem("s_mixd"), sem("s_sg"), sem("s_sgT")
        s_f, s_fa, s_fl, s_fc, s_fp, s_fx = (sem(n) for n in ("s_f", "s_fa", "s_fl", "s_fc", "s_fp", "s_fx"))
        s_oh, s_wn = sems("s_oh"), sem("s_wn")
        s_pl, s_plv, s_pm, s_ph = sem("s_pl"), sem("s_plv"), sem("s_pm"), sem("s_ph")
        s_xn, s_lg, s_lgv, s_ex, s_sel, s_rank, s_pos = (sems(n) for n in ("s_xn", "s_lg", "s_lgv", "s_ex", "s_sel", "s_rank", "s_pos"))
        s_sc, s_xl, s_gu, s_wd = sems("s_sc"), [sems(f"s_xl{l}_", 2) for l in range(2)], [sems(f"s_gu{l}_", 2) for l in range(2)], [sems(f"s_wd{l}_", 2) for l in range(2)]
        s_tx, s_xv, s_g, s_sil, s_act, s_at, s_atv = (sems(n) for n in ("s_tx", "s_xv", "s_g", "s_sil", "s_act", "s_at", "s_atv"))
        s_dn, s_yD, s_yA, s_st = sems("s_dn"), sems("s_yD"), sems("s_yA"), [sems(f"s_st{l}_", 2) for l in range(2)]
        s_ovi, s_end = sems("s_ovi"), sems("s_end")
        s_gam = [sems(f"s_ga{l}_", MT) for l in range(DEPTH)]
        s_cmb, s_e, s_pse, s_gt, s_h = sems("s_cmb"), sems("s_e"), sems("s_pse"), sems("s_gt"), sems("s_h")
        s_dve, s_act_, s_pool = sem("s_dve"), sem("s_actchain"), sem("s_poolchain")
        s_out = sem("s_out")

        def cols(w, c, k=KD):
            return w[:, c * 512:(c + 1) * 512].rearrange("(k p) n -> p k n", p=P)

        wi, wo = a["even_w_in"][0], a["even_w_out"][0]
        oi, oo = a["odd_w_in"][0], a["odd_w_out"][0]
        XD0 = 3 * W + NH
        chunks = [cols(wi, c) for c in (2, 3, 4, 1, 0)] + [cols(wo, 0), cols(wo, 1)]
        first = [0]
        ffn = []
        for l in range(DEPTH):
            ffn.append(len(chunks))
            chunks += [None, cols(a["ple_w_gate"][l], 0), cols(a["ple_w_gate"][l], 1)]
            if l == 0:
                first.append(len(chunks))
                chunks += [cols(oi, 0), cols(oi, 1), cols(oi, 2), oi[:, XD0:XD0 + W].rearrange("(k p) n -> p k n", p=P)]
                chunks += [cols(oo, 0), cols(oo, 1)]
        NIN = [5, 4]

        def chunk_ready(pe, c):
            pe.wait_ge(s_ring[c % 2], 16 * (c // 2 + 1))

        TM, TF, TY, TP, TQ = range(5)
        GI, GO, GE, GG = range(4)
        SM, SF, SE, SP_ = range(4)

        before_t, before_tm, before_m, before_mD, before_mA = {}, {}, {}, {}, {}
        nt = ntm = nm = nD = nA = 0
        for l in range(DEPTH):
            for which, steps, both in ((TM, KD, 1), (TQ, 8, 0), (TY, [4, 0][l], 1), (TF, KD, 0), (TP, KD, 1)):
                before_t[l, which], before_tm[l, which] = nt, ntm
                nt += steps
                ntm += steps if both else steps // 2
            for which, groups, byD, byA in ((GI, MT * NIN[l], [6, 8][l], [14, 8][l]),
                                            (GO, 2 * MT, 2 * MT, 0), (GE, 2 * MT, 0, 2 * MT), (GG, 2 * MT, 0, 0)):
                before_m[l, which], before_mD[l, which], before_mA[l, which] = nm, nD, nA
                nm, nD, nA = nm + groups, nD + byD, nA + byA

        def turn_bank(l, which, j):
            return bank[(j + 4) % 8 if which == TY or (l, which) == (0, TQ) else j][:, :]

        def steps_turned(l, which, n):
            return before_t[l, which] + n

        def steps_moved(l, which, n):
            return before_tm[l, which] + n

        def groups_done(l, which, n):
            return before_m[l, which] + n

        def movedD(l, which, n):
            return before_mD[l, which] + n

        def movedA(l, which, n):
            return before_mA[l, which] + n

        def by_vector(l, c, m):
            return m % 2 == 0 and not (l == 0 and c >= 3)

        def in_moved(l, c):
            n = sum(by_vector(l, k, m) for k in range(c) for m in range(MT))
            return movedD(l, GI, n), movedA(l, GI, MT * c - n)

        last_group = []
        for l in range(DEPTH):
            last_group += [groups_done(l, GI, MT * (j + 1)) for j in range(NIN[l])]
            last_group += [groups_done(l, which, n * MT) for which, n in ((GO, 1), (GO, 2), (GE, 2), (GG, 1), (GG, 2))]

        split = [c for c in range(len(chunks)) if chunks[c] is not None]

        def unit(c, j):
            return 4 * split.index(c) + j

        def raw(c, j):
            return ring[:, c % 2, 2 * j:2 * j + 2, :]

        block = ctx.enter_context(nc.Block())

        @block.sync
        def _(sp):
            def chunk(c):
                if c >= 2 and c - 2 in split:
                    sp.wait_ge(s_lo, unit(c - 2, 3) + 1)
                elif c >= 2:
                    sp.wait_ge(s_m, last_group[c - 2])
                if chunks[c] is None:
                    l = ffn.index(c)
                    sp.dma_start(ring[:, c % 2, 0:2 * KP, :].rearrange("p (k n) c -> p k (n c)", k=KP),
                                 a["ple_w_proj"][l].rearrange("(k p) n -> p k n", p=P)).then_inc(s_ring[c % 2], 16)
                else:
                    sp.dma_start(ring[:, c % 2, :, :], chunks[c]).then_inc(s_ring[c % 2], 16)

            def load_gu(l, e, p):
                sp.dma_start(gu[:, p, :, 0:DE], a["expert_w_gate"][l, e].rearrange("(k p) f -> p k f", p=P)).then_inc(s_gu[l][p], 16)
                sp.dma_start(gu[:, p, :, DE:], a["expert_w_up"][l, e].rearrange("(k p) f -> p k f", p=P)).then_inc(s_gu[l][p], 16)

            def load_wd(l, e, p):
                sp.dma_start(wd[:, p, :, :], a["expert_w_down"][l, e].rearrange("(k p) n -> p k n", p=P)).then_inc(s_wd[l][p], 16)

            def zero(t0, t1):
                sp.dma_start(xg[t0 * P:t1 * P, :].rearrange("(t p) d -> p t d", p=P),
                             zeros.unsqueeze(1).to_broadcast([P, t1 - t0, D])).then_inc(s_xgz, 16)

            for m in range(MT):
                sp.dma_start(h[:, m, :], a["x"][0, m * P:(m + 1) * P, :]).then_inc(s_in[m], 16)
            sp.wait_ge(s_in[0], 16)
            chunk(0)
            sp.wait_ge(s_sgin, 16)
            chunk(1)
            sp.wait_ge(s_zero, 1)
            for l in range(DEPTH):
                if l == 0:
                    for c in range(2, 4):
                        zero(6 * (c - 2), 6 * (c - 1))
                        chunk(c)
                    zero(12, 17)
                    sp.dma_start(yg[NE * P:, :].rearrange("(t p) d -> p t d", p=P),
                                 zeros.unsqueeze(1).to_broadcast([P, OVT, D])).then_inc(s_xgz, 16)
                    zero(17, TILES)
                for c in range(4 if l == 0 else first[l] + 2, ffn[l]):
                    chunk(c)
                if l == 0:
                    sp.wait_ge(s_t, steps_turned(0, TY, 4))
                sp.wait_ge(s_ov[l], NH // 2)
                sp.dma_start(pgain, a["ple_norm"][l].partition_broadcast(P)).then_inc(s_pg[l], 16)
                sp.dma_start(pin, a["p"][l, 0].rearrange("(m p) n -> p m n", p=P)).then_inc(s_pin[l], 16)
                chunk(ffn[l])
                sp.wait_ge(s_m, last_group[ffn[l] - 1])
                for e in range(2):
                    load_gu(l, e, e)
                    load_wd(l, e, e)
                chunk(ffn[l] + 1)
                sp.wait_ge(s_sc[l], 16 * 2 * MT)
                for e in range(2):
                    sp.dma_start(xs[e], xg[e * P:(e + 1) * P, :]).then_inc(s_xl[l][e], 16)
                chunk(ffn[l] + 2)

                def load(t, p, expert):
                    sp.wait_ge(s_tx[l], 2 * (t - 1))
                    sp.dma_start(xs[p], xg.rearrange("(t p) d -> t p d", p=P)[bass.ds(t, 1), :, :].rearrange("t p d -> p (t d)"))\
                        .then_inc(s_xl[l][p], 16)
                    sp.wait_ge(s_g[l], t - 1)
                    sp.dma_start(gu[:, p, :, 0:DE], a["expert_w_gate"][l, bass.ds(expert, 1)].rearrange("e (k p) f -> p (e k) f", p=P))\
                        .then_inc(s_gu[l][p], 16)
                    sp.dma_start(gu[:, p, :, DE:], a["expert_w_up"][l, bass.ds(expert, 1)].rearrange("e (k p) f -> p (e k) f", p=P))\
                        .then_inc(s_gu[l][p], 16)

                with sp.Fori(1, NE // 2) as i:
                    for p in range(2):
                        load(2 * i + p, p, 2 * i + p)
                sp.wait_ge(s_ovi[l], 1)
                n = sp.value_load(ovi[0:1, OVT:OVT + 1], min_val=0, max_val=OVT // 2)
                with sp.If(n > 0):
                    with sp.Fori(0, n) as i:
                        for p in range(2):
                            expert = sp.value_load(ovi[0:1, bass.ds(2 * i + p, 1)], min_val=0, max_val=NE - 1)
                            load(2 * i + (p + NE), p, expert)
                if l == 0:
                    for c in range(first[1], first[1] + 2):
                        chunk(c)
                    sp.wait_ge(s_h[0], 2 * MT)
                    sp.dma_start(mixw[:, :], a["c_bands"].rearrange("p f g t -> p (f g t)")).then_inc(s_mixin, 16)
                    sp.dma_start(poolw, a["pool_w"][0].rearrange("g c d -> c g d")).then_inc(s_mixin, 16)

        @block.scalar
        def _(sc):
            A = nc.scalar
            chain = [0]

            def link(ins):
                chain[0] += 1
                ins.then_inc(s_act_, 1)
                sc.wait_ge(s_act_, chain[0])

            sc.dma_start(cf[:, :, :], a["c_f"]).then_inc(s_ident, 16)
            for rows_, src in ((slice(0, 16), a["norm_mix"].rearrange("l (k p) -> (l k) p", p=P)),
                               (slice(16, 32), a["norm_ffn"].rearrange("l (k p) -> (l k) p", p=P)),
                               (slice(32, 40), a["sgu_b"][0]),
                               (slice(40, 44), a["pool_scale"][0].rearrange("(g p) -> g p", p=P))):
                sc.dma_start(grow[rows_, :], src).then_inc(s_grow, 16)
            for b, name in enumerate(("q_norm", "k_norm")):
                sc.dma_start(grow[44 + b:45 + b, :].rearrange("p (a d) -> p a d", a=2),
                             a[name].unsqueeze(1).to_broadcast([1, 2, HD])).then_inc(s_grow, 16)
            sc.dma_start(sgw, a["sgu_w"][0].rearrange("h t s -> t h s")).then_inc(s_sgin, 16)
            with nc.allow_non_contiguous_dma(reason="narrow weights"):
                for dst, src in ((small[:, :], a["c_small"]),
                                 (wf[:, :, :], oi[:, 3 * W:3 * W + NH].rearrange("(k p) n -> p k n", p=P)),
                                 (fb[:, :], a["forget_bias"][0].partition_broadcast(P)),
                                 (wr[:, 0, :, 0:4], a["router_group_w"][0].rearrange("(k p) n -> p k n", p=P)),
                                 (wr[:, 1, :, 0:4], a["router_group_w"][1].rearrange("(k p) n -> p k n", p=P)),
                                 (wr[:, 0, :, 4:20], a["router_expert_w"][0].rearrange("(k p) n -> p k n", p=P)),
                                 (wr[:, 1, :, 4:20], a["router_expert_w"][1].rearrange("(k p) n -> p k n", p=P)),
                                 (rb[:, 0, 0:4], a["router_group_b"][0].partition_broadcast(P)),
                                 (rb[:, 1, 0:4], a["router_group_b"][1].partition_broadcast(P)),
                                 (rb[:, 0, 4:20], a["router_expert_b"][0].partition_broadcast(P)),
                                 (rb[:, 1, 4:20], a["router_expert_b"][1].partition_broadcast(P)),
                                 (mixg[:, :], a["sgu_norm"][0].rearrange("h d -> (h d)").partition_broadcast(P))):
                    sc.dma_start(dst, src).then_inc(s_const, 16)

            def high(c, j):
                if j == 0:
                    sc.wait_ge(s_ring[c % 2], 16 * (c // 2 + 1))
                q = split.index(c)
                if q and j < 3:
                    sc.wait_ge(s_un, 3 * (q - 1) + j + 1)
                elif q:
                    sc.wait_ge(s_m, last_group[split[q - 1]])
                A.copy(wh[:, j, :, :], raw(c, j)).then_inc(s_hi, 1)

            def highs(c):
                for j in range(4):
                    high(c, j)

            def turn_high(l, which, n, put):
                for j in range(n):
                    sc.wait_ge(s_t, steps_turned(l, which, j + 1))
                    put(j).then_inc(s_tA, 1)

            def stat(l, which, src, dst):
                done = MT * (4 * l + which) + dst
                if done:
                    sc.wait_ge(s_ss, done)
                A.activation(junk, src, ACT.Square, accum_out=ss[:, l, which, dst:dst + 1]).then_inc(s_ss, 1)

            def turn(l, which, n, put):
                for j in range(1, n, 2):
                    sc.wait_ge(s_t, steps_turned(l, which, j + 1))
                    put(j).then_inc(s_tA, 1)

            for l in range(DEPTH):
                if l == 0:
                    sc.wait_ge(s_gcol, 1)
                turn_high(l, TM, KD, lambda j: A.mul(xh[:, j, :], turn_bank(l, TM, j), gmix(l, j)))
                if l == 0:
                    highs(0)
                for m in range(MT):
                    if l == 0:
                        sc.wait_ge(s_in[m], 16)
                    else:
                        sc.wait_ge(s_h[0], MT + m + 1)
                    stat(l, SM, h[:, m, :], m)
                if l == 0:
                    sc.wait_ge(s_const, 16 * 12)
                    A.copy(wfh[:, :, :], wf[:, :, :]).then_inc(s_wf, 1)
                dst = [[Q, K, V, VA, U], [Q, K, V, y[:, :, W:]]][l]
                for c in range(NIN[l] + 1):
                    if c and c < NIN[l]:
                        highs(first[l] + c)
                    elif c:
                        highs(ffn[l] - 2)
                    if c == 0:
                        sc.wait_ge(s_rr, 4 * l + SM + 1)
                        continue
                    k = c - 1
                    if l == 0 and k == 4:
                        sc.wait_ge(s_xgz, 16 * 5)
                    for m in range(MT):
                        if not by_vector(l, k, m):
                            sc.wait_ge(s_m, groups_done(l, GI, MT * k + m + 1))
                            x = dst[k][:, m, :]
                            b = bank[4 * (k % 2) + m][:, :]
                            r = rr[:, l, SM, m:m + 1]
                            if l == 0 and k >= 3:
                                A.activation(x, b, ACT.Gelu_apprx_tanh, scale=r).then_inc(s_mA, 1)
                            else:
                                A.mul(x, b, r).then_inc(s_mA, 1)
                    if l == 1 and k == 0:
                        sc.wait_ge(s_f, 1)
                        link(A.activation(lf[:, 1, :, :], lf[:, 0, :, :], ACT.Abs))
                        link(A.activation(lf[:, 1, :, :], lf[:, 1, :, :], ACT.Exp, scale=-1.0))
                        A.activation(lf[:, 2, :, :], lf[:, 1, :, :], ACT.Ln, bias=1.0).then_inc(s_fl, 1)
                if l == 1:
                    turn(1, TQ, 8, lambda j: A.mul(qT[:, j, :] if j < 4 else kT[:, j - 4, :], turn_bank(1, TQ, j), qkg(j // 4)))
                else:
                    turn(0, TQ, 8, lambda j: A.copy(qT[:, j, :] if j < 4 else kT[:, j - 4, :], turn_bank(0, TQ, j)))
                for v in range(4 * NH + 4):
                    if v < 4 * NH:
                        n = (v % 4 + 1) * P
                        sc.wait_ge(s_z[l], v + 1)
                        if v >= 2:
                            sc.wait_ge(s_pt[l], v - 1)
                        if l == 0:
                            A.activation(attE[:, v % 2, 512 - n:512], bank[v % 2][:, 0:n], ACT.Sigmoid, scale=-SCALE)
                            A.activation(attB[:, v % 2, 0:n], bank[v % 2][:, 0:n], ACT.Sigmoid, scale=SCALE).then_inc(s_pr[0], 1)
                        else:
                            sc.wait_ge(s_w[1], v + 1)
                            A.activation(attB[:, v % 2, 0:n], bank[v % 2][:, 0:n], ACT.Exp, scale=SCALE,
                                         bias=nb[:, v:v + 1], accum_out=rs[:, v:v + 1]).then_inc(s_pr[1], 1)
                    if 2 <= v < 4 * NH + 2:
                        u = v - 2
                        n = (u % 4 + 1) * P
                        sc.wait_ge(s_pt[l], u + 1)
                        A.copy(attP[:, u % 2, 0:n], bank[2 + u % 2][:, 0:n]).then_inc(s_ptv[l], 1)
                    if v >= 11 and v % 8 == 3:
                        pair = (v - 11) // 8
                        sc.wait_ge(s_o[l], pair + 1)
                        A.copy(xh[:, [4, 0][l] + pair, :], bank[6 + pair % 2][:, :]).then_inc(s_oh[l], 1)
                turn_high(l, TY, [4, 0][l], lambda j: A.copy(xh[:, j, :], turn_bank(l, TY, j)))
                if l == 1:
                    for g in range(4):
                        sc.wait_ge(s_pm, 4 + g + 1)
                        A.mul(xh[:, 4 + g, :], bank[2 + g % 2][:, :], pscale(g)).then_inc(s_ph, 1)
                highs(ffn[l] - 1)
                turn(l, TF, KD, lambda j: A.mul(xT[:, j, :], turn_bank(l, TF, j), gffn(l, j)))
                for m in range(MT):
                    sc.wait_ge(s_mD, movedD(l, GO, MT + m + 1))
                    stat(l, SF, h[:, m, :], m)
                sc.wait_ge(s_rr, 4 * l + SF + 1)
                for m in range(1, MT, 2):
                    A.mul(y[:, m, :], h[:, m, :], rr[:, l, SF, m:m + 1]).then_inc(s_xn[l], 1)
                sc.wait_ge(s_e[l], 1)
                for k in range(KP):
                    A.copy(pT[:, k, :], bank[6 + k][:, :]).then_inc(s_pse[l], 1)
                for g in range(2 * MT):
                    m, c = g // 2, g % 2
                    if g == 2:
                        sc.wait_ge(s_lgv[l], 1)
                        A.activation(exps[:, 1, :, :], exps[:, 0, :, :], ACT.Exp).then_inc(s_ex[l], 1)
                    sc.wait_ge(s_m, groups_done(l, GE, g + 1))
                    A.copy(E[:, m, c * 512:(c + 1) * 512], bank[2 + g % 4][:, :]).then_inc(s_mA, 1)
                    if c:
                        sc.wait_ge(s_mA, movedA(l, GE, g + 1))
                        stat(l, SE, E[:, m, :], m)

                def silu(e):
                    sc.wait_ge(s_g[l], e + 1)
                    A.activation(sil, bank[2][:, 0:DE], ACT.Silu).then_inc(s_sil[l], 1)

                def act_moved(e):
                    sc.wait_ge(s_at[l], e + 1)
                    A.copy(actT, bank[3][:, 0:DE]).then_inc(s_atv[l], 1)

                def result(e, p):
                    sc.wait_ge(s_dn[l], 2 * e + 2)
                    A.copy(ys[p][:, 512:D], bank[5][:, :]).then_inc(s_yA[l], 1)

                def store(e, p, done):
                    sc.wait_ge(s_yD[l], e + 1)
                    sc.wait_ge(s_yA[l], e + 1)
                    sc.dma_start(yg.rearrange("(t p) d -> t p d", p=P)[bass.ds(e, 1), :, :].rearrange("t p d -> p (t d)"), ys[p])\
                        .then_inc(done, 16)

                def stage(e, p, i, stored, expert):
                    silu(e - 1)
                    if stored:
                        sc.wait_ge(s_st[l][p], 16 * (i - 1))
                    result(e - 2, p)
                    sc.dma_start(wd[:, p, :, :], a["expert_w_down"][l, bass.ds(expert, 1)].rearrange("e (k p) n -> p (e k) n", p=P))\
                        .then_inc(s_wd[l][p], 16)
                    act_moved(e - 1)
                    store(e - 2, p, s_st[l][p])

                silu(0)
                act_moved(0)
                stage(2, 0, 1, False, 2)
                stage(3, 1, 1, False, 3)
                with sc.Fori(2, NE // 2) as i:
                    for p in range(2):
                        stage(2 * i + p, p, i, True, 2 * i + p)
                sc.wait_ge(s_ovi[l], 1)
                n = sc.value_load(ovi[0:1, OVT:OVT + 1], min_val=0, max_val=OVT // 2)
                with sc.If(n > 0):
                    with sc.Fori(0, n) as i:
                        for p in range(2):
                            expert = sc.value_load(ovi[0:1, bass.ds(2 * i + p, 1)], min_val=0, max_val=NE - 1)
                            stage(2 * i + (p + NE), p, i + NE // 2, True, expert)
                sc.wait_ge(s_st[l][0], 16 * n + 16 * (NE // 2 - 1))
                result(2 * n + (NE - 2), 0)
                store(2 * n + (NE - 2), 0, s_st[l][0])
                silu(2 * n + (NE - 1))
                act_moved(2 * n + (NE - 1))
                sc.wait_ge(s_st[l][1], 16 * n + 16 * (NE // 2 - 1))
                result(2 * n + (NE - 1), 1)
                store(2 * n + (NE - 1), 1, s_st[l][1])
                sc.wait_ge(s_st[l][0], 16 * n + 16 * NE // 2)
                sc.wait_ge(s_st[l][1], 16 * n + 16 * NE // 2)
                sc.sem_inc(s_end[l], 1)
                highs(ffn[l] + 1)
                for m in range(MT):
                    sc.wait_ge(s_cmb[l], m + 1)
                    if m == MT - 1:
                        turn_high(l, TP, KD, lambda j: A.copy(xh[:, j, :], turn_bank(l, TP, j)))
                    stat(l, SP_, h[:, m, :], m)
                highs(ffn[l] + 2)
                sc.wait_ge(s_rr, 4 * l + SP_ + 1)
                for g in range(2 * MT):
                    c, m = g // MT, g % MT
                    if l == 0 and g == MT:
                        for j in range(3):
                            high(first[1], j)
                    sc.wait_ge(s_m, groups_done(l, GG, g + 1))
                    if g >= 2:
                        sc.wait_ge(s_h[l], g - 1)
                    A.activation(gate[:, g % 2, :], bank[4 * c + m][:, :], ACT.Sigmoid, scale=rr[:, l, SP_, m:m + 1])\
                        .then_inc(s_gt[l], 1)
                    if l == 1 and g > MT:
                        sc.wait_ge(s_h[1], g)
                        sc.dma_start(out[0, (m - 1) * P:m * P, :], h[:, m - 1, :]).then_inc(s_out, 16)
                if l == 0:
                    high(first[1], 3)
            sc.wait_ge(s_h[1], 2 * MT)
            sc.dma_start(out[0, (MT - 1) * P:MT * P, :], h[:, MT - 1, :]).then_inc(s_out, 16)
            sc.wait_ge(s_out, 16 * MT)

        @block.gpsimd
        def _(pool):
            G = nc.gpsimd
            chain = [0]

            def link(ins):
                chain[0] += 1
                ins.then_inc(s_pool, 1)
                pool.wait_ge(s_pool, chain[0])

            pool.dma_start(cbf[:, :, :], a["c_bf"]).then_inc(s_cbf, 16)
            G.memset(zeros, 0.0).then_inc(s_zero, 1)
            link(G.memset(pw[:, :], -0.5))

            def root(dst, src, n, width, done):
                link(G.tensor_scalar(dst, src, 1.0 / n, EPS, ALU.mult, ALU.add))
                G.tensor_tensor(dst, dst, pw[:, 0:width], ALU.pow).then_inc(done, 1)

            def stat(l, which):
                pool.wait_ge(s_ss, MT * (4 * l + which + 1))
                root(rr[:, l, which, :], ss[:, l, which, :], D, MT, s_rr)

            for l in range(DEPTH):
                stat(l, SM)
                n = [1, 2][l]
                pool.wait_ge(s_hs[l], n)
                root(hrr[:, 0:n, :].rearrange("p a b -> p (a b)"), hss[:, 0:n, :].rearrange("p a b -> p (a b)"),
                     HD, n * MT * NH, s_hr[l])
                stat(l, SF)
                if l == 0:
                    pool.wait_ge(s_xgz, 16 * 5)
                pool.wait_ge(s_xn[l], MT)
                pool.wait_ge(s_pos[l], 1)
                for j in range(2):
                    for m in range(MT):
                        G.indirect_dma_start(xg, bass.IndirectOffsetOnAxis(posi[:, j, m:m + 1], 0), y[:, m, :], None)\
                            .then_inc(s_sc[l], 16)
                stat(l, SE)
                pool.wait_ge(s_end[l], 1)
                pool.wait_ge(s_sc[l], 16 * 2 * MT)
                for m in range(MT):
                    for j, dst in enumerate((y, G2)):
                        G.indirect_dma_start(dst[:, m, :], None, yg, bass.IndirectOffsetOnAxis(posi[:, j, m:m + 1], 0))\
                            .then_inc(s_gam[l][m], 16)
                stat(l, SP_)
                if l == 0:
                    pool.wait_ge(s_h[0], 2 * MT)
                    pool.dma_start(self_, a["c_sel"]).then_inc(s_selin, 16)

        @block.vector
        def _(dve):
            Ve = nc.vector
            chain = [0]

            def link(ins):
                chain[0] += 1
                ins.then_inc(s_dve, 1)
                dve.wait_ge(s_dve, chain[0])

            def turn(l, which, n, put):
                for j in range(0, n, 2):
                    dve.wait_ge(s_t, steps_turned(l, which, j + 1))
                    put(j).then_inc(s_tD, 1)

            def over(x, n):
                return x.unsqueeze(2).to_broadcast([P, MT, n])

            def first_max(values, n, top, mask, t):
                link(Ve.tensor_reduce(top, values, AX, ALU.max))
                link(Ve.tensor_tensor(t[0], values, over(top, n), ALU.is_ge))
                link(Ve.tensor_tensor(t[1], t[0], small[:, NE - n:NE].unsqueeze(1).to_broadcast([P, MT, n]), ALU.mult))
                link(Ve.tensor_reduce(mxs[:, 7, :], t[1], AX, ALU.max))
                link(Ve.tensor_tensor(mask, t[1], over(mxs[:, 7, :], n), ALU.is_equal))

            def low(c, j):
                dve.wait_ge(s_hi, unit(c, j) + 1)
                Ve.tensor_tensor(wl[:, j, :, :], raw(c, j), f32(wh[:, j, :, :]), ALU.subtract).then_inc(s_lo, 1)

            def lows(c):
                for j in range(4):
                    low(c, j)

            def turn_low(l, which, n, gain=None):
                for j in range(n):
                    dve.wait_ge(s_tA, steps_moved(l, which, j + 1))
                    x, b = xl[:, j, :], turn_bank(l, which, j)
                    if gain:
                        ins = Ve.scalar_tensor_tensor(x, b, gain(j), f32(xh[:, j, :]), ALU.mult, ALU.subtract)
                    else:
                        ins = Ve.tensor_tensor(x, b, f32(xh[:, j, :]), ALU.subtract)
                    ins.then_inc(s_tD, 1)

            dve.wait_ge(s_gT, 1)
            Ve.tensor_copy(gcol[:, :], bank[7][:, 0:46]).then_inc(s_gcol, 1)
            dve.wait_ge(s_gcol, 1)
            for l in range(DEPTH):
                turn_low(l, TM, KD, lambda j: gmix(l, j))
                if l == 0:
                    dve.wait_ge(s_ident, 16)
                    dve.wait_ge(s_sgin, 16)
                    Ve.tensor_tensor(sgw, sgw, tril.unsqueeze(1).to_broadcast([P, NH, P]), ALU.mult).then_inc(s_sg, 1)
                    lows(0)
                heads = lambda x: x.rearrange("p m (h d) -> p (m h) d", d=HD)
                if l == 0:
                    for b in range(2):
                        dve.wait_ge(s_sgT, b + 1)
                        Ve.tensor_copy(sguT[:, 4 * b:4 * b + 4, :].rearrange("p h t -> p (h t)"), bank[6 + b][:, :]).then_inc(s_mixd, 1)
                    dve.wait_ge(s_const, 16 * 12)
                    dve.wait_ge(s_wf, 1)
                    Ve.tensor_tensor(wfl[:, :, :], wf[:, :, :], f32(wfh[:, :, :]), ALU.subtract).then_inc(s_wf, 1)
                else:
                    dve.wait_ge(s_fa, 1)
                    Ve.tensor_copy(Flog, bank[7][0:NH, :]).then_inc(s_fx, 1)
                dve.wait_ge(s_rr, 4 * l + SM + 1)
                if l == 1:
                    dve.wait_ge(s_fa, 2)
                    link(Ve.tensor_tensor(lf[:, 3, :, :], bank[7][:, 0:MT * NH].rearrange("p (m h) -> p m h", h=NH),
                                          over(rr[:, 1, SM, :], NH), ALU.mult))
                    Ve.tensor_tensor(lf[:, 0, :, :], lf[:, 3, :, :], fb[:, :].unsqueeze(1).to_broadcast([P, MT, NH]), ALU.add).then_inc(s_f, 1)
                sq = attB[:, :, :].rearrange("p a n -> p (a n)")
                dst = [[Q, K, V, VA, U], [Q, K, V, y[:, :, W:]]][l]
                for c in range(NIN[l] + 1):
                    if c and c < NIN[l]:
                        lows(first[l] + c)
                    elif c:
                        lows(ffn[l] - 2)
                    if l == 1 and c == 2:
                        dve.wait_ge(s_fl, 1)
                        Ve.scalar_tensor_tensor(lf[:, 3, :, :], lf[:, 0, :, :], 0.0, lf[:, 2, :, :], ALU.min, ALU.subtract).then_inc(s_fc, 1)
                    if l == 1 and c == 4:
                        dve.wait_ge(s_hr[1], 1)
                        for b, x in enumerate((Q, K)):
                            Ve.tensor_tensor(heads(x), heads(x), hrr[:, b, :].unsqueeze(2).to_broadcast([P, MT * NH, HD]), ALU.mult)\
                                .then_inc(s_qn[1], 1)
                    if c == 0:
                        continue
                    k = c - 1
                    for m in range(MT):
                        if by_vector(l, k, m):
                            dve.wait_ge(s_m, groups_done(l, GI, MT * k + m + 1))
                            Ve.tensor_scalar(dst[k][:, m, :], bank[4 * (k % 2) + m][:, :], rr[:, l, SM, m:m + 1], None, ALU.mult)\
                                .then_inc(s_mD, 1)
                    if l == 1 and k == 2:
                        dve.wait_ge(s_fa, 3)
                        link(Ve.tensor_copy(Frow, bank[7][0:NH, :]))
                        link(Ve.memset(Fp[0:96, :], 0.0))
                        Ve.tensor_copy(Fp[0:NH, :], Frow).then_inc(s_fx, 1)
                        dve.wait_ge(s_fx, 2)
                        link(Ve.tensor_tensor(Frest, Frow, Fp[0:NH, :], ALU.subtract))
                        link(Ve.tensor_copy(Fp[32:32 + NH, :], Frest))
                        link(Ve.tensor_copy(Frow, Fp[32:32 + NH, :]))
                        link(Ve.tensor_tensor(Frest, Frest, Frow, ALU.subtract))
                        Ve.tensor_copy(Fp[64:64 + NH, :], Frest).then_inc(s_fp, 1)
                    if l == 1 and k == 1:
                        dve.wait_ge(s_mD, in_moved(1, 2)[0])
                        dve.wait_ge(s_mA, in_moved(1, 2)[1])
                        for b, x in enumerate((Q, K)):
                            if b:
                                dve.wait_ge(s_hs[1], 1)
                            for half in range(2):
                                part = x[:, 2 * half:2 * half + 2, :]
                                link(Ve.tensor_tensor(sq.rearrange("p (m n) -> p m n", m=2), part, part, ALU.mult))
                                ins = Ve.tensor_reduce(hss[:, b, 16 * half:16 * half + 16], sq.rearrange("p (a d) -> p a d", d=HD), AX, ALU.add)
                                if half == 0:
                                    link(ins)
                                else:
                                    ins.then_inc(s_hs[1], 1)
                if l == 0:
                    link(Ve.memset(attS[:, :, 512:513], 1.0))
                    turn(0, TQ, 8, lambda j: Ve.tensor_copy(qT[:, j, :] if j < 4 else kT[:, j - 4, :], turn_bank(0, TQ, j)))
                else:
                    turn(1, TQ, 8, lambda j: Ve.tensor_scalar(qT[:, j, :] if j < 4 else kT[:, j - 4, :], turn_bank(1, TQ, j),
                                                              qkg(j // 4), None, ALU.mult))

                square = rows(xT[:, 0:4, :].rearrange("p k n -> p (k n)"))

                def pair_out(pair):
                    dve.wait_ge(s_oh[l], pair + 1)
                    k = [4, 0][l] + pair
                    Ve.tensor_tensor(xl[:, k, :], bank[6 + pair % 2][:, :], f32(xh[:, k, :]), ALU.subtract).then_inc(s_ov[l], 1)

                for v in range(4 * NH + 5):
                    if v < 4 * NH:
                        n = (v % 4 + 1) * P
                        b = v % 2
                        if l == 0:
                            dve.wait_ge(s_pr[0], v + 1)
                            link(Ve.tensor_tensor_scan(attS[:, b, 512 - n:512][:, ::-1], attE[:, b, 512 - n:512][:, ::-1],
                                                       attE[:, b, 512 - n:512][:, ::-1], 1.0, ALU.mult, ALU.bypass))
                            Ve.tensor_tensor(attB[:, b, 0:n], attB[:, b, 0:n], attS[:, b, 513 - n:513], ALU.mult).then_inc(s_w[0], 1)
                        else:
                            dve.wait_ge(s_z[1], v + 1)
                            link(Ve.tensor_reduce(mx[:, v:v + 1], bank[b][:, 0:n], AX, ALU.max))
                            Ve.tensor_scalar(nb[:, v:v + 1], mx[:, v:v + 1], -SCALE, None, ALU.mult).then_inc(s_w[1], 1)
                    if l == 1 and 1 <= v <= 4 * NH:
                        u = v - 1
                        n = (u % 4 + 1) * P
                        dve.wait_ge(s_pr[1], u + 1)
                        link(Ve.reciprocal(ri[:, u:u + 1], rs[:, u:u + 1]))
                        Ve.tensor_scalar(attB[:, u % 2, 0:n], attB[:, u % 2, 0:n], ri[:, u:u + 1], None, ALU.mult).then_inc(s_wn, 1)
                    if v >= 12 and v % 8 == 4:
                        pair_out((v - 12) // 8)
                    if l == 0 and v == 6:
                        dve.wait_ge(s_mA, in_moved(0, NIN[0])[1])
                        link(Ve.tensor_tensor(square, VA, VA, ALU.mult))
                    if l == 0 and v == 8:
                        Ve.tensor_reduce(hss[:, 0, :], heads(square), AX, ALU.add).then_inc(s_hs[0], 1)
                    if l == 0 and v == 20:
                        dve.wait_ge(s_hr[0], 1)
                        link(Ve.tensor_tensor(heads(VA), heads(VA), hrr[:, 0, :].unsqueeze(2).to_broadcast([P, MT * NH, HD]), ALU.mult))
                    if l == 0 and v == 24:
                        Ve.tensor_tensor(VA, VA, mixg[:, :].unsqueeze(1).to_broadcast([P, MT, W]), ALU.mult).then_inc(s_qn[0], 1)
                if l == 0:
                    for hd in range(NH):
                        if hd % 2 == 0:
                            dve.wait_ge(s_pm, hd // 2 + 1)
                        o = bank[hd // 2][:, 256 * (hd % 2):256 * (hd % 2) + 256].rearrange("p (m d) -> p m d", d=HD)
                        u = U[:, :, hd * HD:(hd + 1) * HD]
                        Ve.scalar_tensor_tensor(u, o, sgb(hd), u, ALU.add, ALU.mult).then_inc(s_y[0], 1)
                turn_low(l, TY, [4, 0][l])
                if l == 1:
                    for g in range(4):
                        dve.wait_ge(s_pl, g + 1)
                        Ve.tensor_copy(pT2[:, g % 2, :], bank[g % 2][:, :]).then_inc(s_plv, 1)
                        dve.wait_ge(s_ph, g + 1)
                        Ve.scalar_tensor_tensor(xl[:, 4 + g, :], bank[2 + g % 2][:, :], pscale(g), f32(xh[:, 4 + g, :]),
                                                ALU.mult, ALU.subtract).then_inc(s_y[1], 1)
                lows(ffn[l] - 1)
                for g in range(2 * MT):
                    c, m = g // MT, g % MT
                    dve.wait_ge(s_m, groups_done(l, GO, g + 1))
                    hh = h[:, m, c * 512:(c + 1) * 512]
                    Ve.tensor_tensor(hh, hh, bank[4 * c + m][:, :], ALU.add).then_inc(s_mD, 1)
                turn(l, TF, KD, lambda j: Ve.tensor_scalar(xT[:, j, :], turn_bank(l, TF, j), gffn(l, j), None, ALU.mult))
                dve.wait_ge(s_rr, 4 * l + SF + 1)
                dve.wait_ge(s_mD, movedD(l, GO, 2 * MT))
                for m in range(0, MT, 2):
                    Ve.tensor_scalar(y[:, m, :], h[:, m, :], rr[:, l, SF, m:m + 1], None, ALU.mult).then_inc(s_xn[l], 1)
                dve.wait_ge(s_lg[l], 1)
                lp = bank[0][:, 0:MT * 20].rearrange("p (m n) -> p m n", n=20)
                link(Ve.tensor_tensor(lg[:, :, :], lp, over(rr[:, l, SF, :], 20), ALU.mult))
                Ve.tensor_tensor(lg[:, :, 0:4], lg[:, :, 0:4], rb[:, l, 0:4].unsqueeze(1).to_broadcast([P, MT, 4]), ALU.add)
                link(Ve.tensor_tensor(le[:, :, :], lg[:, :, 4:20], rb[:, l, 4:20].unsqueeze(1).to_broadcast([P, MT, NE]), ALU.add))
                first_max(lg[:, :, 0:4], NG, mxs[:, 0, :], gmask[:, :, :], (t16[:, 0, :, 0:NG], t16[:, 1, :, 0:NG]))
                Ve.tensor_tensor(exps[:, 0, :, 0:4], lg[:, :, 0:4], over(mxs[:, 0, :], NG), ALU.subtract)
                link(Ve.tensor_scalar(t16[:, 2, :, 0:NG], gmask[:, :, :], -NEG, NEG, ALU.mult, ALU.add))
                link(Ve.tensor_copy(lg[:, :, 0:4], t16[:, 2, :, 0:NG]))
                link(Ve.tensor_copy(row16[:, 5, :], lg[:, :, 0:4]))
                lev = le[:, :, :].rearrange("p m (g e) -> p (m g) e", g=NG)
                link(Ve.tensor_tensor(lev, lev, row16[:, 5, :].unsqueeze(2).to_broadcast([P, MT * NG, EG]), ALU.add))
                first_max(le[:, :, :], NE, mxs[:, 1, :], mask1[:, :, :], (t16[:, 0, :, :], t16[:, 1, :, :]))
                link(Ve.scalar_tensor_tensor(le[:, :, :], mask1[:, :, :], 3 * NEG, le[:, :, :], ALU.mult, ALU.add))
                first_max(le[:, :, :], NE, mxs[:, 2, :], mask2[:, :, :], (t16[:, 0, :, :], t16[:, 1, :, :]))
                Ve.tensor_tensor(exps[:, 0, :, 4:5], mxs[:, 2, :].unsqueeze(2), mxs[:, 1, :].unsqueeze(2), ALU.subtract).then_inc(s_lgv[l], 1)
                Ve.tensor_tensor(selb[:, :, :], mask1[:, :, :], mask2[:, :, :], ALU.add).then_inc(s_sel[l], 1)
                dve.wait_ge(s_rank[l], 1)
                rk = bank[1][:, 0:MT * NE].rearrange("p (m e) -> p m e", e=NE)
                ct = row16[:, 4, :]
                link(Ve.tensor_copy(ct, bank[1][:, 64:64 + NE]))
                link(Ve.tensor_scalar(row16[:, 0, :], ct, float(P + 1), None, ALU.is_ge))
                for k in range(2, S // P):
                    link(Ve.scalar_tensor_tensor(row16[:, 0, :], ct, float(k * P + 1), row16[:, 0, :], ALU.is_ge, ALU.add))
                link(Ve.tensor_tensor_scan(row16[:, 1, :], row16[:, 0, :], row16[:, 0, :], 0.0, ALU.add, ALU.bypass))
                link(Ve.tensor_tensor(row16[:, 2, :], row16[:, 1, :], row16[:, 0, :], ALU.subtract))
                link(Ve.tensor_scalar(row16[:, 2, :], row16[:, 2, :], float(P), float((NE - 1) * P), ALU.mult, ALU.add))
                link(Ve.tensor_tensor(row16[:, 2, :], row16[:, 2, :], small[:, NE:2 * NE], ALU.subtract))
                link(Ve.tensor_scalar(t16[:, 0, :, :], rk, float(P), None, ALU.is_ge))
                link(Ve.tensor_tensor(t16[:, 0, :, :], t16[:, 0, :, :], row16[:, 2, :].unsqueeze(1).to_broadcast([P, MT, NE]), ALU.mult))
                link(Ve.tensor_tensor(t16[:, 0, :, :], t16[:, 0, :, :], rk, ALU.add))
                link(Ve.tensor_tensor(t16[:, 0, :, :], t16[:, 0, :, :], small[:, NE:2 * NE].unsqueeze(1).to_broadcast([P, MT, NE]), ALU.add))
                Ve.tensor_tensor(t16[:, 1, :, :], t16[:, 0, :, :], mask1[:, :, :], ALU.mult)
                link(Ve.tensor_tensor(t16[:, 2, :, :], t16[:, 0, :, :], mask2[:, :, :], ALU.mult))
                Ve.tensor_reduce(posf[:, 0, :], t16[:, 1, :, :], AX, ALU.add)
                link(Ve.tensor_reduce(posf[:, 1, :], t16[:, 2, :, :], AX, ALU.add))
                Ve.tensor_copy(posi[:, :, :], posf[:, :, :]).then_inc(s_pos[l], 1)
                link(Ve.tensor_tensor(ovf[:, :, :], row16[0:1, 1, :].unsqueeze(1).to_broadcast([1, OVT, NE]),
                                      small[0:1, 32:32 + OVT].unsqueeze(2).to_broadcast([1, OVT, NE]), ALU.is_le))
                link(Ve.tensor_reduce(ove[:, 0:OVT], ovf[:, :, :], AX, ALU.add))
                link(Ve.tensor_scalar(ove[:, 0:OVT], ove[:, 0:OVT], float(NE - 1), None, ALU.min))
                link(Ve.tensor_tensor(ovf[:, 0, 0:4], small[0:1, 40:44], row16[0:1, 1, NE - 1:NE].to_broadcast([1, 4]), ALU.is_le))
                link(Ve.tensor_reduce(ove[:, OVT:OVT + 1], ovf[:, 0:1, 0:4], AX, ALU.add))
                Ve.tensor_copy(ovi[:, :], ove[:, :]).then_inc(s_ovi[l], 1)
                dve.wait_ge(s_ex[l], 1)
                link(Ve.tensor_reduce(mxs[:, 3, :], exps[:, 1, :, 0:4], AX, ALU.add))
                ex2 = exps[:, 1, :, 4:5]
                col = lambda k: mxs[:, k, :].unsqueeze(2)
                link(Ve.tensor_scalar(col(4), ex2, 1.0, None, ALU.add))
                link(Ve.tensor_tensor(mxs[:, 5, :], mxs[:, 3, :], mxs[:, 4, :], ALU.mult))
                link(Ve.reciprocal(wts[:, 0, :], mxs[:, 5, :]))
                link(Ve.tensor_tensor(wts[:, 1, :].unsqueeze(2), wts[:, 0, :].unsqueeze(2), ex2, ALU.mult))

                gains = lambda b: gffn(l, 4 * b, 4).unsqueeze(2).to_broadcast([P, 4, P])
                tb = lambda b: bank[b][:, :].rearrange("p (k n) -> p k n", k=4)

                def rows_in(e):
                    for b in range(2):
                        dve.wait_ge(s_tx[l], 2 * e + b + 1)
                        Ve.tensor_tensor(xgT[:, 4 * b:4 * b + 4, :], tb(b), gains(b), ALU.mult).then_inc(s_xv[l], 1)

                def activations(e):
                    dve.wait_ge(s_sil[l], e + 1)
                    Ve.tensor_tensor(act, sil, bank[2][:, DE:2 * DE], ALU.mult).then_inc(s_act[l], 1)

                def result(e, p):
                    dve.wait_ge(s_dn[l], 2 * e + 1)
                    Ve.tensor_copy(ys[p][:, 0:512], bank[4][:, :]).then_inc(s_yD[l], 1)

                def stage(e, p, i, stored):
                    rows_in(e)
                    activations(e - 1)
                    if stored:
                        dve.wait_ge(s_st[l][p], 16 * (i - 1))
                    result(e - 2, p)

                rows_in(0)
                rows_in(1)
                activations(0)
                stage(2, 0, 1, False)
                dve.wait_ge(s_rr, 4 * l + SE + 1)
                dve.wait_ge(s_pg[l], 16)
                for m in range(MT):
                    if m == 2:
                        stage(3, 1, 1, False)
                    ins = Ve.scalar_tensor_tensor(E[:, m, :], E[:, m, :], rr[:, l, SE, m:m + 1], pgain, ALU.mult, ALU.mult)
                link(ins)
                with dve.Fori(2, NE // 2) as i:
                    for p in range(2):
                        stage(2 * i + p, p, i, True)
                n = dve.value_load(ovi[0:1, OVT:OVT + 1], min_val=0, max_val=OVT // 2)
                with dve.If(n > 0):
                    with dve.Fori(0, n) as i:
                        for p in range(2):
                            stage(2 * i + (p + NE), p, i + NE // 2, True)
                dve.wait_ge(s_st[l][0], 16 * n + 16 * (NE // 2 - 1))
                result(2 * n + (NE - 2), 0)
                activations(2 * n + (NE - 1))
                dve.wait_ge(s_st[l][1], 16 * n + 16 * (NE // 2 - 1))
                result(2 * n + (NE - 1), 1)
                lows(ffn[l] + 1)
                for m in range(MT):
                    dve.wait_ge(s_gam[l][m], 32)
                    link(Ve.scalar_tensor_tensor(h[:, m, :], y[:, m, :], wts[:, 0, m:m + 1], h[:, m, :], ALU.mult, ALU.add))
                    Ve.scalar_tensor_tensor(h[:, m, :], G2[:, m, :], wts[:, 1, m:m + 1], h[:, m, :], ALU.mult, ALU.add).then_inc(s_cmb[l], 1)
                turn_low(l, TP, KD)
                lows(ffn[l] + 2)
                for g in range(2 * MT):
                    c, m = g // MT, g % MT
                    if l == 0 and g == MT:
                        for j in range(3):
                            low(first[1], j)
                    dve.wait_ge(s_gt[l], g + 1)
                    part = slice(c * 512, (c + 1) * 512)
                    link(Ve.tensor_tensor(E[:, m, part], E[:, m, part], gate[:, g % 2, :], ALU.mult))
                    Ve.tensor_tensor(h[:, m, part], h[:, m, part], E[:, m, part], ALU.add).then_inc(s_h[l], 1)
                if l == 0:
                    low(first[1], 3)

        @block.tensor
        def _(pe):
            T = nc.tensor

            both = (TM, TY, TP)

            def turn(l, which, n, src, ready=None):
                for j in range(n):
                    for m in range(MT):
                        if ready:
                            ready(j, m)
                        mm = T.transpose(turn_bank(l, which, j)[:, m * P:(m + 1) * P], src(j, m), ident)
                    mm.then_inc(s_t, 1)

            def turned(l, which, n):
                pe.wait_ge(s_tD, steps_moved(l, which, n if which in both else n // 2))
                pe.wait_ge(s_tA, steps_moved(l, which, n if which in both else n // 2))

            def three(dst, x0, x1, w0, w1, start, stop):
                T.matmul(dst, x0, w0, start=start, stop=False)
                T.matmul(dst, x0, w1, start=False, stop=False)
                return T.matmul(dst, x1, w0, start=False, stop=stop)

            def product(c, banks):
                for j in range(4):
                    pe.wait_ge(s_lo, unit(c, j) + 1)
                    for k in (2 * j, 2 * j + 1):
                        for m in range(MT):
                            tok = slice(m * P, (m + 1) * P)
                            mm = three(banks[m][:, :], xh[:, k, tok], xl[:, k, tok], wh[:, j, k % 2, :], wl[:, j, k % 2, :],
                                       k == 0, k == KD - 1)
                            if k == KD - 1:
                                mm.then_inc(s_m, 1)
                    if j < 3:
                        mm.then_inc(s_un, 1)

            def group(dst, m, w, nk, x=None):
                for k in range(nk):
                    mm = T.matmul(dst, (x if x is not None else xT)[:, k, m * P:(m + 1) * P], w(k), start=(k == 0), stop=(k == nk - 1))
                return mm

            pe.wait_ge(s_ident, 16)
            pe.wait_ge(s_cbf, 16)
            pe.wait_ge(s_grow, 16 * 6)
            T.transpose(bank[7][:, 0:46], grow[:, :], ident[0:46, 0:46]).then_inc(s_gT, 1)
            for l in range(DEPTH):
                def mixer_input(j, m):
                    if l == 0 and j == 0:
                        pe.wait_ge(s_in[m], 16)
                    if l == 0 and j == KD - 1:
                        pe.wait_ge(s_gcol, 1)
                    if l == 1 and j % 4 == 0:
                        pe.wait_ge(s_h[0], MT * (j // 4) + m + 1)

                turn(l, TM, KD, lambda j, m: h[:, m, j * P:(j + 1) * P], mixer_input)
                turned(l, TM, KD)
                if l == 0:
                    pe.wait_ge(s_sg, 1)
                    for hd in range(NH):
                        mm = T.transpose(bank[6 + hd // 4][:, (hd % 4) * P:(hd % 4 + 1) * P], sgw[:, hd, :], ident)
                        if hd % 4 == 3:
                            mm.then_inc(s_sgT, 1)
                else:
                    pe.wait_ge(s_wf, 2)
                    for k in range(KD):
                        mm = three(bank[7][0:NH, :], wfh[:, k, :], wfl[:, k, :], xh[:, k, :], xl[:, k, :], k == 0, k == KD - 1)
                    mm.then_inc(s_fa, 1)
                    pe.wait_ge(s_fx, 1)
                    for m in range(MT):
                        mm = T.transpose(bank[7][:, m * NH:(m + 1) * NH], Flog[:, m * P:(m + 1) * P], ident[0:NH, 0:NH])
                    mm.then_inc(s_fa, 1)
                for c in range(NIN[l]):
                    if c == 1 and l == 0:
                        pe.wait_ge(s_mixd, 2)
                    if c == 1 and l == 1:
                        pe.wait_ge(s_f, 1)
                    if c >= 2:
                        pe.wait_ge(s_mD, in_moved(l, c - 1)[0])
                        pe.wait_ge(s_mA, in_moved(l, c - 1)[1])
                    if l == 1 and c == 3:
                        pe.wait_ge(s_fc, 1)
                        for i in range(MT):
                            for j in range(i + 1):
                                mm = T.matmul(bank[7][0:NH, i * P:(i + 1) * P], lf[:, 3, j, :], upto if i == j else ones,
                                              start=(j == 0), stop=(j == i))
                        mm.then_inc(s_fa, 1)
                        pe.wait_ge(s_fx, 2)
                    product(first[l] + c, bank[4 * (c % 2):4 * (c % 2) + 4])
                if l == 1:
                    pe.wait_ge(s_qn[1], 2)

                def heads_input(j, m):
                    if m == 0 and j % 4 == 0:
                        pe.wait_ge(s_mD, in_moved(l, NIN[l] - 1 + j // 4)[0])
                        pe.wait_ge(s_mA, in_moved(l, NIN[l] - 1 + j // 4)[1])

                turn(l, TQ, 8, lambda j, m: (Q if j < 4 else K)[:, m, (j % 4) * P:(j % 4 + 1) * P], heads_input)
                turned(l, TQ, 8)
                if l == 1:
                    pe.wait_ge(s_fp, 1)
                    pe.wait_ge(s_mixin, 32)
                    pe.wait_ge(s_selin, 16)
                for v in range(4 * NH + 3):
                    if v < 4 * NH:
                        hd, i = v // 4, v % 4
                        n = (i + 1) * P
                        r = slice(HD * (hd % 2), HD * (hd % 2) + HD)
                        if v >= 2:
                            pe.wait_ge(s_pr[l], v - 1)
                        T.matmul(bank[v % 2][:, n - P:n], identb, strictb if l == 0 else causalb, start=True, stop=False,
                                 skip_group_check=True)
                        if l == 1:
                            T.matmul(bank[v % 2][:, 0:n], self_[0:96, hd, :], Fp[0:96, 0:n], start=False, stop=False,
                                     skip_group_check=True)
                        T.matmul(bank[v % 2][:, 0:n], qT[r, hd // 2, i * P:(i + 1) * P], kT[r, hd // 2, 0:n], start=False, stop=True,
                                 skip_group_check=True).then_inc(s_z[l], 1)
                    if 2 <= v < 4 * NH + 2:
                        u = v - 2
                        pe.wait_ge(s_w[0] if l == 0 else s_wn, u + 1)
                        for j in range(u % 4 + 1):
                            mm = T.transpose(bank[2 + u % 2][:, j * P:(j + 1) * P], attB[:, u % 2, j * P:(j + 1) * P], ident)
                        mm.then_inc(s_pt[l], 1)
                    if v >= 3:
                        u = v - 3
                        hd, i = u // 4, u % 4
                        pe.wait_ge(s_ptv[l], u + 1)
                        if i == 0 and hd % 2 == 0 and hd >= 4:
                            pe.wait_ge(s_ov[l], hd // 2 - 1)
                        for j in range(i + 1):
                            mm = T.matmul(bank[6 + hd // 2 % 2][HD * (hd % 2):HD * (hd % 2) + HD, i * P:(i + 1) * P],
                                          V[:, j, hd * HD:(hd + 1) * HD], attP[:, u % 2, j * P:(j + 1) * P], start=(j == 0), stop=(j == i))
                        if i == 3 and hd % 2:
                            mm.then_inc(s_o[l], 1)
                if l == 0:
                    pe.wait_ge(s_qn[0], 1)
                    for hd in range(NH):
                        mm = T.matmul(bank[hd // 2][:, 256 * (hd % 2):256 * (hd % 2) + 256], sguT[:, hd, :],
                                      VA[:, :, hd * HD:(hd + 1) * HD], start=True, stop=True)
                        if hd % 2:
                            mm.then_inc(s_pm, 1)
                    pe.wait_ge(s_y[0], NH)
                    pe.wait_ge(s_ov[0], NH // 2)
                    turn(0, TY, 4, lambda j, m: y[:, m, j * P:(j + 1) * P])
                    turned(0, TY, 4)
                else:
                    for g in range(4):
                        for j in range(MT):
                            width = BW if j < MT - 1 else P
                            mm = T.matmul(bank[g % 2][:, j * P:j * P + width], y[:, j, W + g * P:W + (g + 1) * P],
                                          bands[:, 1 if j == 0 else 0, g, 0:width], start=(j == 0), stop=(j == MT - 1),
                                          skip_group_check=True)
                        mm.then_inc(s_pl, 1)
                        pe.wait_ge(s_plv, g + 1)
                        T.matmul(bank[2 + g % 2][:, :], poolw[:, g, :], pT2[:, g % 2, :], start=True, stop=True).then_inc(s_pm, 1)
                    pe.wait_ge(s_ov[1], NH // 2)
                    pe.wait_ge(s_y[1], 4)
                for c in range(2):
                    product(ffn[l] - 2 + c, bank[4 * c:4 * c + 4])
                turn(l, TF, KD, lambda j, m: h[:, m, j * P:(j + 1) * P],
                     lambda j, m: pe.wait_ge(s_mD, movedD(l, GO, MT * (j // 4) + m + 1)) if j % 4 == 0 else None)
                turned(l, TF, KD)
                pe.wait_ge(s_const, 16 * 12)
                for m in range(MT):
                    mm = group(bank[0][:, m * 20:(m + 1) * 20], m, lambda k: wr[:, l, k, :], KD)
                mm.then_inc(s_lg[l], 1)
                pe.wait_ge(s_pin[l], 16)
                for k in range(KP):
                    for m in range(MT):
                        mm = T.transpose(bank[6 + k][:, m * P:(m + 1) * P], pin[:, m, k * P:(k + 1) * P], ident)
                mm.then_inc(s_e[l], 1)
                pe.wait_ge(s_pse[l], KP)
                c = ffn[l]
                chunk_ready(pe, c)
                wp = ring[:, c % 2, 0:2 * KP, :].rearrange("p (k n) c -> p k (n c)", k=KP)

                def embed(g):
                    if g >= 4:
                        pe.wait_ge(s_mA, movedA(l, GE, g - 3))
                    group(bank[2 + g % 4][:, :], g // 2, lambda k: wp[:, k, (g % 2) * 512:(g % 2 + 1) * 512], KP, pT).then_inc(s_m, 1)

                embed(0)
                pe.wait_ge(s_sel[l], 1)
                for m in range(MT):
                    for j in range(m + 1):
                        T.matmul(bank[1][:, m * NE:(m + 1) * NE], beforeb if j == m else onesb, selb[:, j, :],
                                 start=(j == 0), stop=(j == m))
                for j in range(MT):
                    mm = T.matmul(bank[1][:, 64:64 + NE], onesb, selb[:, j, :], start=(j == 0), stop=(j == MT - 1))
                mm.then_inc(s_rank[l], 1)
                for g in range(1, 2 * MT):
                    embed(g)
                pe.wait_ge(s_pos[l], 1)
                pe.wait_ge(s_mA, movedA(l, GE, 2 * MT))

                def rows_turned(e, p, i):
                    pe.wait_ge(s_xl[l][p], 16 * i + 16)
                    turn_rows(e, p)

                def turn_rows(e, p):
                    for b in range(2):
                        for k in range(4):
                            mm = T.transpose(bank[b][:, k * P:(k + 1) * P], xs[p][:, (4 * b + k) * P:(4 * b + k + 1) * P], ident)
                        mm.then_inc(s_tx[l], 1)

                def gate_up(e, p, i):
                    pe.wait_ge(s_gu[l][p], 32 * i + 32)
                    multiply_gate_up(e, p)

                def multiply_gate_up(e, p):
                    pe.wait_ge(s_xv[l], 2 * e + 2)
                    for k in range(KD):
                        mm = T.matmul(bank[2][:, :], xgT[:, k, :], gu[:, p, k, :], start=(k == 0), stop=(k == KD - 1))
                    mm.then_inc(s_g[l], 1)

                def act_turned(e):
                    pe.wait_ge(s_act[l], e + 1)
                    for f in range(DE // P):
                        mm = T.transpose(bank[3][:, f * P:(f + 1) * P], act[:, f * P:(f + 1) * P], ident)
                    mm.then_inc(s_at[l], 1)

                def down(e, p, i):
                    pe.wait_ge(s_wd[l][p], 16 * i + 16)
                    multiply_down(e, p, first=isinstance(e, int) and e == 0)

                def multiply_down(e, p, first=False):
                    pe.wait_ge(s_atv[l], e + 1)
                    if not first:
                        pe.wait_ge(s_yD[l], e)
                        pe.wait_ge(s_yA[l], e)
                    for c in range(2):
                        for f in range(DE // P):
                            mm = T.matmul(bank[4 + c][:, :], actT[:, f * P:(f + 1) * P], wd[:, p, f, c * 512:(c + 1) * 512],
                                          start=(f == 0), stop=(f == DE // P - 1))
                        mm.then_inc(s_dn[l], 1)

                rows_turned(0, 0, 0)
                gate_up(0, 0, 0)
                rows_turned(1, 1, 0)
                act_turned(0)
                gate_up(1, 1, 0)

                def stage(e, p, i):
                    rows_turned(e, p, i)
                    down(e - 2, p, i - 1)
                    act_turned(e - 1)
                    gate_up(e, p, i)

                stage(2, 0, 1)
                stage(3, 1, 1)
                with pe.Fori(2, NE // 2) as i:
                    for p in range(2):
                        stage(2 * i + p, p, i)
                pe.wait_ge(s_ovi[l], 1)
                n = pe.value_load(ovi[0:1, OVT:OVT + 1], min_val=0, max_val=OVT // 2)
                with pe.If(n > 0):
                    with pe.Fori(0, n) as i:
                        for p in range(2):
                            stage(2 * i + (p + NE), p, i + NE // 2)
                down(2 * n + (NE - 2), 0, n + (NE // 2 - 1))
                act_turned(2 * n + (NE - 1))
                down(2 * n + (NE - 1), 1, n + (NE // 2 - 1))
                turn(l, TP, KD, lambda j, m: h[:, m, j * P:(j + 1) * P],
                     lambda j, m: None if j else pe.wait_ge(s_cmb[l], m + 1))
                turned(l, TP, KD)
                for c in range(2):
                    product(ffn[l] + 1 + c, bank[4 * c:4 * c + 4])
                pe.wait_ge(s_gt[l], 2 * MT)


_OUT = ((1, 512, 1024), "float32")


def kernel(**inputs):
    import numpy as _np
    import concourse.bacc as _bacc
    from concourse import mybir as _mybir
    from concourse.bass_utils import run_bass_kernel_spmd as _run

    nc = _bacc.Bacc("TRN2", target_bir_lowering=False, num_devices=1)
    arrays, aps = {}, {}
    for name, value in {**inputs, **constants()}.items():
        v = _np.ascontiguousarray(value)
        arrays[f"in_{name}_dram"] = v
        aps[name] = nc.dram_tensor(f"in_{name}_dram", v.shape, _mybir.dt.from_np(v.dtype), kind="ExternalInput").ap()
    out = nc.dram_tensor("out_dram", _OUT[0], _mybir.dt.from_np(_np.dtype(_OUT[1])), kind="ExternalOutput").ap()
    trunk(nc, aps, out)
    r = _run(nc, [arrays], core_ids=[0])
    return r.results[0]["out_dram"]
```

```python
from contextlib import ExitStack

import numpy as np
import concourse.bass as bass
from concourse import mybir

F32 = mybir.dt.float32
F32R = mybir.dt.float32r
BF16 = mybir.dt.bfloat16
I32 = mybir.dt.int32
ALU = mybir.AluOpType
ACT = mybir.ActivationFunctionType
AX = mybir.AxisListType.X

P = 128
D = 1024
S = 512
MT = S // P
KD = D // P
HD = 64
NH = 8
W = NH * HD
DEPTH = 2
PLE = 256
KP = PLE // P
NE = 16
NG = 4
EG = NE // NG
DE = 256
OV = 7
OVT = OV + OV % 2
TILES = NE + OVT
EPS = 1e-6
SCALE = HD ** -0.5
NEG = -1e30
WINDOWS = (2, 4, 8, 16)
BW = P + 16
SMALL = 48


def constants():
    i = np.arange(P)
    ident = np.eye(P, dtype=np.float32)
    strict = np.where(i[None, :] >= i[:, None], NEG, 0.0)
    causal = np.where(i[None, :] > i[:, None], NEG, 0.0)
    before = (i[:, None] < i[None, :]).astype(np.float32)
    cb = np.stack([ident, strict, causal, before, np.ones((P, P))], 1).astype(np.float32)
    upto = (i[:, None] <= i[None, :]).astype(np.float32)
    tril = (i[None, :] <= i[:, None]).astype(np.float32)
    cf = np.stack([ident, upto, np.ones((P, P), np.float32), tril], 1)
    bands = np.zeros((P, 2, len(WINDOWS), BW), np.float32)
    t = np.arange(BW)
    for first in (0, 1):
        for g, win in enumerate(WINDOWS):
            inside = (t[None, :] >= i[:, None]) & (t[None, :] - i[:, None] < win)
            count = np.minimum(t + 1, win) if first else np.full(BW, win)
            bands[:, first, g] = inside / count[None, :].astype(np.float32) - (t[None, :] == i[:, None])
    sel = np.zeros((P, NH, P), np.float32)
    for part in range(3):
        for h in range(NH):
            sel[32 * part + h, h, :] = -1.0 / SCALE
    small = np.zeros((P, SMALL), np.float32)
    small[:, 0:NE] = NE - np.arange(NE)
    small[:, NE:2 * NE] = P * np.arange(NE)
    small[:, 32:32 + OVT] = np.arange(OVT)
    small[:, 40:44] = 1 + 2 * np.arange(4)
    return {"c_bf": cb, "c_f": cf, "c_bands": bands, "c_sel": sel, "c_small": small}


def trunk(nc, a, out):
    ctx = ExitStack()
    with ctx:
        def sb(name, shape, dt=F32):
            return ctx.enter_context(nc.sbuf_tensor(name, shape, dt))

        def sem(name):
            return ctx.enter_context(nc.semaphore(name))

        def sems(name, n=DEPTH):
            return [sem(f"{name}{i}") for i in range(n)]

        bank = [ctx.enter_context(nc.psum_tensor(f"bank{i}", [P, 512], F32)) for i in range(8)]

        h = sb("h", [P, MT, D])
        def at_(name, offset, shape, dt=F32):
            return nc.alloc_sbuf_tensor_at(name, shape, dt, offset=arena + offset)

        arena = nc.sbuf_base
        sb("arena", [P, 16 * 1024])
        KB = 1024
        xT = at_("xT", 0, [P, KD, S])
        xh = at_("xh", 0, [P, KD, S], F32R)
        gu = at_("gu", 16 * KB, [P, 2, KD, 2 * DE])
        wd = at_("wd", 48 * KB, [P, 2, DE // P, D])
        ghi = at_("ghi", 0, [P, KD, 2 * DE], F32R)
        glo = at_("glo", 16 * KB, [P, 2, KD, 2 * DE], F32R)
        xl = at_("xl", 16 * KB, [P, KD, S], F32R)
        wh = at_("wh", 32 * KB, [P, 4, 2, 512], F32R)
        wl = at_("wl", 48 * KB, [P, 4, 2, 512], F32R)
        y_at = nc.sbuf_base
        y = sb("y", [P, MT, D])
        R1 = sb("R1", [P, 4 * S * MT // 2])
        R2 = sb("R2", [P, 4 * S * MT // 2])
        qk_at = nc.sbuf_base
        qkT = sb("qkT", [P, 8 * S])
        ring_at = nc.sbuf_base
        ring = sb("ring", [P, 2, KD, 512])
        attE = sb("attE", [P, 2, 512])
        attB = sb("attB", [P, 2, 512])
        attS = sb("attS", [P, 2, 513])
        attP = sb("attP", [P, 2, 512])
        cbf = sb("cbf", [P, 5, P], BF16)
        cf = sb("cf", [P, 4, P])
        small = sb("small", [P, SMALL])
        mixw = sb("mixw", [P, 2 * len(WINDOWS) * BW])
        mixg = sb("mixg", [P, 512])
        grow = sb("grow", [46, P])
        gcol = sb("gcol", [P, 46])
        wf = sb("wf", [P, KD, NH])
        wfh = sb("wfh", [P, KD, NH], F32R)
        wfl = sb("wfl", [P, KD, NH], F32R)
        fb = sb("fb", [P, NH])
        wr = sb("wr", [P, DEPTH, KD, 20])
        rb = sb("rb", [P, DEPTH, 20])
        ss = sb("ss", [P, DEPTH, 4, MT])
        rr = sb("rr", [P, DEPTH, 4, MT])
        hss = sb("hss", [P, 2, MT * NH])
        hrr = sb("hrr", [P, 2, MT * NH])
        pw = sb("pw", [P, 2 * MT * NH])
        mxs = sb("mxs", [P, 8, MT])
        wts = sb("wts", [P, 2, MT])
        selb = sb("selb", [P, MT, NE], BF16)
        posf = sb("posf", [P, 2, MT])
        posi = sb("posi", [P, 2, MT], I32)
        ove = sb("ove", [1, OVT + 1])
        ovi = sb("ovi", [1, OVT + 1], I32)
        rs = sb("rs", [P, 4 * NH])
        ri = sb("ri", [P, 4 * NH])
        mx = sb("mx", [P, 4 * NH])
        nb = sb("nb", [P, 4 * NH])
        lf = sb("lf", [P, 4, MT, NH])

        gmix = lambda l, k: gcol[:, l * KD + k:l * KD + k + 1]
        gffn = lambda l, k, n=1: gcol[:, (2 + l) * KD + k:(2 + l) * KD + k + n]
        sgb = lambda hd: gcol[:, 32 + hd:33 + hd]
        pscale = lambda g: gcol[:, 40 + g:41 + g]
        qkg = lambda b: gcol[:, 44 + b:45 + b]
        f32 = lambda x: x.bitcast(F32)
        ident, upto, ones, tril = (cf[:, i, :] for i in range(4))
        identb, strictb, causalb, beforeb, onesb = (cbf[:, i, :] for i in range(5))
        rows = lambda x: x.rearrange("p (m n) -> p m n", m=MT)
        VA, Q = rows(R1[:, 0:MT * W]), rows(R1[:, MT * W:])
        K, V = rows(R2[:, 0:MT * W]), rows(R2[:, MT * W:])
        U = y[:, :, 0:W]
        E = rows(R1[:, :])
        zeros = y[:, MT - 1, :]
        G2 = rows(R2[:, :])
        xs = [R2[:, p * D:(p + 1) * D] for p in range(2)]
        ys = [R2[:, (2 + p) * D:(3 + p) * D] for p in range(2)]
        qT = qkT[:, 0:4 * S].rearrange("p (c n) -> p c n", c=4)
        kT = qkT[:, 4 * S:].rearrange("p (c n) -> p c n", c=4)
        xgh = nc.alloc_sbuf_tensor_at("xgh", [P, KD, P], F32R, offset=qk_at)
        xgl = nc.alloc_sbuf_tensor_at("xgl", [P, KD, P], F32R, offset=qk_at + 2 * KD * P * 4)
        sil, act, actT = (qkT[:, D + i * DE:D + (i + 1) * DE] for i in range(3))
        pin = qkT[:, 2048:3072].rearrange("p (m n) -> p m n", m=MT)
        pT = qkT[:, 3072:4096].rearrange("p (k n) -> p k n", k=KP)
        pgain = attB[:, :, :].rearrange("p a n -> p (a n)")
        routing = attP[:, :, :].rearrange("p a n -> p (a n)")
        at = [0]

        def part(*shape):
            n = int(np.prod(shape))
            at[0] += n
            x = routing[:, at[0] - n:at[0]]
            names = " ".join(f"d{i}" for i in range(len(shape)))
            return x.rearrange(f"p ({names}) -> p {names}", **{f"d{i}": k for i, k in enumerate(shape)})

        t16, le, lg, exps = part(3, MT, NE), part(MT, NE), part(MT, 20), part(2, MT, 5)
        mask1, mask2, gmask, row16 = part(MT, NE), part(MT, NE), part(MT, NG), part(6, NE)
        ovf = part(OVT, NE)[0:1]
        junk = attS[:, :, :].rearrange("p a n -> p (a n)")[:, 0:D]
        gate = attE
        lgT = attE[0:20, 0, :]
        sgw = attP[:, :, :].rearrange("p a (h s) -> p (a h) s", s=P)
        sguT = mixw[:, 0:NH * P].rearrange("p (h t) -> p h t", h=NH)
        bands = mixw[:, :].rearrange("p (f g t) -> p f g t", f=2, g=4)
        ring_low = nc.alloc_sbuf_tensor_at("ring_low", [P, 2, KD, 512], F32R, offset=ring_at)
        y_low = nc.alloc_sbuf_tensor_at("y_low", [P, KD, 512], F32R, offset=y_at)
        frow = mixw[:, 0:D]
        poolw = mixg[:, :].rearrange("p (g d) -> p g d", g=4)
        self_ = attE[:, 0, :].bitcast(BF16).rearrange("p (h n) -> p h n", h=NH)
        Fp = attE[:, 1, :].bitcast(BF16)[:, 0:S]
        Frow = attS[0:NH, 0, 0:S]
        Frest = attS[0:NH, 1, 0:S]
        Flog = attP[0:NH, 0, :]
        pT2 = y[:, 0, 0:W]

        xg = nc.dram_tensor("xg", [TILES * P, D], F32, kind="Internal").ap()
        yg = nc.dram_tensor("yg", [TILES * P, D], F32, kind="Internal").ap()

        s_cbf, s_selin = sem("s_cbf"), sem("s_selin")
        s_grow, s_gT, s_gcol, s_sgin, s_wf = sem("s_grow"), sem("s_gT"), sem("s_gcol"), sem("s_sgin"), sem("s_wf")
        s_hi, s_lo, s_un = sem("s_hi"), sem("s_lo"), sem("s_un")
        s_const, s_ident, s_zero, s_xgz = sem("s_const"), sem("s_ident"), sem("s_zero"), sem("s_xgz")
        s_in = sems("s_in", MT)
        s_ring = sems("s_ring", 2)
        s_mixin, s_pin, s_pg = sem("s_mixin"), sems("s_pin"), sems("s_pg")
        s_ss, s_rr = sem("s_ss"), sem("s_rr")
        s_t, s_tD, s_tA = sem("s_t"), sem("s_tD"), sem("s_tA")
        s_m, s_mD, s_mA = sem("s_m"), sem("s_mD"), sem("s_mA")
        s_z, s_pr, s_w, s_pt, s_ptv, s_o, s_ov = (sems(n) for n in ("s_z", "s_pr", "s_w", "s_pt", "s_ptv", "s_o", "s_ov"))
        s_qn, s_hs, s_hr = sems("s_qn"), sems("s_hs"), sems("s_hr")
        s_y, s_mixd, s_sg, s_sgT = sems("s_y"), sem("s_mixd"), sem("s_sg"), sem("s_sgT")
        s_f, s_fa, s_fl, s_fc, s_fp, s_fx = (sem(n) for n in ("s_f", "s_fa", "s_fl", "s_fc", "s_fp", "s_fx"))
        s_fourth = sem("s_fourth")
        s_last = sem("s_last")
        s_third = sem("s_third")
        s_xh, s_ehi, s_elo, s_eun = (sems(n) for n in ("s_xh", "s_ehi", "s_elo", "s_eun"))
        s_lgx = sem("s_lgx")
        s_oh, s_wn = sems("s_oh"), sem("s_wn")
        s_pl, s_plv, s_pm, s_ph = sem("s_pl"), sem("s_plv"), sem("s_pm"), sem("s_ph")
        s_xn, s_lg = sems("s_xn"), sems("s_lg")
        s_lgv, s_ex, s_sel, s_rank, s_pos = (sem(n) for n in ("s_lgv", "s_ex", "s_sel", "s_rank", "s_pos"))
        s_sc, s_xl, s_gu, s_wd = sems("s_sc"), [sems(f"s_xl{l}_", 2) for l in range(2)], [sems(f"s_gu{l}_", 2) for l in range(2)], [sems(f"s_wd{l}_", 2) for l in range(2)]
        s_tx, s_xv, s_g, s_sil, s_act, s_at, s_atv = (sems(n) for n in ("s_tx", "s_xv", "s_g", "s_sil", "s_act", "s_at", "s_atv"))
        s_dn, s_yD, s_yA, s_st = sems("s_dn"), sems("s_yD"), sems("s_yA"), [sems(f"s_st{l}_", 2) for l in range(2)]
        s_ovi, s_end = sem("s_ovi"), sem("s_end")
        s_gam = [sems(f"s_ga{j}_", MT) for j in range(2)]
        s_cmb, s_e, s_pse, s_gt, s_h = sems("s_cmb"), sem("s_e"), sems("s_pse"), sems("s_gt"), sems("s_h")
        s_dve, s_act_, s_pool = sem("s_dve"), sem("s_actchain"), sem("s_poolchain")
        s_out = sem("s_out")

        def cols(w, c, k=KD):
            return w[:, c * 512:(c + 1) * 512].rearrange("(k p) n -> p k n", p=P)

        wi, wo = a["even_w_in"][0], a["even_w_out"][0]
        oi, oo = a["odd_w_in"][0], a["odd_w_out"][0]
        XD0 = 3 * W + NH
        chunks = [cols(wi, c) for c in (2, 3, 4, 1, 0)] + [cols(wo, 0), cols(wo, 1)]
        first = [0]
        ffn = []
        for l in range(DEPTH):
            ffn.append(len(chunks))
            chunks += [None, cols(a["ple_w_gate"][l], 0), cols(a["ple_w_gate"][l], 1)]
            if l == 0:
                first.append(len(chunks))
                chunks += [cols(oi, 0), cols(oi, 1), cols(oi, 2), oi[:, XD0:XD0 + W].rearrange("(k p) n -> p k n", p=P)]
                chunks += [cols(oo, 0), cols(oo, 1)]
        NIN = [5, 4]

        def chunk_ready(engine, c):
            engine.wait_ge(s_ring[c % 2], 16 * ((c + 1) // 2))

        TM, TF, TY, TP, TQ = range(5)
        GI, GO, GE, GG = range(4)
        SM, SF, SE, SP_ = range(4)

        before_t, before_tm, before_m, before_mD, before_mA = {}, {}, {}, {}, {}
        nt = ntm = nm = nD = nA = 0
        for l in range(DEPTH):
            for which, steps, both in ((TM, KD, 1), (TQ, 8, 0), (TY, [4, 0][l], 1), (TF, KD, 0), (TP, KD, 1)):
                before_t[l, which], before_tm[l, which] = nt, ntm
                nt += steps
                ntm += steps if both else steps // 2
            for which, groups, byD, byA in ((GI, MT * NIN[l], [6, 8][l], [14, 8][l]),
                                            (GO, 2 * MT, 2 * MT, 0), (GE, 2 * MT, 0, 2 * MT), (GG, 2 * MT, 0, 0)):
                before_m[l, which], before_mD[l, which], before_mA[l, which] = nm, nD, nA
                nm, nD, nA = nm + groups, nD + byD, nA + byA

        def turn_bank(l, which, j):
            return bank[5 if which == TY else (j + 4) % 8 if (l, which) == (0, TQ) else j][:, :]

        def steps_turned(l, which, n):
            return before_t[l, which] + n

        def steps_moved(l, which, n):
            return before_tm[l, which] + n

        def groups_done(l, which, n):
            return before_m[l, which] + n

        def movedD(l, which, n):
            return before_mD[l, which] + n

        def movedA(l, which, n):
            return before_mA[l, which] + n

        def by_vector(l, c, m):
            return m % 2 == 0 and not (l == 0 and c >= 3)

        def in_moved(l, c):
            n = sum(by_vector(l, k, m) for k in range(c) for m in range(MT))
            return movedD(l, GI, n), movedA(l, GI, MT * c - n)

        last_group = []
        for l in range(DEPTH):
            last_group += [groups_done(l, GI, MT * (j + 1)) for j in range(NIN[l])]
            last_group += [groups_done(l, which, n * MT) for which, n in ((GO, 1), (GO, 2), (GE, 2), (GG, 1), (GG, 2))]

        split = [c for c in range(len(chunks)) if chunks[c] is not None]

        def unit(c, j):
            return 4 * split.index(c) + j

        def weights(l, v, n):
            third = y[:, 0, W:] if l == 0 else attS[:, 0, 0:512]
            return attB[:, v % 3, 0:n] if v % 3 < 2 else third[:, 0:n]

        def place(e, p, i):
            if isinstance(e, int) and e < 4:
                return e, 1
            return p, i

        def place_down(e, p, i):
            if isinstance(e, int) and e < 3:
                return e, 1
            return 1 - p, i + p

        def gate_up_at(l, b):
            return gu[:, b, :, :] if b < 2 else ring[:, (ffn[l] + 1) % 2, :, :] if b == 2 else y[:, :, :].rearrange("p m (k n) -> p (m k) n", n=512)

        def gate_up_low_at(l, b):
            return glo[:, b, :, :] if b < 2 else ring_low[:, (ffn[l] + 1) % 2, :, :] if b == 2 else y_low[:, :, :]

        def down_at(l, b):
            return wd[:, b, :, :] if b < 2 else ring[:, ffn[l] % 2, 4:8, :].rearrange("p (f n) c -> p f (n c)", f=DE // P)

        def raw(c, j):
            return ring[:, c % 2, 2 * j:2 * j + 2, :]

        block = ctx.enter_context(nc.Block())

        @block.sync
        def _(sp):
            def chunk(c):
                if c >= 2 and c - 2 in split:
                    sp.wait_ge(s_lo, unit(c - 2, 3) + 1)
                elif c >= 2:
                    sp.wait_ge(s_m, last_group[c - 2])
                if chunks[c] is None:
                    l = ffn.index(c)
                    sp.dma_start(ring[:, c % 2, 0:2 * KP, :].rearrange("p (k n) c -> p k (n c)", k=KP),
                                 a["ple_w_proj"][l].rearrange("(k p) n -> p k n", p=P)).then_inc(s_ring[c % 2], 16)
                else:
                    sp.dma_start(ring[:, c % 2, :, :], chunks[c]).then_inc(s_ring[c % 2], 16)

            def load_gu(l, e, p):
                sp.dma_start(gu[:, p, :, 0:DE], a["expert_w_gate"][l, e].rearrange("(k p) f -> p k f", p=P)).then_inc(s_gu[l][p], 16)
                sp.dma_start(gu[:, p, :, DE:], a["expert_w_up"][l, e].rearrange("(k p) f -> p k f", p=P)).then_inc(s_gu[l][p], 16)

            def load_wd(l, e, p):
                sp.dma_start(wd[:, p, :, :], a["expert_w_down"][l, e].rearrange("(k p) n -> p k n", p=P)).then_inc(s_wd[l][p], 16)

            def zero(t0, t1):
                sp.dma_start(xg[t0 * P:t1 * P, :].rearrange("(t p) d -> p t d", p=P),
                             zeros.unsqueeze(1).to_broadcast([P, t1 - t0, D])).then_inc(s_xgz, 16)

            for m in range(MT):
                sp.dma_start(h[:, m, :], a["x"][0, m * P:(m + 1) * P, :]).then_inc(s_in[m], 16)
            sp.wait_ge(s_in[1], 16)
            for j in range(4):
                sp.wait_ge(s_in[j], 16)
                sp.dma_start(raw(0, j), chunks[0][:, 2 * j:2 * j + 2, :]).then_inc(s_in[j], 16)
            sp.wait_ge(s_sgin, 16)
            chunk(1)
            sp.wait_ge(s_zero, 1)
            for l in range(DEPTH):
                if l == 0:
                    for c in range(2, 4):
                        zero(6 * (c - 2), 6 * (c - 1))
                        chunk(c)
                    zero(12, 17)
                    sp.dma_start(yg[NE * P:, :].rearrange("(t p) d -> p t d", p=P),
                                 zeros.unsqueeze(1).to_broadcast([P, OVT, D])).then_inc(s_xgz, 16)
                    zero(17, TILES)
                for c in range(4 if l == 0 else first[l] + 2, ffn[l]):
                    chunk(c)
                if l == 0:
                    sp.wait_ge(s_t, steps_turned(0, TY, 4))
                sp.wait_ge(s_ov[l], NH // 2)
                sp.wait_ge(*((s_pm, 4) if l == 0 else (s_pl, 4)))
                sp.dma_start(frow, a["norm_ffn"][l].partition_broadcast(P)).then_inc(s_pg[l], 16)
                sp.dma_start(pgain, a["ple_norm"][l].partition_broadcast(P)).then_inc(s_pg[l], 16)
                sp.dma_start(pin, a["p"][l, 0].rearrange("(m p) n -> p m n", p=P)).then_inc(s_pin[l], 16)
                chunk(ffn[l])
                sp.wait_ge(s_lo, unit(ffn[l] - 1, 3) + 1)
                for half, name in enumerate(("expert_w_gate", "expert_w_up")):
                    sp.dma_start(gate_up_at(l, 2)[:, :, half * DE:(half + 1) * DE], a[name][l, 2].rearrange("(k p) f -> p k f", p=P))\
                        .then_inc(s_third, 16)
                sp.dma_start(down_at(l, 2), a["expert_w_down"][l, 2].rearrange("(k p) n -> p k n", p=P)).then_inc(s_third, 16)
                sp.wait_ge(s_m, last_group[ffn[l] - 1])
                for e in range(2):
                    load_gu(l, e, e)
                    load_wd(l, e, e)
                sp.wait_ge(s_sc[l], 16 * 2 * MT)
                for e in range(2):
                    sp.dma_start(xs[e], xg[e * P:(e + 1) * P, :]).then_inc(s_xl[l][e], 16)

                def load_rows(t, p):
                    sp.wait_ge(s_tx[l], 2 * (t - 1))
                    sp.dma_start(xs[p], xg.rearrange("(t p) d -> t p d", p=P)[bass.ds(t, 1), :, :].rearrange("t p d -> p (t d)"))\
                        .then_inc(s_xl[l][p], 16)

                def load(t, p, expert):
                    load_rows(t, p)
                    sp.wait_ge(s_g[l], t - 1)
                    sp.dma_start(gu[:, p, :, 0:DE], a["expert_w_gate"][l, bass.ds(expert, 1)].rearrange("e (k p) f -> p (e k) f", p=P))\
                        .then_inc(s_gu[l][p], 16)
                    sp.dma_start(gu[:, p, :, DE:], a["expert_w_up"][l, bass.ds(expert, 1)].rearrange("e (k p) f -> p (e k) f", p=P))\
                        .then_inc(s_gu[l][p], 16)

                for half, name in enumerate(("expert_w_gate", "expert_w_up")):
                    sp.dma_start(gate_up_at(l, 3)[:, :, half * DE:(half + 1) * DE], a[name][l, 3].rearrange("(k p) f -> p k f", p=P))\
                        .then_inc(s_fourth, 16)
                for e in (4, 5):
                    load_rows(e - 2, e % 2)
                    sp.wait_ge(s_g[l], e - 3)
                    load_gu(l, e, e % 2)
                load_rows(4, 0)
                load_rows(5, 1)
                with sp.Fori(3, NE // 2) as i:
                    for p in range(2):
                        load(2 * i + p, p, 2 * i + p)
                sp.wait_ge(s_ovi, l + 1)
                n = sp.value_load(ovi[0:1, OVT:OVT + 1], min_val=0, max_val=OVT // 2)
                with sp.If(n > 0):
                    with sp.Fori(0, n) as i:
                        for p in range(2):
                            expert = sp.value_load(ovi[0:1, bass.ds(2 * i + p, 1)], min_val=0, max_val=NE - 1)
                            load(2 * i + (p + NE), p, expert)
                sp.wait_ge(s_last, l + 1)
                chunk(ffn[l] + 1)
                sp.wait_ge(s_cmb[l], MT)
                chunk(ffn[l] + 2)
                if l == 0:
                    for c in range(first[1], first[1] + 2):
                        chunk(c)
                    sp.wait_ge(s_h[0], 2 * MT)
                    sp.dma_start(mixw[:, :], a["c_bands"].rearrange("p f g t -> p (f g t)")).then_inc(s_mixin, 16)
                    sp.dma_start(poolw, a["pool_w"][0].rearrange("g c d -> c g d")).then_inc(s_mixin, 16)

        @block.scalar
        def _(sc):
            A = nc.scalar
            chain = [0]

            def link(ins):
                chain[0] += 1
                ins.then_inc(s_act_, 1)
                sc.wait_ge(s_act_, chain[0])

            sc.dma_start(cf[:, :, :], a["c_f"]).then_inc(s_ident, 16)
            for rows_, src in ((slice(0, 16), a["norm_mix"].rearrange("l (k p) -> (l k) p", p=P)),
                               (slice(16, 32), a["norm_ffn"].rearrange("l (k p) -> (l k) p", p=P)),
                               (slice(32, 40), a["sgu_b"][0]),
                               (slice(40, 44), a["pool_scale"][0].rearrange("(g p) -> g p", p=P))):
                sc.dma_start(grow[rows_, :], src).then_inc(s_grow, 16)
            for b, name in enumerate(("q_norm", "k_norm")):
                sc.dma_start(grow[44 + b:45 + b, :].rearrange("p (a d) -> p a d", a=2),
                             a[name].unsqueeze(1).to_broadcast([1, 2, HD])).then_inc(s_grow, 16)
            sc.dma_start(sgw, a["sgu_w"][0].rearrange("h t s -> t h s")).then_inc(s_sgin, 16)

            def load_constants():
                with nc.allow_non_contiguous_dma(reason="narrow weights"):
                    for dst, src in ((small[:, :], a["c_small"]),
                                     (wf[:, :, :], oi[:, 3 * W:3 * W + NH].rearrange("(k p) n -> p k n", p=P)),
                                     (fb[:, :], a["forget_bias"][0].partition_broadcast(P)),
                                     (wr[:, 0, :, 0:4], a["router_group_w"][0].rearrange("(k p) n -> p k n", p=P)),
                                     (wr[:, 1, :, 0:4], a["router_group_w"][1].rearrange("(k p) n -> p k n", p=P)),
                                     (wr[:, 0, :, 4:20], a["router_expert_w"][0].rearrange("(k p) n -> p k n", p=P)),
                                     (wr[:, 1, :, 4:20], a["router_expert_w"][1].rearrange("(k p) n -> p k n", p=P)),
                                     (rb[:, 0, 0:4], a["router_group_b"][0].partition_broadcast(P)),
                                     (rb[:, 1, 0:4], a["router_group_b"][1].partition_broadcast(P)),
                                     (rb[:, 0, 4:20], a["router_expert_b"][0].partition_broadcast(P)),
                                     (rb[:, 1, 4:20], a["router_expert_b"][1].partition_broadcast(P)),
                                     (mixg[:, :], a["sgu_norm"][0].rearrange("h d -> (h d)").partition_broadcast(P))):
                        sc.dma_start(dst, src).then_inc(s_const, 16)

            def high(c, j):
                if c == 0:
                    sc.wait_ge(s_in[j], 32)
                elif j == 0:
                    chunk_ready(sc, c)
                q = split.index(c)
                if q and j < 3:
                    sc.wait_ge(s_un, 3 * (q - 1) + j + 1)
                elif q:
                    sc.wait_ge(s_m, last_group[split[q - 1]])
                A.copy(wh[:, j, :, :], raw(c, j)).then_inc(s_hi, 1)

            def highs(c):
                for j in range(4):
                    high(c, j)

            def turn_high(l, which, steps, put):
                for j in steps:
                    sc.wait_ge(s_t, steps_turned(l, which, j + 1))
                    put(j).then_inc(s_tA, 1)

            def stat(l, which, src, dst):
                done = MT * (4 * l + which) + dst
                if done:
                    sc.wait_ge(s_ss, done)
                A.activation(junk, src, ACT.Square, accum_out=ss[:, l, which, dst:dst + 1]).then_inc(s_ss, 1)

            def turn(l, which, n, put):
                for j in range(1, n, 2):
                    sc.wait_ge(s_t, steps_turned(l, which, j + 1))
                    put(j).then_inc(s_tA, 1)

            def output(g):
                c, m = g // MT, g % MT
                sc.dma_start(out[0, m * P:(m + 1) * P, c * 512:(c + 1) * 512], h[:, m, c * 512:(c + 1) * 512]).then_inc(s_out, 16)

            for l in range(DEPTH):
                if l == 0:
                    sc.wait_ge(s_pool, 1)
                    A.mul(nb[:, 0:1], pw[:, 0:1], pw[:, 0:1])
                    sc.wait_ge(s_gcol, 1)
                for half in range(2):
                    turn_high(l, TM, range(4 * half, 4 * half + 4), lambda j: A.mul(xh[:, j, :], turn_bank(l, TM, j), gmix(l, j)))
                    if l == 0:
                        high(0, 2 * half)
                        high(0, 2 * half + 1)
                if l == 0:
                    load_constants()
                for m in range(MT):
                    if l == 0:
                        sc.wait_ge(s_in[m], 16)
                    else:
                        sc.wait_ge(s_h[0], MT + m + 1)
                    stat(l, SM, h[:, m, :], m)
                dst = [[Q, K, V, VA, U], [Q, K, V, y[:, :, W:]]][l]
                for c in range(NIN[l] + 1):
                    if l == 0 and c == 3:
                        sc.wait_ge(s_const, 16 * 12)
                        A.copy(wfh[:, :, :], wf[:, :, :]).then_inc(s_wf, 1)
                    if c and c < NIN[l]:
                        highs(first[l] + c)
                    elif c:
                        highs(ffn[l] - 2)
                    if c == 0:
                        sc.wait_ge(s_rr, 4 * l + SM + 1)
                        continue
                    k = c - 1
                    if l == 0 and k == 4:
                        sc.wait_ge(s_xgz, 16 * 5)
                    for m in range(MT):
                        if not by_vector(l, k, m):
                            sc.wait_ge(s_m, groups_done(l, GI, MT * k + m + 1))
                            x = dst[k][:, m, :]
                            b = bank[4 * (k % 2) + m][:, :]
                            r = rr[:, l, SM, m:m + 1]
                            if l == 0 and k >= 3:
                                A.activation(x, b, ACT.Gelu_apprx_tanh, scale=r).then_inc(s_mA, 1)
                            else:
                                A.mul(x, b, r).then_inc(s_mA, 1)
                    if l == 1 and k == 0:
                        sc.wait_ge(s_f, 1)
                        link(A.activation(lf[:, 1, :, :], lf[:, 0, :, :], ACT.Abs))
                        link(A.activation(lf[:, 1, :, :], lf[:, 1, :, :], ACT.Exp, scale=-1.0))
                        A.activation(lf[:, 2, :, :], lf[:, 1, :, :], ACT.Ln, bias=1.0).then_inc(s_fl, 1)
                if l == 1:
                    turn(1, TQ, 8, lambda j: A.mul(qT[:, j, :] if j < 4 else kT[:, j - 4, :], turn_bank(1, TQ, j), qkg(j // 4)))
                else:
                    sc.wait_ge(s_hs[0], 1)
                    turn(0, TQ, 8, lambda j: A.copy(qT[:, j, :] if j < 4 else kT[:, j - 4, :], turn_bank(0, TQ, j)))
                for v in range(4 * NH + 5):
                    if 3 <= v < 4 * NH + 3:
                        u = v - 3
                        n = (u % 4 + 1) * P
                        sc.wait_ge(s_pt[l], u + 1)
                        A.copy(attP[:, u % 2, 0:n], bank[2 + u % 2][:, 0:n]).then_inc(s_ptv[l], 1)
                    if v < 4 * NH:
                        n = (v % 4 + 1) * P
                        sc.wait_ge(s_z[l], v + 1)
                        if v >= 3:
                            sc.wait_ge(s_pt[l], v - 2)
                        if l == 0:
                            if v >= 2:
                                sc.wait_ge(s_w[0], v - 1)
                            A.activation(attE[:, v % 2, 512 - n:512], bank[v % 2][:, 0:n], ACT.Sigmoid, scale=-SCALE)
                            A.activation(weights(l, v, n), bank[v % 2][:, 0:n], ACT.Sigmoid, scale=SCALE).then_inc(s_pr[0], 1)
                        else:
                            sc.wait_ge(s_w[1], v + 1)
                            A.activation(weights(l, v, n), bank[v % 2][:, 0:n], ACT.Exp, scale=SCALE,
                                         bias=nb[:, v:v + 1], accum_out=rs[:, v:v + 1]).then_inc(s_pr[1], 1)
                    if l == 0 and v % 8 == 7 and v <= 31:
                        j = (v - 7) // 8
                        sc.wait_ge(s_t, steps_turned(0, TY, j + 1))
                        A.copy(xh[:, j, :], turn_bank(0, TY, j)).then_inc(s_tA, 1)
                    if l == 1 and v >= 7 and v % 8 == 7:
                        g = (v - 7) // 8
                        sc.wait_ge(s_pm, 4 + g + 1)
                        A.mul(xh[:, 4 + g, :], bank[5][:, :], pscale(g)).then_inc(s_ph, 1)
                    if v >= 12 and v % 8 == 4:
                        pair = (v - 12) // 8
                        sc.wait_ge(s_o[l], pair + 1)
                        A.copy(xh[:, [4, 0][l] + pair, :], bank[6 + pair % 2][:, :]).then_inc(s_oh[l], 1)
                highs(ffn[l] - 1)
                turn(l, TF, KD, lambda j: A.mul(xT[:, j, :], turn_bank(l, TF, j), gffn(l, j)))
                for m in range(MT):
                    sc.wait_ge(s_mD, movedD(l, GO, MT + m + 1))
                    stat(l, SF, h[:, m, :], m)
                sc.wait_ge(s_e, l + 1)
                for k in range(KP):
                    A.copy(pT[:, k, :], bank[6 + k][:, :]).then_inc(s_pse[l], 1)
                for g in range(2 * MT):
                    m, c = g // 2, g % 2
                    if g == 2:
                        sc.wait_ge(s_lgv, l + 1)
                        A.activation(exps[:, 1, :, :], exps[:, 0, :, :], ACT.Exp).then_inc(s_ex, 1)
                    sc.wait_ge(s_m, groups_done(l, GE, g + 1))
                    A.copy(E[:, m, c * 512:(c + 1) * 512], bank[2 + g % 4][:, :]).then_inc(s_mA, 1)
                    if c:
                        sc.wait_ge(s_mA, movedA(l, GE, g + 1))
                        stat(l, SE, E[:, m, :], m)

                def silu(e):
                    sc.wait_ge(s_g[l], e + 1)
                    A.activation(sil, bank[2][:, 0:DE], ACT.Silu).then_inc(s_sil[l], 1)

                def rows_high(e):
                    for b in range(2):
                        sc.wait_ge(s_tx[l], 2 * e + b + 1)
                        A.copy(xgh[:, 4 * b:4 * b + 4, :].rearrange("p k n -> p (k n)"), bank[b][:, :]).then_inc(s_xh[l], 1)

                def split_high(e, p, i):
                    b, loads = place(e, p, i)
                    if b == 2:
                        sc.wait_ge(s_third, 48 * (l + 1))
                    elif b == 3:
                        sc.wait_ge(s_fourth, 32 * (l + 1))
                    else:
                        sc.wait_ge(s_gu[l][b], 32 * loads)
                    for j in range(4):
                        if not (isinstance(e, int) and e == 0):
                            if j < 3:
                                sc.wait_ge(s_eun[l], 3 * e + (j - 2))
                            else:
                                sc.wait_ge(s_g[l], e)
                        A.copy(ghi[:, 2 * j:2 * j + 2, :], gate_up_at(l, b)[:, 2 * j:2 * j + 2, :]).then_inc(s_ehi[l], 1)

                def act_moved(e):
                    sc.wait_ge(s_at[l], e + 1)
                    A.copy(actT, bank[3][:, 0:DE]).then_inc(s_atv[l], 1)

                def result(e, p):
                    sc.wait_ge(s_dn[l], 2 * e + 2)
                    A.copy(ys[p][:, 512:D], bank[5][:, :]).then_inc(s_yA[l], 1)

                def store(e, p, done):
                    sc.wait_ge(s_yD[l], e + 1)
                    sc.wait_ge(s_yA[l], e + 1)
                    sc.dma_start(yg.rearrange("(t p) d -> t p d", p=P)[bass.ds(e, 1), :, :].rearrange("t p d -> p (t d)"), ys[p])\
                        .then_inc(done, 16)

                def stage(e, p, i, stored, expert, b):
                    silu(e - 1)
                    rows_high(e)
                    split_high(e, p, i)
                    if stored:
                        sc.wait_ge(s_st[l][p], 16 * (i - 1))
                    result(e - 2, p)
                    if expert is not None:
                        sc.dma_start(wd[:, b, :, :], a["expert_w_down"][l, bass.ds(expert, 1)].rearrange("e (k p) n -> p (e k) n", p=P))\
                            .then_inc(s_wd[l][b], 16)
                    act_moved(e - 1)
                    store(e - 2, p, s_st[l][p])

                split_high(0, 0, 0)
                rows_high(0)
                silu(0)
                rows_high(1)
                split_high(1, 1, 0)
                act_moved(0)
                stage(2, 0, 1, False, 3, 0)
                stage(3, 1, 1, False, 4, 1)
                stage(4, 0, 2, True, None, None)
                stage(5, 1, 2, True, 5, 0)
                with sc.Fori(3, NE // 2) as i:
                    for p in range(2):
                        stage(2 * i + p, p, i, True, 2 * i + p, 1 - p)
                sc.wait_ge(s_ovi, l + 1)
                n = sc.value_load(ovi[0:1, OVT:OVT + 1], min_val=0, max_val=OVT // 2)
                with sc.If(n > 0):
                    with sc.Fori(0, n) as i:
                        for p in range(2):
                            expert = sc.value_load(ovi[0:1, bass.ds(2 * i + p, 1)], min_val=0, max_val=NE - 1)
                            stage(2 * i + (p + NE), p, i + NE // 2, True, expert, 1 - p)
                sc.sem_inc(s_last, 1)
                sc.wait_ge(s_st[l][0], 16 * n + 16 * (NE // 2 - 1))
                silu(2 * n + (NE - 1))
                result(2 * n + (NE - 2), 0)
                store(2 * n + (NE - 2), 0, s_st[l][0])
                act_moved(2 * n + (NE - 1))
                sc.wait_ge(s_st[l][1], 16 * n + 16 * (NE // 2 - 1))
                result(2 * n + (NE - 1), 1)
                store(2 * n + (NE - 1), 1, s_st[l][1])
                sc.wait_ge(s_st[l][0], 16 * n + 16 * NE // 2)
                sc.wait_ge(s_st[l][1], 16 * n + 16 * NE // 2)
                sc.sem_inc(s_end, 1)
                highs(ffn[l] + 1)
                for m in range(MT):
                    sc.wait_ge(s_cmb[l], m + 1)
                    if m == MT - 1:
                        turn_high(l, TP, range(KD), lambda j: A.copy(xh[:, j, :], turn_bank(l, TP, j)))
                    stat(l, SP_, h[:, m, :], m)
                highs(ffn[l] + 2)
                sc.wait_ge(s_rr, 4 * l + SP_ + 1)
                for g in range(2 * MT):
                    c, m = g // MT, g % MT
                    if l == 0 and g == MT:
                        for j in range(3):
                            high(first[1], j)
                    sc.wait_ge(s_m, groups_done(l, GG, g + 1))
                    if g >= 2:
                        sc.wait_ge(s_h[l], g - 1)
                    A.activation(gate[:, g % 2, :], bank[4 * c + m][:, :], ACT.Sigmoid, scale=rr[:, l, SP_, m:m + 1])\
                        .then_inc(s_gt[l], 1)
                    if l == 1 and g:
                        sc.wait_ge(s_h[1], g)
                        output(g - 1)
                if l == 0:
                    high(first[1], 3)
            sc.wait_ge(s_h[1], 2 * MT)
            output(2 * MT - 1)
            sc.wait_ge(s_out, 16 * 2 * MT)

        @block.gpsimd
        def _(pool):
            G = nc.gpsimd
            chain = [0]

            def link(ins):
                chain[0] += 1
                ins.then_inc(s_pool, 1)
                pool.wait_ge(s_pool, chain[0])

            pool.dma_start(cbf[:, :, :], a["c_bf"]).then_inc(s_cbf, 16)
            G.memset(zeros, 0.0).then_inc(s_zero, 1)
            link(G.memset(pw[:, :], -0.5))

            def root(dst, src, n, width, done):
                link(G.tensor_scalar(dst, src, 1.0 / n, EPS, ALU.mult, ALU.add))
                G.tensor_tensor(dst, dst, pw[:, 0:width], ALU.pow).then_inc(done, 1)

            def stat(l, which):
                pool.wait_ge(s_ss, MT * (4 * l + which + 1))
                root(rr[:, l, which, :], ss[:, l, which, :], D, MT, s_rr)

            for l in range(DEPTH):
                stat(l, SM)
                n = [1, 2][l]
                pool.wait_ge(s_hs[l], n)
                root(hrr[:, 0:n, :].rearrange("p a b -> p (a b)"), hss[:, 0:n, :].rearrange("p a b -> p (a b)"),
                     HD, n * MT * NH, s_hr[l])
                stat(l, SF)
                if l == 0:
                    pool.wait_ge(s_xgz, 16 * 5)
                pool.wait_ge(s_pos, l + 1)
                for m in range(MT):
                    pool.wait_ge(s_xn[l], m + 1)
                    for j in range(2):
                        G.indirect_dma_start(xg, bass.IndirectOffsetOnAxis(posi[:, j, m:m + 1], 0), y[:, m, :], None)\
                            .then_inc(s_sc[l], 16)
                stat(l, SE)
                pool.wait_ge(s_end, l + 1)
                pool.wait_ge(s_sc[l], 16 * 2 * MT)
                for m in range(MT):
                    for j, dst in enumerate((y, G2)):
                        G.indirect_dma_start(dst[:, m, :], None, yg, bass.IndirectOffsetOnAxis(posi[:, j, m:m + 1], 0))\
                            .then_inc(s_gam[j][m], 16)
                stat(l, SP_)
                if l == 0:
                    pool.wait_ge(s_h[0], 2 * MT)
                    pool.dma_start(self_, a["c_sel"]).then_inc(s_selin, 16)

        @block.vector
        def _(dve):
            Ve = nc.vector
            chain = [0]

            def link(ins):
                chain[0] += 1
                ins.then_inc(s_dve, 1)
                dve.wait_ge(s_dve, chain[0])

            def turn(l, which, n, put):
                for j in range(0, n, 2):
                    dve.wait_ge(s_t, steps_turned(l, which, j + 1))
                    put(j).then_inc(s_tD, 1)

            def over(x, n):
                return x.unsqueeze(2).to_broadcast([P, MT, n])

            def first_max(values, n, top, mask, t):
                link(Ve.tensor_reduce(top, values, AX, ALU.max))
                link(Ve.tensor_tensor(t[0], values, over(top, n), ALU.is_ge))
                link(Ve.tensor_tensor(t[1], t[0], small[:, NE - n:NE].unsqueeze(1).to_broadcast([P, MT, n]), ALU.mult))
                link(Ve.tensor_reduce(mxs[:, 7, :], t[1], AX, ALU.max))
                link(Ve.tensor_tensor(mask, t[1], over(mxs[:, 7, :], n), ALU.is_equal))

            def low(c, j):
                dve.wait_ge(s_hi, unit(c, j) + 1)
                Ve.tensor_tensor(wl[:, j, :, :], raw(c, j), f32(wh[:, j, :, :]), ALU.subtract).then_inc(s_lo, 1)

            def lows(c):
                for j in range(4):
                    low(c, j)

            def turn_low(l, which, steps, gain=None):
                for j in steps:
                    dve.wait_ge(s_tA, steps_moved(l, which, j + 1))
                    x, b = xl[:, j, :], turn_bank(l, which, j)
                    if gain:
                        ins = Ve.scalar_tensor_tensor(x, b, gain(j), f32(xh[:, j, :]), ALU.mult, ALU.subtract)
                    else:
                        ins = Ve.tensor_tensor(x, b, f32(xh[:, j, :]), ALU.subtract)
                    ins.then_inc(s_tD, 1)

            dve.wait_ge(s_gT, 1)
            Ve.tensor_copy(gcol[:, :], bank[7][:, 0:46]).then_inc(s_gcol, 1)
            dve.wait_ge(s_gcol, 1)
            for l in range(DEPTH):
                for half in range(2):
                    turn_low(l, TM, range(4 * half, 4 * half + 4), lambda j: gmix(l, j))
                    if l == 0:
                        low(0, 2 * half)
                        low(0, 2 * half + 1)
                if l == 0:
                    dve.wait_ge(s_ident, 16)
                    dve.wait_ge(s_sgin, 16)
                    Ve.tensor_tensor(sgw, sgw, tril.unsqueeze(1).to_broadcast([P, NH, P]), ALU.mult).then_inc(s_sg, 1)
                heads = lambda x: x.rearrange("p m (h d) -> p (m h) d", d=HD)
                dve.wait_ge(s_rr, 4 * l + SM + 1)
                sq = attB[:, :, :].rearrange("p a n -> p (a n)")
                dst = [[Q, K, V, VA, U], [Q, K, V, y[:, :, W:]]][l]
                for c in range(NIN[l] + 1):
                    if l == 0 and c == 4:
                        dve.wait_ge(s_wf, 1)
                        Ve.tensor_tensor(wfl[:, :, :], wf[:, :, :], f32(wfh[:, :, :]), ALU.subtract).then_inc(s_wf, 1)
                    if c == 1:
                        for j in range(3):
                            low(first[l] + c, j)
                        if l == 0:
                            for b in range(2):
                                dve.wait_ge(s_sgT, b + 1)
                                Ve.tensor_copy(sguT[:, 4 * b:4 * b + 4, :].rearrange("p h t -> p (h t)"), bank[4 + b][:, :]).then_inc(s_mixd, 1)
                        else:
                            dve.wait_ge(s_fa, 1)
                            Ve.tensor_copy(Flog, bank[7][0:NH, :]).then_inc(s_fx, 1)
                            dve.wait_ge(s_fa, 2)
                            link(Ve.tensor_tensor(lf[:, 3, :, :], bank[6][:, 0:MT * NH].rearrange("p (m h) -> p m h", h=NH),
                                                  over(rr[:, 1, SM, :], NH), ALU.mult))
                            Ve.tensor_tensor(lf[:, 0, :, :], lf[:, 3, :, :], fb[:, :].unsqueeze(1).to_broadcast([P, MT, NH]), ALU.add)\
                                .then_inc(s_f, 1)
                        low(first[l] + c, 3)
                    elif l == 1 and c == 3:
                        for j in range(3):
                            low(first[l] + c, j)
                        dve.wait_ge(s_fa, 3)
                        Ve.tensor_copy(Frow, bank[7][0:NH, :]).then_inc(s_fx, 1)
                        dve.wait_ge(s_fx, 2)
                        low(first[l] + c, 3)
                    elif c and c < NIN[l]:
                        lows(first[l] + c)
                    elif l == 0 and c:
                        square = rows(qkT[:, 0:MT * W])
                        dve.wait_ge(s_mA, in_moved(0, 4)[1])
                        link(Ve.tensor_tensor(square, VA, VA, ALU.mult))
                        Ve.tensor_reduce(hss[:, 0, :], heads(square), AX, ALU.add).then_inc(s_hs[0], 1)
                        for j in range(2):
                            low(ffn[0] - 2, j)
                        dve.wait_ge(s_hr[0], 1)
                        link(Ve.tensor_tensor(heads(VA), heads(VA), hrr[:, 0, :].unsqueeze(2).to_broadcast([P, MT * NH, HD]), ALU.mult))
                        low(ffn[0] - 2, 2)
                        Ve.tensor_tensor(VA, VA, mixg[:, :].unsqueeze(1).to_broadcast([P, MT, W]), ALU.mult).then_inc(s_qn[0], 1)
                        low(ffn[0] - 2, 3)
                    elif c:
                        lows(ffn[l] - 2)
                    if l == 1 and c == 2:
                        dve.wait_ge(s_fl, 1)
                        Ve.scalar_tensor_tensor(lf[:, 3, :, :], lf[:, 0, :, :], 0.0, lf[:, 2, :, :], ALU.min, ALU.subtract).then_inc(s_fc, 1)
                    if c == 0:
                        continue
                    k = c - 1
                    for m in range(MT):
                        if by_vector(l, k, m):
                            dve.wait_ge(s_m, groups_done(l, GI, MT * k + m + 1))
                            Ve.tensor_scalar(dst[k][:, m, :], bank[4 * (k % 2) + m][:, :], rr[:, l, SM, m:m + 1], None, ALU.mult)\
                                .then_inc(s_mD, 1)
                    if l == 1 and k == 2:
                        link(Ve.memset(Fp[0:96, :], 0.0))
                        link(Ve.tensor_copy(Fp[0:NH, :], Frow))
                        link(Ve.tensor_tensor(Frest, Frow, Fp[0:NH, :], ALU.subtract))
                        link(Ve.tensor_copy(Fp[32:32 + NH, :], Frest))
                        link(Ve.tensor_copy(Frow, Fp[32:32 + NH, :]))
                        link(Ve.tensor_tensor(Frest, Frest, Frow, ALU.subtract))
                        Ve.tensor_copy(Fp[64:64 + NH, :], Frest).then_inc(s_fp, 1)
                        dve.wait_ge(s_hr[1], 1)
                        for b, x in enumerate((Q, K)):
                            Ve.tensor_tensor(heads(x), heads(x), hrr[:, b, :].unsqueeze(2).to_broadcast([P, MT * NH, HD]), ALU.mult)\
                                .then_inc(s_qn[1], 1)
                    if l == 1 and k == 1:
                        dve.wait_ge(s_mD, in_moved(1, 2)[0])
                        dve.wait_ge(s_mA, in_moved(1, 2)[1])
                        for b, x in enumerate((Q, K)):
                            if b:
                                dve.wait_ge(s_hs[1], 1)
                            for half in range(2):
                                part = x[:, 2 * half:2 * half + 2, :]
                                link(Ve.tensor_tensor(sq.rearrange("p (m n) -> p m n", m=2), part, part, ALU.mult))
                                ins = Ve.tensor_reduce(hss[:, b, 16 * half:16 * half + 16], sq.rearrange("p (a d) -> p a d", d=HD), AX, ALU.add)
                                if half == 0:
                                    link(ins)
                                else:
                                    ins.then_inc(s_hs[1], 1)
                if l == 0:
                    link(Ve.memset(attS[:, :, 512:513], 1.0))
                    turn(0, TQ, 8, lambda j: Ve.tensor_copy(qT[:, j, :] if j < 4 else kT[:, j - 4, :], turn_bank(0, TQ, j)))
                else:
                    turn(1, TQ, 8, lambda j: Ve.tensor_scalar(qT[:, j, :] if j < 4 else kT[:, j - 4, :], turn_bank(1, TQ, j),
                                                              qkg(j // 4), None, ALU.mult))

                def pair_out(pair):
                    dve.wait_ge(s_oh[l], pair + 1)
                    k = [4, 0][l] + pair
                    Ve.tensor_tensor(xl[:, k, :], bank[6 + pair % 2][:, :], f32(xh[:, k, :]), ALU.subtract).then_inc(s_ov[l], 1)

                for v in range(4 * NH + 6):
                    if v < 4 * NH:
                        n = (v % 4 + 1) * P
                        b = v % 2
                        if l == 0:
                            dve.wait_ge(s_pr[0], v + 1)
                            link(Ve.tensor_tensor_scan(attS[:, b, 512 - n:512][:, ::-1], attE[:, b, 512 - n:512][:, ::-1],
                                                       attE[:, b, 512 - n:512][:, ::-1], 1.0, ALU.mult, ALU.bypass))
                            Ve.tensor_tensor(weights(0, v, n), weights(0, v, n), attS[:, b, 513 - n:513], ALU.mult).then_inc(s_w[0], 1)
                        else:
                            dve.wait_ge(s_z[1], v + 1)
                            link(Ve.tensor_reduce(mx[:, v:v + 1], bank[b][:, 0:n], AX, ALU.max))
                            Ve.tensor_scalar(nb[:, v:v + 1], mx[:, v:v + 1], -SCALE, None, ALU.mult).then_inc(s_w[1], 1)
                    if l == 1 and 1 <= v <= 4 * NH:
                        u = v - 1
                        n = (u % 4 + 1) * P
                        dve.wait_ge(s_pr[1], u + 1)
                        link(Ve.reciprocal(ri[:, u:u + 1], rs[:, u:u + 1]))
                        Ve.tensor_scalar(weights(1, u, n), weights(1, u, n), ri[:, u:u + 1], None, ALU.mult).then_inc(s_wn, 1)
                    if v >= 13 and v % 8 == 5:
                        pair_out((v - 13) // 8)
                    if l == 0 and v % 8 == 3 and v <= 27:
                        g = (v - 3) // 8
                        dve.wait_ge(s_pm, g + 1)
                        dve.wait_ge(s_mA, in_moved(0, 5)[1])
                        for b in range(2):
                            hd = 2 * g + b
                            o = bank[4][:, 256 * b:256 * b + 256].rearrange("p (m d) -> p m d", d=HD)
                            u = U[:, :, hd * HD:(hd + 1) * HD]
                            Ve.scalar_tensor_tensor(u, o, sgb(hd), u, ALU.add, ALU.mult).then_inc(s_y[0], 1)
                    if l == 0 and v % 8 == 0 and 8 <= v <= 32:
                        j = (v - 8) // 8
                        dve.wait_ge(s_tA, steps_moved(0, TY, j + 1))
                        Ve.tensor_tensor(xl[:, j, :], turn_bank(0, TY, j), f32(xh[:, j, :]), ALU.subtract).then_inc(s_tD, 1)
                    if l == 1 and v >= 5 and v % 8 == 5 and v <= 29:
                        dve.wait_ge(s_pl, (v - 5) // 8 + 1)
                        Ve.tensor_copy(pT2, bank[4][:, :]).then_inc(s_plv, 1)
                    if l == 1 and v >= 8 and v % 8 == 0:
                        g = (v - 8) // 8
                        dve.wait_ge(s_ph, g + 1)
                        Ve.scalar_tensor_tensor(xl[:, 4 + g, :], bank[5][:, :], pscale(g), f32(xh[:, 4 + g, :]),
                                                ALU.mult, ALU.subtract).then_inc(s_y[1], 1)
                lows(ffn[l] - 1)
                for g in range(2 * MT):
                    c, m = g // MT, g % MT
                    dve.wait_ge(s_m, groups_done(l, GO, g + 1))
                    hh = h[:, m, c * 512:(c + 1) * 512]
                    Ve.tensor_tensor(hh, hh, bank[4 * c + m][:, :], ALU.add).then_inc(s_mD, 1)
                turn(l, TF, KD, lambda j: Ve.tensor_scalar(xT[:, j, :], turn_bank(l, TF, j), gffn(l, j), None, ALU.mult))
                dve.wait_ge(s_lg[l], 1)
                Ve.tensor_copy(lgT, bank[0][0:20, :]).then_inc(s_lgx, 1)
                dve.wait_ge(s_rr, 4 * l + SF + 1)
                dve.wait_ge(s_lg[l], 2)
                lp = bank[1][:, 0:MT * 20].rearrange("p (m n) -> p m n", n=20)
                link(Ve.tensor_tensor(lg[:, :, :], lp, over(rr[:, l, SF, :], 20), ALU.mult))
                Ve.tensor_tensor(lg[:, :, 0:4], lg[:, :, 0:4], rb[:, l, 0:4].unsqueeze(1).to_broadcast([P, MT, 4]), ALU.add)
                link(Ve.tensor_tensor(le[:, :, :], lg[:, :, 4:20], rb[:, l, 4:20].unsqueeze(1).to_broadcast([P, MT, NE]), ALU.add))
                first_max(lg[:, :, 0:4], NG, mxs[:, 0, :], gmask[:, :, :], (t16[:, 0, :, 0:NG], t16[:, 1, :, 0:NG]))
                Ve.tensor_tensor(exps[:, 0, :, 0:4], lg[:, :, 0:4], over(mxs[:, 0, :], NG), ALU.subtract)
                link(Ve.tensor_scalar(row16[:, 5, :], gmask[:, :, :].rearrange("p m g -> p (m g)"), -NEG, NEG, ALU.mult, ALU.add))
                lev = le[:, :, :].rearrange("p m (g e) -> p (m g) e", g=NG)
                link(Ve.tensor_tensor(lev, lev, row16[:, 5, :].unsqueeze(2).to_broadcast([P, MT * NG, EG]), ALU.add))
                first_max(le[:, :, :], NE, mxs[:, 1, :], mask1[:, :, :], (t16[:, 0, :, :], t16[:, 1, :, :]))
                link(Ve.scalar_tensor_tensor(le[:, :, :], mask1[:, :, :], 3 * NEG, le[:, :, :], ALU.mult, ALU.add))
                first_max(le[:, :, :], NE, mxs[:, 2, :], mask2[:, :, :], (t16[:, 0, :, :], t16[:, 1, :, :]))
                Ve.tensor_tensor(exps[:, 0, :, 4:5], mxs[:, 2, :].unsqueeze(2), mxs[:, 1, :].unsqueeze(2), ALU.subtract).then_inc(s_lgv, 1)
                Ve.tensor_tensor(selb[:, :, :], mask1[:, :, :], mask2[:, :, :], ALU.add).then_inc(s_sel, 1)
                dve.wait_ge(s_mD, movedD(l, GO, 2 * MT))
                dve.wait_ge(s_pg[l], 32)

                def normalised(m):
                    Ve.scalar_tensor_tensor(y[:, m, :], h[:, m, :], rr[:, l, SF, m:m + 1], frow, ALU.mult, ALU.mult).then_inc(s_xn[l], 1)

                normalised(0)
                dve.wait_ge(s_rank, l + 1)
                rk = bank[1][:, 0:MT * NE].rearrange("p (m e) -> p m e", e=NE)
                ct = bank[1][:, 64:64 + NE]
                link(Ve.tensor_scalar(row16[:, 0, :], ct, float(P + 1), None, ALU.is_ge))
                for k in range(2, S // P):
                    link(Ve.scalar_tensor_tensor(row16[:, 0, :], ct, float(k * P + 1), row16[:, 0, :], ALU.is_ge, ALU.add))
                link(Ve.tensor_tensor_scan(row16[:, 1, :], row16[:, 0, :], row16[:, 0, :], 0.0, ALU.add, ALU.bypass))
                link(Ve.tensor_tensor(row16[:, 2, :], row16[:, 1, :], row16[:, 0, :], ALU.subtract))
                link(Ve.tensor_scalar(row16[:, 2, :], row16[:, 2, :], float(P), float((NE - 1) * P), ALU.mult, ALU.add))
                link(Ve.tensor_tensor(row16[:, 2, :], row16[:, 2, :], small[:, NE:2 * NE], ALU.subtract))
                link(Ve.tensor_scalar(t16[:, 0, :, :], rk, float(P), None, ALU.is_ge))
                link(Ve.tensor_tensor(t16[:, 0, :, :], t16[:, 0, :, :], row16[:, 2, :].unsqueeze(1).to_broadcast([P, MT, NE]), ALU.mult))
                link(Ve.tensor_tensor(t16[:, 0, :, :], t16[:, 0, :, :], rk, ALU.add))
                link(Ve.tensor_tensor(t16[:, 0, :, :], t16[:, 0, :, :], small[:, NE:2 * NE].unsqueeze(1).to_broadcast([P, MT, NE]), ALU.add))
                Ve.tensor_tensor(t16[:, 1, :, :], t16[:, 0, :, :], mask1[:, :, :], ALU.mult)
                link(Ve.tensor_tensor(t16[:, 2, :, :], t16[:, 0, :, :], mask2[:, :, :], ALU.mult))
                Ve.tensor_reduce(posf[:, 0, :], t16[:, 1, :, :], AX, ALU.add)
                link(Ve.tensor_reduce(posf[:, 1, :], t16[:, 2, :, :], AX, ALU.add))
                Ve.tensor_copy(posi[:, :, :], posf[:, :, :]).then_inc(s_pos, 1)
                normalised(1)
                normalised(2)
                normalised(3)
                link(Ve.tensor_tensor(ovf[:, :, :], row16[0:1, 1, :].unsqueeze(1).to_broadcast([1, OVT, NE]),
                                      small[0:1, 32:32 + OVT].unsqueeze(2).to_broadcast([1, OVT, NE]), ALU.is_le))
                link(Ve.tensor_reduce(ove[:, 0:OVT], ovf[:, :, :], AX, ALU.add))
                link(Ve.tensor_scalar(ove[:, 0:OVT], ove[:, 0:OVT], float(NE - 1), None, ALU.min))
                link(Ve.tensor_tensor(ovf[:, 0, 0:4], small[0:1, 40:44], row16[0:1, 1, NE - 1:NE].to_broadcast([1, 4]), ALU.is_le))
                link(Ve.tensor_reduce(ove[:, OVT:OVT + 1], ovf[:, 0:1, 0:4], AX, ALU.add))
                Ve.tensor_copy(ovi[:, :], ove[:, :]).then_inc(s_ovi, 1)
                dve.wait_ge(s_ex, l + 1)
                link(Ve.tensor_reduce(mxs[:, 3, :], exps[:, 1, :, 0:4], AX, ALU.add))
                ex2 = exps[:, 1, :, 4:5]
                col = lambda k: mxs[:, k, :].unsqueeze(2)
                link(Ve.tensor_scalar(col(4), ex2, 1.0, None, ALU.add))
                link(Ve.tensor_tensor(mxs[:, 5, :], mxs[:, 3, :], mxs[:, 4, :], ALU.mult))
                link(Ve.reciprocal(wts[:, 0, :], mxs[:, 5, :]))
                link(Ve.tensor_tensor(wts[:, 1, :].unsqueeze(2), wts[:, 0, :].unsqueeze(2), ex2, ALU.mult))

                def rows_low(e):
                    for b in range(2):
                        dve.wait_ge(s_xh[l], 2 * e + b + 1)
                        part = lambda x: x[:, 4 * b:4 * b + 4, :].rearrange("p k n -> p (k n)")
                        Ve.tensor_tensor(part(xgl), bank[b][:, :], f32(part(xgh)), ALU.subtract).then_inc(s_xv[l], 1)

                def split_low(e, b):
                    for j in range(4):
                        dve.wait_ge(s_ehi[l], 4 * e + j + 1)
                        unit_ = slice(2 * j, 2 * j + 2)
                        Ve.tensor_tensor(gate_up_low_at(l, b)[:, unit_, :], gate_up_at(l, b)[:, unit_, :], f32(ghi[:, unit_, :]), ALU.subtract).then_inc(s_elo[l], 1)

                def activations(e):
                    dve.wait_ge(s_sil[l], e + 1)
                    Ve.tensor_tensor(act, sil, bank[2][:, DE:2 * DE], ALU.mult).then_inc(s_act[l], 1)

                def result(e, p):
                    dve.wait_ge(s_dn[l], 2 * e + 1)
                    Ve.tensor_copy(ys[p][:, 0:512], bank[4][:, :]).then_inc(s_yD[l], 1)

                def stage(e, p, i, stored):
                    activations(e - 1)
                    rows_low(e)
                    split_low(e, place(e, p, i)[0])
                    if stored:
                        dve.wait_ge(s_st[l][p], 16 * (i - 1))
                    result(e - 2, p)

                split_low(0, 0)
                rows_low(0)
                activations(0)
                rows_low(1)
                split_low(1, 1)
                stage(2, 0, 1, False)
                dve.wait_ge(s_rr, 4 * l + SE + 1)
                dve.wait_ge(s_pg[l], 32)
                for m in range(MT):
                    if m == 2:
                        stage(3, 1, 1, False)
                    ins = Ve.scalar_tensor_tensor(E[:, m, :], E[:, m, :], rr[:, l, SE, m:m + 1], pgain, ALU.mult, ALU.mult)
                link(ins)
                stage(4, 0, 2, True)
                stage(5, 1, 2, True)
                with dve.Fori(3, NE // 2) as i:
                    for p in range(2):
                        stage(2 * i + p, p, i, True)
                n = dve.value_load(ovi[0:1, OVT:OVT + 1], min_val=0, max_val=OVT // 2)
                with dve.If(n > 0):
                    with dve.Fori(0, n) as i:
                        for p in range(2):
                            stage(2 * i + (p + NE), p, i + NE // 2, True)
                dve.wait_ge(s_st[l][0], 16 * n + 16 * (NE // 2 - 1))
                activations(2 * n + (NE - 1))
                result(2 * n + (NE - 2), 0)
                dve.wait_ge(s_st[l][1], 16 * n + 16 * (NE // 2 - 1))
                result(2 * n + (NE - 1), 1)
                lows(ffn[l] + 1)
                for m in range(MT):
                    dve.wait_ge(s_gam[0][m], 16 * (l + 1))
                    link(Ve.scalar_tensor_tensor(h[:, m, :], y[:, m, :], wts[:, 0, m:m + 1], h[:, m, :], ALU.mult, ALU.add))
                    dve.wait_ge(s_gam[1][m], 16 * (l + 1))
                    Ve.scalar_tensor_tensor(h[:, m, :], G2[:, m, :], wts[:, 1, m:m + 1], h[:, m, :], ALU.mult, ALU.add).then_inc(s_cmb[l], 1)
                turn_low(l, TP, range(KD))
                lows(ffn[l] + 2)
                for g in range(2 * MT):
                    c, m = g // MT, g % MT
                    if l == 0 and g == MT:
                        for j in range(3):
                            low(first[1], j)
                    dve.wait_ge(s_gt[l], g + 1)
                    part = slice(c * 512, (c + 1) * 512)
                    link(Ve.tensor_tensor(E[:, m, part], E[:, m, part], gate[:, g % 2, :], ALU.mult))
                    Ve.tensor_tensor(h[:, m, part], h[:, m, part], E[:, m, part], ALU.add).then_inc(s_h[l], 1)
                if l == 0:
                    low(first[1], 3)

        @block.tensor
        def _(pe):
            T = nc.tensor

            both = (TM, TY, TP)

            def turn_step(l, which, j, m, src):
                mm = T.transpose(turn_bank(l, which, j)[:, m * P:(m + 1) * P], src(j, m), ident)
                if m == MT - 1:
                    mm.then_inc(s_t, 1)

            def turn(l, which, steps, src, ready=None):
                for j in steps:
                    for m in range(MT):
                        if ready:
                            ready(j, m)
                        turn_step(l, which, j, m, src)

            def turn_by_tile(l, which, steps, src, ready):
                for m in range(MT):
                    ready(m)
                    for j in steps:
                        turn_step(l, which, j, m, src)

            def turned(l, which, n):
                pe.wait_ge(s_tD, steps_moved(l, which, n if which in both else (n + 1) // 2))
                pe.wait_ge(s_tA, steps_moved(l, which, n if which in both else n // 2))

            def three(dst, x0, x1, w0, w1, start, stop):
                T.matmul(dst, x0, w0, start=start, stop=False)
                T.matmul(dst, x0, w1, start=False, stop=False)
                return T.matmul(dst, x1, w0, start=False, stop=stop)

            def product(c, banks, before=None):
                for j in range(4):
                    pe.wait_ge(s_lo, unit(c, j) + 1)
                    for k in (2 * j, 2 * j + 1):
                        if before and k:
                            before(k)
                        for m in range(MT):
                            if before and k == 0:
                                before(0, m)
                            tok = slice(m * P, (m + 1) * P)
                            mm = three(banks[m][:, :], xh[:, k, tok], xl[:, k, tok], wh[:, j, k % 2, :], wl[:, j, k % 2, :],
                                       k == 0, k == KD - 1)
                            if k == KD - 1:
                                mm.then_inc(s_m, 1)
                    if j < 3:
                        mm.then_inc(s_un, 1)

            def group(dst, m, w, nk, x=None):
                for k in range(nk):
                    mm = T.matmul(dst, (x if x is not None else xT)[:, k, m * P:(m + 1) * P], w(k), start=(k == 0), stop=(k == nk - 1))
                return mm

            pe.wait_ge(s_ident, 16)
            for l in range(DEPTH):
                hrow = lambda j, m: h[:, m, j * P:(j + 1) * P]
                if l == 0:
                    turn_by_tile(0, TM, range(KD - 1), hrow, lambda m: pe.wait_ge(s_in[m], 16))
                    pe.wait_ge(s_grow, 16 * 6)
                    T.transpose(bank[7][:, 0:46], grow[:, :], ident[0:46, 0:46]).then_inc(s_gT, 1)
                    pe.wait_ge(s_gcol, 1)
                    turn(0, TM, [KD - 1], hrow)
                else:
                    turn_by_tile(1, TM, range(KD // 2), hrow, lambda m: pe.wait_ge(s_h[0], m + 1))
                    turn_by_tile(1, TM, range(KD // 2, KD), hrow, lambda m: pe.wait_ge(s_h[0], MT + m + 1))

                def with_first_chunk(k, m=0):
                    if k == 0:
                        turned(l, TM, m + 1)
                    elif k >= 4:
                        turned(l, TM, k + 1)
                    if l == 0 and k == 6:
                        turned(0, TM, KD)
                        pe.wait_ge(s_sg, 1)
                        for hd in range(NH):
                            mm = T.transpose(bank[4 + hd // 4][:, (hd % 4) * P:(hd % 4 + 1) * P], sgw[:, hd, :], ident)
                            if hd % 4 == 3:
                                mm.then_inc(s_sgT, 1)
                    if l == 1:
                        if k == 6:
                            turned(1, TM, KD)
                            pe.wait_ge(s_wf, 2)
                            for kk in range(KD):
                                mm = three(bank[7][0:NH, :], wfh[:, kk, :], wfl[:, kk, :], xh[:, kk, :], xl[:, kk, :], kk == 0, kk == KD - 1)
                            mm.then_inc(s_fa, 1)
                        if k == 7:
                            pe.wait_ge(s_fx, 1)
                            for m in range(MT):
                                mm = T.transpose(bank[6][:, m * NH:(m + 1) * NH], Flog[:, m * P:(m + 1) * P], ident[0:NH, 0:NH])
                            mm.then_inc(s_fa, 1)

                def cumulate(k, m=0):
                    if k == 6:
                        pe.wait_ge(s_fc, 1)
                        pe.wait_ge(s_mD, in_moved(1, 2)[0])
                        pe.wait_ge(s_mA, in_moved(1, 2)[1])
                        for i in range(MT):
                            for j in range(i + 1):
                                mm = T.matmul(bank[7][0:NH, i * P:(i + 1) * P], lf[:, 3, j, :], upto if i == j else ones,
                                              start=(j == 0), stop=(j == i))
                        mm.then_inc(s_fa, 1)

                for c in range(NIN[l]):
                    if c == 1 and l == 0:
                        pe.wait_ge(s_mixd, 2)
                    if c == 1 and l == 1:
                        pe.wait_ge(s_f, 1)
                    if c >= 2:
                        pe.wait_ge(s_mD, in_moved(l, c - 1)[0])
                        pe.wait_ge(s_mA, in_moved(l, c - 1)[1])
                    if l == 1 and c == 3:
                        pe.wait_ge(s_fx, 2)
                    product(first[l] + c, bank[4 * (c % 2):4 * (c % 2) + 4],
                            with_first_chunk if c == 0 else cumulate if (l, c) == (1, 2) else None)
                if l == 1:
                    pe.wait_ge(s_qn[1], 2)

                def heads_input(j, m):
                    if m == 0 and j % 4 == 0:
                        pe.wait_ge(s_mD, in_moved(l, NIN[l] - 1 + j // 4)[0])
                        pe.wait_ge(s_mA, in_moved(l, NIN[l] - 1 + j // 4)[1])

                pe.wait_ge(s_cbf, 16)
                turn(l, TQ, range(8), lambda j, m: (Q if j < 4 else K)[:, m, (j % 4) * P:(j % 4 + 1) * P], heads_input)
                turned(l, TQ, 8)
                def mix(g):
                    if g == 0:
                        pe.wait_ge(s_qn[0], 1)
                    else:
                        pe.wait_ge(s_y[0], 2 * g)
                    for b in range(2):
                        hd = 2 * g + b
                        mm = T.matmul(bank[4][:, 256 * b:256 * b + 256], sguT[:, hd, :], VA[:, :, hd * HD:(hd + 1) * HD], start=True, stop=True)
                    mm.then_inc(s_pm, 1)

                def mixed_turned(j):
                    pe.wait_ge(s_y[0], 2 * j + 2)
                    if j:
                        turned(0, TY, j)
                    turn(0, TY, [j], lambda j, m: y[:, m, j * P:(j + 1) * P])

                def pool_means(g):
                    if g:
                        pe.wait_ge(s_plv, g)
                    for j in range(MT):
                        width = BW if j < MT - 1 else P
                        mm = T.matmul(bank[4][:, j * P:j * P + width], y[:, j, W + g * P:W + (g + 1) * P],
                                      bands[:, 1 if j == 0 else 0, g, 0:width], start=(j == 0), stop=(j == MT - 1),
                                      skip_group_check=True)
                    mm.then_inc(s_pl, 1)

                def pool_mix(g):
                    pe.wait_ge(s_plv, g + 1)
                    if g:
                        pe.wait_ge(s_y[1], g)
                    T.matmul(bank[5][:, :], poolw[:, g, :], pT2, start=True, stop=True).then_inc(s_pm, 1)

                if l == 1:
                    pe.wait_ge(s_fp, 1)
                    pe.wait_ge(s_mixin, 32)
                    pe.wait_ge(s_selin, 16)
                for v in range(4 * NH + 4):
                    if v < 4 * NH:
                        hd, i = v // 4, v % 4
                        n = (i + 1) * P
                        r = slice(HD * (hd % 2), HD * (hd % 2) + HD)
                        if v >= 2:
                            pe.wait_ge(s_pr[l], v - 1)
                        T.matmul(bank[v % 2][:, n - P:n], identb, strictb if l == 0 else causalb, start=True, stop=False,
                                 skip_group_check=True)
                        if l == 1:
                            T.matmul(bank[v % 2][:, 0:n], self_[0:96, hd, :], Fp[0:96, 0:n], start=False, stop=False,
                                     skip_group_check=True)
                        T.matmul(bank[v % 2][:, 0:n], qT[r, hd // 2, i * P:(i + 1) * P], kT[r, hd // 2, 0:n], start=False, stop=True,
                                 skip_group_check=True).then_inc(s_z[l], 1)
                    if 3 <= v < 4 * NH + 3:
                        u = v - 3
                        pe.wait_ge(s_w[0] if l == 0 else s_wn, u + 1)
                        for j in range(u % 4 + 1):
                            mm = T.transpose(bank[2 + u % 2][:, j * P:(j + 1) * P], weights(l, u, 512)[:, j * P:(j + 1) * P], ident)
                        mm.then_inc(s_pt[l], 1)
                    if v >= 4:
                        u = v - 4
                        hd, i = u // 4, u % 4
                        pe.wait_ge(s_ptv[l], u + 1)
                        if i == 0 and hd % 2 == 0 and hd >= 4:
                            pe.wait_ge(s_ov[l], hd // 2 - 1)
                        for j in range(i + 1):
                            mm = T.matmul(bank[6 + hd // 2 % 2][HD * (hd % 2):HD * (hd % 2) + HD, i * P:(i + 1) * P],
                                          V[:, j, hd * HD:(hd + 1) * HD], attP[:, u % 2, j * P:(j + 1) * P], start=(j == 0), stop=(j == i))
                        if i == 3 and hd % 2:
                            mm.then_inc(s_o[l], 1)
                    if l == 0 and v % 8 == 2 and v <= 26:
                        mix((v - 2) // 8)
                    if l == 0 and v % 8 == 6 and v <= 30:
                        mixed_turned((v - 6) // 8)
                    if l == 1 and v % 8 == 4 and v <= 28:
                        pool_means((v - 4) // 8)
                    if l == 1 and v % 8 == 6 and v <= 30:
                        pool_mix((v - 6) // 8)

                def with_out_projection(k, m=0):
                    if m:
                        return
                    if l == 0 and k < 4:
                        turned(0, TY, k + 1)
                    if l == 1 and k < 4 or l == 0 and k >= 4:
                        pe.wait_ge(s_ov[l], k % 4 + 1)
                    if l == 1 and k >= 4:
                        pe.wait_ge(s_y[1], k - 4 + 1)

                for c in range(2):
                    product(ffn[l] - 2 + c, bank[4 * c:4 * c + 4], None if c else with_out_projection)
                turn(l, TF, range(KD), lambda j, m: h[:, m, j * P:(j + 1) * P],
                     lambda j, m: pe.wait_ge(s_mD, movedD(l, GO, MT * (j // 4) + m + 1)) if j % 4 == 0 else None)
                pe.wait_ge(s_const, 16 * 12)
                for k in range(KD):
                    turned(l, TF, k + 1)
                    mm = T.matmul(bank[0][0:20, :], wr[:, l, k, :], xT[:, k, :], start=(k == 0), stop=(k == KD - 1))
                mm.then_inc(s_lg[l], 1)
                pe.wait_ge(s_pin[l], 16)
                for k in range(KP):
                    for m in range(MT):
                        mm = T.transpose(bank[6 + k][:, m * P:(m + 1) * P], pin[:, m, k * P:(k + 1) * P], ident)
                mm.then_inc(s_e, 1)
                pe.wait_ge(s_lgx, l + 1)
                for m in range(MT):
                    mm = T.transpose(bank[1][:, m * 20:(m + 1) * 20], lgT[:, m * P:(m + 1) * P], ident[0:20, 0:20])
                mm.then_inc(s_lg[l], 1)
                pe.wait_ge(s_pse[l], KP)
                c = ffn[l]
                chunk_ready(pe, c)
                wp = ring[:, c % 2, 0:2 * KP, :].rearrange("p (k n) c -> p k (n c)", k=KP)

                def embed(g):
                    if g >= 4:
                        pe.wait_ge(s_mA, movedA(l, GE, g - 3))
                    group(bank[2 + g % 4][:, :], g // 2, lambda k: wp[:, k, (g % 2) * 512:(g % 2 + 1) * 512], KP, pT).then_inc(s_m, 1)

                embed(0)
                pe.wait_ge(s_sel, l + 1)
                for m in range(MT):
                    for j in range(m + 1):
                        T.matmul(bank[1][:, m * NE:(m + 1) * NE], beforeb if j == m else onesb, selb[:, j, :],
                                 start=(j == 0), stop=(j == m))
                for j in range(MT):
                    mm = T.matmul(bank[1][:, 64:64 + NE], onesb, selb[:, j, :], start=(j == 0), stop=(j == MT - 1))
                mm.then_inc(s_rank, 1)
                for g in range(1, 2 * MT):
                    embed(g)
                pe.wait_ge(s_pos, l + 1)
                pe.wait_ge(s_mA, movedA(l, GE, 2 * MT))

                def rows_turned(e, p, i):
                    pe.wait_ge(s_xl[l][p], 16 * i + 16)
                    turn_rows(e, p)

                def turn_rows(e, p):
                    for b in range(2):
                        for k in range(4):
                            mm = T.transpose(bank[b][:, k * P:(k + 1) * P], xs[p][:, (4 * b + k) * P:(4 * b + k + 1) * P], ident)
                        mm.then_inc(s_tx[l], 1)

                def gate_up(e, b):
                    pe.wait_ge(s_xv[l], 2 * e + 2)
                    for j in range(4):
                        pe.wait_ge(s_elo[l], 4 * e + j + 1)
                        for k in (2 * j, 2 * j + 1):
                            mm = three(bank[2][:, :], xgh[:, k, :], xgl[:, k, :], ghi[:, k, :], gate_up_low_at(l, b)[:, k, :], k == 0, k == KD - 1)
                        mm.then_inc((s_eun if j < 3 else s_g)[l], 1)

                def act_turned(e):
                    pe.wait_ge(s_act[l], e + 1)
                    for f in range(DE // P):
                        mm = T.transpose(bank[3][:, f * P:(f + 1) * P], act[:, f * P:(f + 1) * P], ident)
                    mm.then_inc(s_at[l], 1)

                def down(e, p, i):
                    b, loads = place_down(e, p, i)
                    if b == 2:
                        pe.wait_ge(s_third, 48 * (l + 1))
                    else:
                        pe.wait_ge(s_wd[l][b], 16 * loads)
                    pe.wait_ge(s_atv[l], e + 1)
                    if not (isinstance(e, int) and e == 0):
                        pe.wait_ge(s_yD[l], e)
                        pe.wait_ge(s_yA[l], e)
                    for c in range(2):
                        for f in range(DE // P):
                            mm = T.matmul(bank[4 + c][:, :], actT[:, f * P:(f + 1) * P], down_at(l, b)[:, f, c * 512:(c + 1) * 512],
                                          start=(f == 0), stop=(f == DE // P - 1))
                        mm.then_inc(s_dn[l], 1)

                rows_turned(0, 0, 0)
                gate_up(0, 0)
                rows_turned(1, 1, 0)
                act_turned(0)
                gate_up(1, 1)

                def stage(e, p, i):
                    rows_turned(e, p, i)
                    down(e - 2, p, i - 1)
                    act_turned(e - 1)
                    gate_up(e, place(e, p, i)[0])

                stage(2, 0, 1)
                stage(3, 1, 1)
                stage(4, 0, 2)
                stage(5, 1, 2)
                with pe.Fori(3, NE // 2) as i:
                    for p in range(2):
                        stage(2 * i + p, p, i)
                pe.wait_ge(s_ovi, l + 1)
                n = pe.value_load(ovi[0:1, OVT:OVT + 1], min_val=0, max_val=OVT // 2)
                with pe.If(n > 0):
                    with pe.Fori(0, n) as i:
                        for p in range(2):
                            stage(2 * i + (p + NE), p, i + NE // 2)
                down(2 * n + (NE - 2), 0, n + (NE // 2 - 1))
                act_turned(2 * n + (NE - 1))
                down(2 * n + (NE - 1), 1, n + (NE // 2 - 1))
                turn_by_tile(l, TP, range(KD), hrow, lambda m: pe.wait_ge(s_cmb[l], m + 1))
                for c in range(2):
                    product(ffn[l] + 1 + c, bank[4 * c:4 * c + 4],
                            None if c else lambda k, m=0: turned(l, TP, max(k, m) + 1) if k == 0 or k >= 4 else None)
                pe.wait_ge(s_gt[l], 2 * MT)


_OUT = ((1, 512, 1024), "float32")


def kernel(**inputs):
    import numpy as _np
    import concourse.bacc as _bacc
    from concourse import mybir as _mybir
    from concourse.bass_utils import run_bass_kernel_spmd as _run

    nc = _bacc.Bacc("TRN2", target_bir_lowering=False, num_devices=1)
    arrays, aps = {}, {}
    for name, value in {**inputs, **constants()}.items():
        v = _np.ascontiguousarray(value)
        arrays[f"in_{name}_dram"] = v
        aps[name] = nc.dram_tensor(f"in_{name}_dram", v.shape, _mybir.dt.from_np(v.dtype), kind="ExternalInput").ap()
    out = nc.dram_tensor("out_dram", _OUT[0], _mybir.dt.from_np(_np.dtype(_OUT[1])), kind="ExternalOutput").ap()
    trunk(nc, aps, out)
    r = _run(nc, [arrays], core_ids=[0])
    return r.results[0]["out_dram"]
```
